# Optimizing a Trainium2 kernel written in Bass

```python
import jax, jax.numpy as jnp
from jax import lax
import numpy as np

D_MODEL = 1024
BATCH = 1
SEQ = 512
DEPTH = 1

HEAD_DIM_A = 64
WIDTH_A = D_MODEL // 2
N_HEADS_A = WIDTH_A // HEAD_DIM_A
HEAD_DIM_B = 64
WIDTH_B = D_MODEL // 2
N_HEADS_B = WIDTH_B // HEAD_DIM_B
CONV_K = 5
CHUNK = 64
N_DIR = 2
N_GROUPS = 4
EXPERTS_PER_GROUP = 8
N_EXPERTS = N_GROUPS * EXPERTS_PER_GROUP
TOP_K = 2
D_EXPERT = D_MODEL // 4
N_MOD = 6
EPS = 1e-6
NEG_INF = -1e30

SPLIT_WIDTHS = (3 * WIDTH_A, WIDTH_A, 2 * N_DIR * N_HEADS_A,
                2 * WIDTH_B, WIDTH_B, WIDTH_B, 2 * N_DIR * N_HEADS_B, 2 * D_MODEL)
D_IN = sum(SPLIT_WIDTHS)
SPLIT_POINTS = tuple(sum(SPLIT_WIDTHS[: i + 1]) for i in range(len(SPLIT_WIDTHS) - 1))


def rmsnorm(x, g):
    xf = x.astype(jnp.float32)
    y = xf * lax.rsqrt(jnp.mean(xf * xf, axis=-1, keepdims=True) + EPS)
    return y * g.astype(jnp.float32)

def l2norm(t):
    return t * lax.rsqrt(jnp.sum(t * t, axis=-1, keepdims=True) + EPS)

def head_layernorm(t, g):
    mu = jnp.mean(t, axis=-1, keepdims=True)
    tc = t - mu
    return tc * lax.rsqrt(jnp.mean(tc * tc, axis=-1, keepdims=True) + EPS) * g

def centred_conv(x, w):
    c = x.shape[-1]
    return lax.conv_general_dilated(
        x, w[:, None, :].astype(x.dtype), window_strides=(1,),
        padding=[(CONV_K // 2, CONV_K // 2)],
        dimension_numbers=("NWC", "WIO", "NWC"), feature_group_count=c)

def chunk_heads(t):
    b, s, h, d = t.shape
    return t.reshape(b, s // CHUNK, CHUNK, h, d).transpose(0, 3, 1, 2, 4)

def chunk_scalar(t):
    b, s, h = t.shape
    return t.reshape(b, s // CHUNK, CHUNK, h).transpose(0, 3, 1, 2)

def unchunk(t):
    b, h, n, l, d = t.shape
    return t.transpose(0, 2, 3, 1, 4).reshape(b, n * l, h, d)

def flip_seq(t):
    return jnp.flip(t, axis=1)

def gated_delta_chunked(q, k, v, g, beta):
    L = q.shape[-2]
    dv = v.shape[-1]
    b, h, n, _, dk = k.shape
    tri_incl = jnp.tril(jnp.ones((L, L), dtype=bool))
    tri_strict = jnp.tril(jnp.ones((L, L), dtype=bool), -1)
    g_cum = jnp.cumsum(g, axis=-1)
    decay = jnp.exp(jnp.where(tri_incl, g_cum[..., :, None] - g_cum[..., None, :], NEG_INF))
    k_beta = k * beta[..., None]
    lower = jnp.where(tri_strict, jnp.einsum("bhnid,bhnjd->bhnij", k_beta, k) * decay, 0.0)
    lhs = lower + jnp.eye(L, dtype=lower.dtype)
    rhs = jnp.concatenate([v * beta[..., None], k_beta * jnp.exp(g_cum)[..., None]], axis=-1)
    sol = lax.linalg.triangular_solve(lhs, rhs, left_side=True, lower=True, unit_diagonal=True)
    u, w = sol[..., :dv], sol[..., dv:]
    k_to_end = k * jnp.exp(g_cum[..., -1:] - g_cum)[..., None]
    chunk_decay = jnp.exp(g_cum[..., -1])

    def step(state, xs):
        u_c, w_c, kd_c, cd_c = xs
        v_new = u_c - jnp.einsum("bhlk,bhkv->bhlv", w_c, state)
        state_next = state * cd_c[..., None, None] + jnp.einsum("bhlk,bhlv->bhkv", kd_c, v_new)
        return state_next, (state, v_new)

    s0 = jnp.zeros((b, h, dk, dv), jnp.float32)
    xs = tuple(jnp.moveaxis(t, 2, 0) for t in (u, w, k_to_end, chunk_decay))
    _, (s_prev, v_new) = lax.scan(step, s0, xs)
    s_prev = jnp.moveaxis(s_prev, 0, 2)
    v_new = jnp.moveaxis(v_new, 0, 2)
    intra = jnp.einsum("bhnid,bhnjd->bhnij", q, k) * decay
    return (jnp.einsum("bhnlk,bhnkv->bhnlv", q * jnp.exp(g_cum)[..., None], s_prev)
            + jnp.einsum("bhnij,bhnjv->bhniv", intra, v_new))

def mlstm_chunked(q, k, v, i_pre, f_pre):
    L = q.shape[-2]
    b, h, n, _, dk = k.shape
    dv = v.shape[-1]
    tri_incl = jnp.tril(jnp.ones((L, L), dtype=bool))
    bcum = jnp.cumsum(jax.nn.log_sigmoid(f_pre), axis=-1)
    b_last = bcum[..., -1]
    a_end = b_last[..., None] - bcum + i_pre

    def step(carry, xs):
        c_st, n_st, m_st = carry
        k_c, v_c, a_c, bl_c = xs
        m_next = jnp.maximum(bl_c + m_st, jnp.max(a_c, axis=-1))
        scale_prev = jnp.exp(bl_c + m_st - m_next)
        wgt = jnp.exp(a_c - m_next[..., None])
        c_next = c_st * scale_prev[..., None, None] + jnp.einsum("bhlk,bhlv->bhkv", k_c * wgt[..., None], v_c)
        n_next = n_st * scale_prev[..., None] + jnp.einsum("bhl,bhlk->bhk", wgt, k_c)
        return (c_next, n_next, m_next), (c_st, n_st, m_st)

    init = (jnp.zeros((b, h, dk, dv), jnp.float32), jnp.zeros((b, h, dk), jnp.float32),
            jnp.zeros((b, h), jnp.float32))
    xs = tuple(jnp.moveaxis(t, 2, 0) for t in (k, v, a_end, b_last))
    _, (c_prev, n_prev, m_prev) = lax.scan(step, init, xs)
    c_prev = jnp.moveaxis(c_prev, 0, 2)
    n_prev = jnp.moveaxis(n_prev, 0, 2)
    m_prev = jnp.moveaxis(m_prev, 0, 2)
    log_d = jnp.where(tri_incl, bcum[..., :, None] - bcum[..., None, :] + i_pre[..., None, :], NEG_INF)
    log_inter = bcum + m_prev[..., None]
    m_t = jnp.maximum(log_inter, jnp.max(log_d, axis=-1))
    d_mat = jnp.exp(log_d - m_t[..., None])
    inter_w = jnp.exp(log_inter - m_t)
    qk = jnp.einsum("bhntd,bhnsd->bhnts", q, k) * d_mat
    num = (jnp.einsum("bhnts,bhnsv->bhntv", qk, v)
           + inter_w[..., None] * jnp.einsum("bhntk,bhnkv->bhntv", q, c_prev))
    den = jnp.sum(qk, axis=-1) + inter_w * jnp.einsum("bhntk,bhnk->bhnt", q, n_prev)
    return num / jnp.maximum(jnp.abs(den), jnp.exp(-m_t))[..., None]

def run_gdn(q, k, v, g, beta):
    return unchunk(gated_delta_chunked(chunk_heads(q), chunk_heads(k), chunk_heads(v),
                                       chunk_scalar(g), chunk_scalar(beta)))

def run_mlstm(q, k, v, i_pre, f_pre):
    return unchunk(mlstm_chunked(chunk_heads(q), chunk_heads(k), chunk_heads(v),
                                 chunk_scalar(i_pre), chunk_scalar(f_pre)))

def hybrid_mixer(h, w_in, gdn_conv_w, gdn_a_log, gdn_dt_bias, gdn_norm_g,
                 mlstm_conv_w, mlstm_i_bias, mlstm_f_bias, mlstm_norm_g,
                 w_branch_a, w_branch_b, w_out):
    bsz, s, _ = h.shape
    proj = jnp.einsum("bsd,de->bse", h, w_in.astype(jnp.float32))
    a_qkv, a_z, a_gates, b_qk, b_v, b_o, b_gates, merge = jnp.split(proj, SPLIT_POINTS, axis=-1)

    a_qkv = jax.nn.silu(centred_conv(a_qkv, gdn_conv_w.astype(jnp.float32)))
    aq, ak, av = jnp.split(a_qkv, 3, axis=-1)
    aq = l2norm(aq.reshape(bsz, s, N_HEADS_A, HEAD_DIM_A)) * (HEAD_DIM_A ** -0.5)
    ak = l2norm(ak.reshape(bsz, s, N_HEADS_A, HEAD_DIM_A))
    av = av.reshape(bsz, s, N_HEADS_A, HEAD_DIM_A)
    a_gates = jnp.moveaxis(a_gates.reshape(bsz, s, N_DIR, 2, N_HEADS_A), 2, 0)
    g = -jnp.exp(gdn_a_log.astype(jnp.float32))[:, None, None, :] * jax.nn.softplus(
        a_gates[..., 0, :] + gdn_dt_bias.astype(jnp.float32)[:, None, None, :])
    beta = jax.nn.sigmoid(a_gates[..., 1, :])
    o_a = (run_gdn(aq, ak, av, g[0], beta[0])
           + flip_seq(run_gdn(flip_seq(aq), flip_seq(ak), flip_seq(av), flip_seq(g[1]), flip_seq(beta[1]))))
    o_a = rmsnorm(o_a, gdn_norm_g) * jax.nn.silu(a_z.reshape(bsz, s, N_HEADS_A, HEAD_DIM_A))
    o_a = o_a.reshape(bsz, s, WIDTH_A)

    b_qk = jax.nn.silu(centred_conv(b_qk, mlstm_conv_w.astype(jnp.float32)))
    bq, bk = jnp.split(b_qk, 2, axis=-1)
    bq = bq.reshape(bsz, s, N_HEADS_B, HEAD_DIM_B)
    bk = bk.reshape(bsz, s, N_HEADS_B, HEAD_DIM_B) * (HEAD_DIM_B ** -0.5)
    bv = b_v.reshape(bsz, s, N_HEADS_B, HEAD_DIM_B)
    b_gates = jnp.moveaxis(b_gates.reshape(bsz, s, N_DIR, 2, N_HEADS_B), 2, 0)
    i_pre = b_gates[..., 0, :] + mlstm_i_bias.astype(jnp.float32)[:, None, None, :]
    f_pre = b_gates[..., 1, :] + mlstm_f_bias.astype(jnp.float32)[:, None, None, :]
    h_b = (run_mlstm(bq, bk, bv, i_pre[0], f_pre[0])
           + flip_seq(run_mlstm(flip_seq(bq), flip_seq(bk), flip_seq(bv), flip_seq(i_pre[1]), flip_seq(f_pre[1]))))
    h_b = head_layernorm(h_b, mlstm_norm_g.astype(jnp.float32).reshape(N_HEADS_B, HEAD_DIM_B))
    h_b = (h_b * jax.nn.sigmoid(b_o.reshape(bsz, s, N_HEADS_B, HEAD_DIM_B))).reshape(bsz, s, WIDTH_B)

    gate_a, gate_b = jnp.split(jax.nn.sigmoid(merge), 2, axis=-1)
    y = (gate_a * jnp.einsum("bse,ed->bsd", o_a, w_branch_a.astype(jnp.float32))
         + gate_b * jnp.einsum("bse,ed->bsd", h_b, w_branch_b.astype(jnp.float32)))
    return jnp.einsum("bsd,de->bse", y, w_out.astype(jnp.float32))

def hierarchical_moe(h, router_group, router_expert, w_gate, w_up, w_down):
    bsz, s, d = h.shape
    ht = h.reshape(bsz * s, d)
    group_logits = ht @ router_group.astype(jnp.float32)
    group_probs = jax.nn.softmax(group_logits, axis=-1)
    p_group, g_sel = lax.top_k(group_probs, 1)
    expert_logits = (ht @ router_expert.astype(jnp.float32)).reshape(-1, N_GROUPS, EXPERTS_PER_GROUP)
    in_group = jnp.take_along_axis(expert_logits, g_sel[:, :, None], axis=1)[:, 0]
    top_vals, top_idx = lax.top_k(in_group, TOP_K)
    top_w = jax.nn.softmax(top_vals, axis=-1) * p_group
    expert_id = g_sel * EXPERTS_PER_GROUP + top_idx
    combine = jnp.sum(jax.nn.one_hot(expert_id, N_EXPERTS, dtype=jnp.float32) * top_w[..., None], axis=1)
    y = jnp.zeros_like(ht)
    for grp in range(N_GROUPS):
        sl = slice(grp * EXPERTS_PER_GROUP, (grp + 1) * EXPERTS_PER_GROUP)
        hg = jnp.einsum("td,edf->tef", ht, w_gate[sl].astype(jnp.float32))
        hu = jnp.einsum("td,edf->tef", ht, w_up[sl].astype(jnp.float32))
        act = jax.nn.silu(hg) * hu * combine[:, sl, None]
        y = y + jnp.einsum("tef,efd->td", act, w_down[sl].astype(jnp.float32))
    return y.reshape(bsz, s, d)

def first_inputs(seed: int = 0) -> dict:
    key = jax.random.key(seed)
    ks = jax.random.split(key, 24)
    nrm = lambda k, shape, scale: jax.random.normal(k, shape, jnp.float32) * scale
    gain = lambda k, shape: 1.0 + 0.02 * jax.random.normal(k, shape, jnp.float32)
    dt = jnp.exp(jax.random.uniform(ks[9], (DEPTH, N_DIR, N_HEADS_A), jnp.float32,
                                    np.log(1e-3), np.log(1e-1)))
    return {
        "x": nrm(ks[0], (BATCH, SEQ, D_MODEL), 1.0),
        "c": nrm(ks[1], (BATCH, D_MODEL), 1.0),
        "ada_w": nrm(ks[2], (DEPTH, D_MODEL, N_MOD * D_MODEL), 0.5 * D_MODEL ** -0.5),
        "ada_b": nrm(ks[3], (DEPTH, N_MOD * D_MODEL), 0.01),
        "norm_mix_g": gain(ks[4], (DEPTH, D_MODEL)),
        "norm_ffn_g": gain(ks[5], (DEPTH, D_MODEL)),
        "w_in": nrm(ks[6], (DEPTH, D_MODEL, D_IN), D_MODEL ** -0.5),
        "gdn_conv_w": nrm(ks[7], (DEPTH, CONV_K, 3 * WIDTH_A), CONV_K ** -0.5),
        "gdn_a_log": jnp.log(jax.random.uniform(ks[8], (DEPTH, N_DIR, N_HEADS_A), jnp.float32, 1.0, 16.0)),
        "gdn_dt_bias": jnp.log(jnp.expm1(dt)),
        "gdn_norm_g": gain(ks[10], (DEPTH, HEAD_DIM_A)),
        "mlstm_conv_w": nrm(ks[11], (DEPTH, CONV_K, 2 * WIDTH_B), CONV_K ** -0.5),
        "mlstm_i_bias": nrm(ks[12], (DEPTH, N_DIR, N_HEADS_B), 0.1),
        "mlstm_f_bias": 3.0 + 3.0 * jax.random.uniform(ks[13], (DEPTH, N_DIR, N_HEADS_B), jnp.float32),
        "mlstm_norm_g": gain(ks[14], (DEPTH, WIDTH_B)),
        "w_branch_a": nrm(ks[15], (DEPTH, WIDTH_A, D_MODEL), WIDTH_A ** -0.5),
        "w_branch_b": nrm(ks[16], (DEPTH, WIDTH_B, D_MODEL), WIDTH_B ** -0.5),
        "w_out": nrm(ks[17], (DEPTH, D_MODEL, D_MODEL), D_MODEL ** -0.5),
        "router_group": nrm(ks[18], (DEPTH, D_MODEL, N_GROUPS), D_MODEL ** -0.5),
        "router_expert": nrm(ks[19], (DEPTH, D_MODEL, N_EXPERTS), D_MODEL ** -0.5),
        "w_gate": nrm(ks[20], (DEPTH, N_EXPERTS, D_MODEL, D_EXPERT), D_MODEL ** -0.5),
        "w_up": nrm(ks[21], (DEPTH, N_EXPERTS, D_MODEL, D_EXPERT), D_MODEL ** -0.5),
        "w_down": nrm(ks[22], (DEPTH, N_EXPERTS, D_EXPERT, D_MODEL), D_EXPERT ** -0.5),
        "final_norm_g": gain(ks[23], (D_MODEL,)),
    }

def first_block(x, c, ada_w, ada_b, norm_mix_g, norm_ffn_g, w_in, gdn_conv_w, gdn_a_log,
              gdn_dt_bias, gdn_norm_g, mlstm_conv_w, mlstm_i_bias, mlstm_f_bias, mlstm_norm_g,
              w_branch_a, w_branch_b, w_out, router_group, router_expert, w_gate, w_up, w_down,
              final_norm_g):
    out_dtype = x.dtype
    h_res = x.astype(jnp.float32)
    c_act = jax.nn.silu(c.astype(jnp.float32))
    for l in range(DEPTH):
        mod = c_act @ ada_w[l].astype(jnp.float32) + ada_b[l].astype(jnp.float32)
        sh1, sc1, gt1, sh2, sc2, gt2 = [m[:, None, :] for m in jnp.split(mod, N_MOD, axis=-1)]
        hn = rmsnorm(h_res, norm_mix_g[l]) * (1.0 + sc1) + sh1
        h_res = h_res + gt1 * hybrid_mixer(
            hn, w_in[l], gdn_conv_w[l], gdn_a_log[l], gdn_dt_bias[l], gdn_norm_g[l],
            mlstm_conv_w[l], mlstm_i_bias[l], mlstm_f_bias[l], mlstm_norm_g[l],
            w_branch_a[l], w_branch_b[l], w_out[l])
        hn = rmsnorm(h_res, norm_ffn_g[l]) * (1.0 + sc2) + sh2
        h_res = h_res + gt2 * hierarchical_moe(hn, router_group[l], router_expert[l],
                                               w_gate[l], w_up[l], w_down[l])
    return rmsnorm(h_res, final_norm_g).astype(out_dtype)


DEPTH_2 = 2

MLA_HEADS = 4
QK_NOPE_DIM = 128
QK_ROPE_DIM = 64
QK_HEAD_DIM = QK_NOPE_DIM + QK_ROPE_DIM
V_HEAD_DIM = 128
Q_LORA_RANK = 256
KV_LORA_RANK = 128
ROPE_THETA = 10000.0
SB_HEADS = 4
SB_HEAD_DIM = 128
D_FF = 2816
CONV_WIDTH = 3
BLOCK_Q = 128
SUB = 16
N_SUB = BLOCK_Q // SUB

MLA_WIDTH = MLA_HEADS * V_HEAD_DIM
SB_WIDTH = SB_HEADS * SB_HEAD_DIM
IN_SPLITS = (Q_LORA_RANK, KV_LORA_RANK, QK_ROPE_DIM, SB_WIDTH, SB_WIDTH, SB_WIDTH, D_MODEL, D_MODEL)
D_IN_2 = sum(IN_SPLITS)
IN_SPLIT_POINTS = [sum(IN_SPLITS[:i + 1]) for i in range(len(IN_SPLITS) - 1)]


def rms_norm(x, g):
    x32 = x.astype(jnp.float32)
    y = x32 * lax.rsqrt(jnp.mean(x32 * x32, axis=-1, keepdims=True) + EPS)
    return (y * g.astype(jnp.float32)).astype(x.dtype)

def rope(x, positions):
    dr = x.shape[-1]
    half = dr // 2
    inv_freq = 1.0 / (ROPE_THETA ** (jnp.arange(half, dtype=jnp.float32) * (2.0 / dr)))
    ang = positions.astype(jnp.float32)[..., None] * inv_freq
    ang = ang.reshape(ang.shape[:2] + (1,) * (x.ndim - 3) + (half,))
    cos, sin = jnp.cos(ang), jnp.sin(ang)
    x32 = x.astype(jnp.float32)
    x1, x2 = x32[..., :half], x32[..., half:]
    return jnp.concatenate([x1 * cos - x2 * sin, x2 * cos + x1 * sin], axis=-1).astype(x.dtype)

def causal_softmax_attention(q, k, v):
    b, s, h, _ = q.shape
    scale = QK_HEAD_DIM ** -0.5
    qh = q.transpose(0, 2, 1, 3).astype(jnp.float32)
    kh = k.transpose(0, 2, 1, 3).astype(jnp.float32)
    vh = v.transpose(0, 2, 1, 3).astype(jnp.float32)
    outs = []
    for i in range(s // BLOCK_Q):
        st = i * BLOCK_Q
        ln = st + BLOCK_Q
        sc = jnp.einsum('bhqd,bhkd->bhqk', qh[:, :, st:ln], kh[:, :, :ln]) * scale
        mask = np.arange(ln)[None, :] <= np.arange(st, ln)[:, None]
        p = jax.nn.softmax(jnp.where(mask, sc, -jnp.inf), axis=-1)
        outs.append(jnp.einsum('bhqk,bhkd->bhqd', p, vh[:, :, :ln]))
    o = jnp.concatenate(outs, axis=2)
    return o.transpose(0, 2, 1, 3).reshape(b, s, h * v.shape[-1]).astype(v.dtype)

def reverse_cumsum_keys(l):
    lead = l.shape[:-1]
    nk = l.shape[-1] // BLOCK_Q
    r = l.reshape(lead + (nk, N_SUB, SUB))
    c0 = lax.cumsum(r, axis=r.ndim - 1, reverse=True)
    s0 = c0[..., 0]
    c1 = lax.cumsum(s0, axis=s0.ndim - 1, reverse=True)
    s1 = c1[..., 0]
    c2 = lax.cumsum(s1, axis=s1.ndim - 1, reverse=True) - s1
    tot = c0 + (c1 - s0)[..., None] + c2[..., None, None]
    return tot.reshape(l.shape)

def stick_breaking_attention(q, k, v):
    b, s, h, d = q.shape
    scale = d ** -0.5
    qh = q.transpose(0, 2, 1, 3).astype(jnp.float32)
    kh = k.transpose(0, 2, 1, 3).astype(jnp.float32)
    vh = v.transpose(0, 2, 1, 3).astype(jnp.float32)
    outs = []
    for i in range(s // BLOCK_Q):
        st = i * BLOCK_Q
        ln = st + BLOCK_Q
        z = jnp.einsum('bhqd,bhkd->bhqk', qh[:, :, st:ln], kh[:, :, :ln]) * scale
        past = np.arange(ln)[None, :] < np.arange(st, ln)[:, None]
        l = jnp.where(past, jax.nn.log_sigmoid(-z), 0.0)
        a = jnp.where(past, jnp.exp(z + reverse_cumsum_keys(l)), 0.0)
        outs.append(jnp.einsum('bhqk,bhkd->bhqd', a, vh[:, :, :ln]))
    o = jnp.concatenate(outs, axis=2)
    return o.transpose(0, 2, 1, 3).reshape(b, s, h * d).astype(v.dtype)

def causal_depthwise_conv(u, w, bias):
    ch = u.shape[-1]
    out = lax.conv_general_dilated(
        u, w[:, None, :].astype(u.dtype), window_strides=(1,),
        padding=[(CONV_WIDTH - 1, 0)], dimension_numbers=('NWC', 'WIO', 'NWC'),
        feature_group_count=ch)
    return out + bias

def second_inputs(seed: int = 0) -> dict:
    key = jax.random.key(seed)
    ks = jax.random.split(key, 24)
    f32 = jnp.float32

    def nrm(k, shape, scale):
        return jax.random.normal(k, shape, f32) * scale

    def gain(k, n):
        return 1.0 + 0.02 * jax.random.normal(k, (DEPTH_2, n), f32)

    return {
        "x": nrm(ks[0], (BATCH, SEQ, D_MODEL), 1.0),
        "c": nrm(ks[1], (BATCH, D_MODEL), 1.0),
        "positions": jnp.broadcast_to(jnp.arange(SEQ, dtype=jnp.int32)[None, :], (BATCH, SEQ)),
        "w_ada": nrm(ks[2], (DEPTH_2, D_MODEL, N_MOD * D_MODEL), 0.5 * D_MODEL ** -0.5),
        "b_ada": nrm(ks[3], (DEPTH_2, N_MOD * D_MODEL), 0.02),
        "g_norm1": gain(ks[4], D_MODEL),
        "w_in": nrm(ks[5], (DEPTH_2, D_MODEL, D_IN_2), D_MODEL ** -0.5),
        "b_in": nrm(ks[6], (DEPTH_2, D_IN_2), 0.02),
        "g_q_lat": gain(ks[7], Q_LORA_RANK),
        "w_uq": nrm(ks[8], (DEPTH_2, Q_LORA_RANK, MLA_HEADS * QK_HEAD_DIM), Q_LORA_RANK ** -0.5),
        "g_kv_lat": gain(ks[9], KV_LORA_RANK),
        "w_ukv": nrm(ks[10], (DEPTH_2, KV_LORA_RANK, MLA_HEADS * (QK_NOPE_DIM + V_HEAD_DIM)), KV_LORA_RANK ** -0.5),
        "g_q_head": gain(ks[11], QK_HEAD_DIM),
        "g_k_head": gain(ks[12], QK_HEAD_DIM),
        "w_branch_mla": nrm(ks[13], (DEPTH_2, MLA_WIDTH, D_MODEL), MLA_WIDTH ** -0.5),
        "w_branch_sb": nrm(ks[14], (DEPTH_2, SB_WIDTH, D_MODEL), SB_WIDTH ** -0.5),
        "w_out": nrm(ks[15], (DEPTH_2, D_MODEL, D_MODEL), D_MODEL ** -0.5),
        "g_norm2": gain(ks[16], D_MODEL),
        "w_up": nrm(ks[17], (DEPTH_2, D_MODEL, 2 * D_FF), D_MODEL ** -0.5),
        "w_conv": nrm(ks[18], (DEPTH_2, CONV_WIDTH, 2 * D_FF), CONV_WIDTH ** -0.5),
        "b_conv": nrm(ks[19], (DEPTH_2, 2 * D_FF), 0.02),
        "w_down": nrm(ks[20], (DEPTH_2, D_FF, D_MODEL), D_FF ** -0.5),
    }

def second_block(x, c, positions, w_ada, b_ada, g_norm1, w_in, b_in, g_q_lat, w_uq, g_kv_lat,
              w_ukv, g_q_head, g_k_head, w_branch_mla, w_branch_sb, w_out, g_norm2, w_up,
              w_conv, b_conv, w_down):
    b, s, _ = x.shape
    c_act = jax.nn.silu(c)
    for l in range(DEPTH_2):
        mod = c_act @ w_ada[l] + b_ada[l]
        sh1, sc1, gt1, sh2, sc2, gt2 = [m[:, None, :] for m in jnp.split(mod, N_MOD, axis=-1)]

        h = rms_norm(x, g_norm1[l]) * (1.0 + sc1) + sh1
        u = h @ w_in[l] + b_in[l]
        q_lat, kv_lat, k_rope, q_sb, k_sb, v_sb, gate_mla, gate_sb = jnp.split(u, IN_SPLIT_POINTS, axis=-1)

        q = (rms_norm(q_lat, g_q_lat[l]) @ w_uq[l]).reshape(b, s, MLA_HEADS, QK_HEAD_DIM)
        kv = (rms_norm(kv_lat, g_kv_lat[l]) @ w_ukv[l]).reshape(b, s, MLA_HEADS, QK_NOPE_DIM + V_HEAD_DIM)
        k_nope, v_mla = kv[..., :QK_NOPE_DIM], kv[..., QK_NOPE_DIM:]
        k_rope_h = jnp.broadcast_to(k_rope[:, :, None, :], (b, s, MLA_HEADS, QK_ROPE_DIM))
        k = jnp.concatenate([k_nope, k_rope_h], axis=-1)
        q = rms_norm(q, g_q_head[l])
        k = rms_norm(k, g_k_head[l])
        q = jnp.concatenate([q[..., :QK_NOPE_DIM], rope(q[..., QK_NOPE_DIM:], positions)], axis=-1)
        k = jnp.concatenate([k[..., :QK_NOPE_DIM], rope(k[..., QK_NOPE_DIM:], positions)], axis=-1)
        y_mla = causal_softmax_attention(q, k, v_mla)

        y_sb = stick_breaking_attention(
            q_sb.reshape(b, s, SB_HEADS, SB_HEAD_DIM),
            k_sb.reshape(b, s, SB_HEADS, SB_HEAD_DIM),
            v_sb.reshape(b, s, SB_HEADS, SB_HEAD_DIM))

        merged = (jax.nn.sigmoid(gate_mla) * (y_mla @ w_branch_mla[l])
                  + jax.nn.sigmoid(gate_sb) * (y_sb @ w_branch_sb[l]))
        x = x + gt1 * (merged @ w_out[l])

        h = rms_norm(x, g_norm2[l]) * (1.0 + sc2) + sh2
        up = causal_depthwise_conv(h @ w_up[l], w_conv[l], b_conv[l])
        a, v_ff = jnp.split(up, 2, axis=-1)
        x = x + gt2 * ((jax.nn.silu(a) * v_ff) @ w_down[l])
    return x


def setup_inputs(seed=0):
    out = dict(first_inputs(seed))
    for name, value in second_inputs(seed + 1).items():
        if name != "x":
            out[name + "_2"] = value
    return out


def reference(
    x, c, ada_w, ada_b, norm_mix_g, norm_ffn_g, w_in, gdn_conv_w, gdn_a_log, gdn_dt_bias,
    gdn_norm_g, mlstm_conv_w, mlstm_i_bias, mlstm_f_bias, mlstm_norm_g, w_branch_a, w_branch_b,
    w_out, router_group, router_expert, w_gate, w_up, w_down, final_norm_g, c_2, positions_2,
    w_ada_2, b_ada_2, g_norm1_2, w_in_2, b_in_2, g_q_lat_2, w_uq_2, g_kv_lat_2, w_ukv_2,
    g_q_head_2, g_k_head_2, w_branch_mla_2, w_branch_sb_2, w_out_2, g_norm2_2, w_up_2, w_conv_2,
    b_conv_2, w_down_2,
):
    x = first_block(
        x, c, ada_w, ada_b, norm_mix_g, norm_ffn_g, w_in, gdn_conv_w, gdn_a_log, gdn_dt_bias,
        gdn_norm_g, mlstm_conv_w, mlstm_i_bias, mlstm_f_bias, mlstm_norm_g, w_branch_a,
        w_branch_b, w_out, router_group, router_expert, w_gate, w_up, w_down, final_norm_g,
    )
    return second_block(
        x, c_2, positions_2, w_ada_2, b_ada_2, g_norm1_2, w_in_2, b_in_2, g_q_lat_2, w_uq_2,
        g_kv_lat_2, w_ukv_2, g_q_head_2, g_k_head_2, w_branch_mla_2, w_branch_sb_2, w_out_2,
        g_norm2_2, w_up_2, w_conv_2, b_conv_2, w_down_2,
    )


_drawn_inputs = setup_inputs


def setup_inputs(seed=0):
    import zlib

    import numpy as np

    out = dict(_drawn_inputs(seed))
    spreads = {}
    factors = {'ada_b': 5.421,
     'norm_mix_g': 8.0,
     'norm_ffn_g': 5.012,
     'gdn_norm_g': 8.0,
     'mlstm_i_bias': 31.403,
     'mlstm_f_bias': 2.734,
     'mlstm_norm_g': 8.0,
     'final_norm_g': 2.78,
     'g_norm1_2': 8.0,
     'b_in_2': 7.641,
     'g_q_lat_2': 8.0,
     'g_kv_lat_2': 8.0,
     'g_q_head_2': 8.0,
     'g_k_head_2': 8.0,
     'g_norm2_2': 6.512,
     'b_conv_2': 7.055}
    for name, (base, spread) in spreads.items():
        noise = np.random.default_rng([zlib.crc32(name.encode()), seed]).standard_normal(out[name].shape)
        drawn = base * np.exp(spread * noise) if base else spread * noise
        out[name] = __import__('jax').numpy.asarray(drawn.astype(out[name].dtype))
    for name, factor in factors.items():
        out[name] = (out[name] * factor).astype(out[name].dtype)
    return out
```

```python
from contextlib import ExitStack

import concourse.bass as bass
from concourse import mybir

ALU = mybir.AluOpType
ACT = mybir.ActivationFunctionType
F32 = mybir.dt.float32
I32 = mybir.dt.int32
U32 = mybir.dt.uint32
AX_X = mybir.AxisListType.X

P = 128
S = 512
NT = S // P
D = 1024
KC = D // P
EPS = 1e-6
NEG = -1e30
WA = 512
NH = 8
HD = 64
CH = 64
NMOD = 6 * KC
TAPS = 5
NE = 32
DE = 256
NG = 4
RING = 3
SLOT = KC * 512
LAYERS = 2
DFF = 2816
FT = DFF // P
MH = 4
NOPE, ROPE = 128, 64
MLA_SCALE = (NOPE + ROPE) ** -0.5
SB_SCALE = 128 ** -0.5
PI2 = 6.283185307179586

MASKS = ["ident", "ones", "cum0", "cum1", "blk64", "nstr0", "nstr1", "ninc0", "ninc1", "b16n", "off16",
         "ncaus", "nml0", "nml1", "trin", "negones", "sbneg", "sbpast", "rot", "iota"]

N_ADA = 2 * NMOD * P // D
B1_BLOCKS = N_ADA + 2 + 1 + 1 + 3 + 1 + 6 + 2
MOE_BLOCKS = 3
L_BLOCKS = N_ADA + 4 + 1 + 6 + 2 + 11 + 6
MOE_TRIPS = -(-((2 * S + NE * (P - 1)) // P) // 2)
MOE_SLOTS = 2 * MOE_TRIPS
MOE_AT = B1_BLOCKS
L_AT = B1_BLOCKS + MOE_BLOCKS * MOE_TRIPS
B1_GROUPS = 4 + 8 + 4 + 4 + 12 + 4 + 32 + 8 + 4
L_GROUPS = 4 + 4 + 4 + 4 + 8 + 4 + 4 + 32 + 8 + 2 * FT + 8
DVE_LAYER = 262
ACT_LAYER = 44


def masks_array():
    import numpy as np
    p, f = np.arange(P)[:, None], np.arange(P)[None, :]
    same = p // CH == f // CH
    hide = lambda keep: np.where(keep, 0.0, NEG)
    rot = np.zeros((P, P))
    for m in range(ROPE // 2):
        rot[m + ROPE // 2, m] = -1.0
        rot[m, m + ROPE // 2] = 1.0
    same16 = p // 16 == f // 16
    made = {
        "ident": p == f, "ones": np.ones((P, P)), "cum0": same & (p <= f), "cum1": same & (p >= f), "blk64": same,
        "nstr0": hide(same & (p < f)), "nstr1": hide(same & (p > f)), "ninc0": hide(same & (p <= f)),
        "ninc1": hide(same & (p >= f)), "b16n": -1.0 * same16, "off16": ~same16, "ncaus": hide(f <= p),
        "nml0": hide(p <= f), "nml1": hide(p >= f), "trin": -1.0 * (p >= f), "negones": -np.ones((P, P)),
        "sbneg": hide(p < f), "sbpast": p < f, "rot": rot, "iota": f + 0 * p}
    return np.concatenate([np.asarray(made[n], np.float32) for n in MASKS], axis=1)


def freq_array():
    import numpy as np
    half = ROPE // 2
    inv = (1.0 / (10000.0 ** (np.arange(half, dtype=np.float32) * np.float32(2.0 / ROPE)))).astype(np.float32)
    return np.concatenate([inv, inv])[:, None]


class Own:

    def __init__(self, eng, sem):
        self.eng, self.sem, self.n, self.reg, self.per = eng, sem, 0, None, 0

    def __call__(self, ins):
        self.n += 1
        ins.then_inc(self.sem, 1)
        self.eng.wait_ge(self.sem, self.n if self.reg is None else self.reg * self.per + self.n)

    def enter(self, reg, per):
        self.reg, self.per, self.start = reg, per, self.n

    def leave(self, trips):
        used = self.n - self.start
        assert used == self.per, (self.sem, used, self.per)
        self.n, self.reg = self.start + trips * self.per, None


def build(nc, a, hn_rows, idx_rows, y_rows, out):
    with ExitStack() as ctx:
        def sb(name, shape, dt=F32):
            return ctx.enter_context(nc.sbuf_tensor(name, shape, dt))

        def sem(name):
            return ctx.enter_context(nc.semaphore(name))

        H = sb("H", [P, KC, S])
        HN = sb("HN", [P, KC, S])
        W = [sb(f"W{r}", [P, SLOT]) for r in range(RING)]
        MK = sb("MK", [P, len(MASKS), P])
        mask = {n: MK[:, i, :] for i, n in enumerate(MASKS)}
        ident, ones = mask["ident"], mask["ones"]
        PACK = sb("PACK", [P, 3, P])
        VEC = sb("VEC", [P, 3, P])
        MOD = sb("MOD", [P, NMOD])
        GAIN = sb("GAIN", [P, 2, KC])
        CACT = sb("CACT", [P, KC])
        EPSC = sb("EPSC", [P, 4])
        GW = sb("GW", [P, KC, 64])
        RW = sb("RW", [P, KC, NG + NE])
        BC = sb("BC", [P, 32 + HD + WA])
        IFB = sb("IFB", [NH, 4])
        SQ = sb("SQ", [P, 2, S])
        RSTD = sb("RSTD", [P, S])
        TMP = sb("TMP", [P, 2, S])
        HBT = sb("HBT", [P, NT, S])
        COS, SIN = HBT[0:ROPE, 0, :], HBT[0:ROPE, 1, :]
        ROW = HBT[0:1, 2, :]
        CPAD = sb("CPAD", [P, 2 * (S + 4)])
        GT = sb("GT", [P, NT, 64])
        SM = sb("SM", [P, 208])
        FREQ = sb("FREQ", [ROPE, 1])
        ARENA_N = 21504
        AR = sb("AR", [P, ARENA_N])
        PS = [ctx.enter_context(nc.psum_tensor(f"PS{i}", [P, 512], F32)) for i in range(8)]

        def ar(off, *shape):
            n = 1
            for s in shape:
                n *= s
            assert off + n <= ARENA_N, (off, shape)
            v = AR[:, off:off + n]
            if len(shape) == 2:
                v = v.rearrange("p (a b) -> p a b", b=shape[1])
            elif len(shape) == 3:
                v = v.rearrange("p (a b c) -> p a b c", b=shape[1], c=shape[2])
            elif len(shape) == 4:
                v = v.rearrange("p (a b c d) -> p a b c d", b=shape[1], c=shape[2], d=shape[3])
            return v

        V_GMIX, V_GFFN, V_GFIN, V_ADAB, V_C, V_BCONV = 0, 8, 16, 24, 72, 80
        V2_ADAB, V2_G1, V2_G2, V2_GQL, V2_GKV, V2_C, V2_BIN, V2_GQH, V2_GKH = 0, 48, 56, 64, 66, 67, 75, 106, 108

        w_loaded = [sem(f"w_loaded{r}") for r in range(RING)]
        consts_in, pack_in, x_in = sem("consts_in"), sem("pack_in"), sem("x_in")
        cols_done, cols_ready = sem("cols_done"), sem("cols_ready")
        filled = sem("filled")
        xt_done, h_ready = sem("xt_done"), sem("h_ready")
        cact_ready = sem("cact_ready")
        ada_acc, ada_sum, mod_ready = sem("ada_acc"), sem("ada_sum"), sem("mod_ready")
        sq_ready, ss_done, rstd_ready, hn_ready = sem("sq_ready"), sem("ss_done"), sem("rstd_ready"), sem("hn_ready")
        proj_done, proj_taken = sem("proj_done"), sem("proj_taken")
        merged, res_added = sem("merged"), sem("res_added")
        dve_own, act_own, pool_own = sem("dve_own"), sem("act_own"), sem("pool_own")
        conv_done, conv_out = sem("conv_done"), sem("conv_out")
        down_part = sem("down_part")
        ff_conv, ff_pad, ff_ready, ff_silu = sem("ff_conv"), sem("ff_pad"), sem("ff_ready"), sem("ff_silu")
        gd_intra, gd_kv, gd_o, gd_out, gd_read = sem("gd_intra"), sem("gd_kv"), sem("gd_o"), sem("gd_out"), sem("gd_read")
        gd_rstd, gd_state, gd_var, gd_vnew, gd_zero = sem("gd_rstd"), sem("gd_state"), sem("gd_var"), sem("gd_vnew"), sem("gd_zero")
        gg_abs, gg_cum, gg_exp, gg_ln, gg_ready = sem("gg_abs"), sem("gg_cum"), sem("gg_exp"), sem("gg_ln"), sem("gg_ready")
        gg_sum = sem("gg_sum")
        hb_copied, hb_t = sem("hb_copied"), sem("hb_t")
        hd_done, hd_n, hd_r, hd_rot, hd_sq = sem("hd_done"), sem("hd_n"), sem("hd_r"), sem("hd_rot"), sem("hd_sq")
        hd_ss = sem("hd_ss")
        kd_ready = sem("kd_ready")
        l2_done, l2_r, l2_sq, l2_ss = sem("l2_done"), sem("l2_r"), sem("l2_sq"), sem("l2_ss")
        la_e, la_max, la_out, la_p, la_pt = sem("la_e"), sem("la_max"), sem("la_out"), sem("la_p"), sem("la_pt")
        la_s, la_t, la_y = sem("la_s"), sem("la_t"), sem("la_y")
        lat_n, lat_r, lat_sq, lat_ss = sem("lat_n"), sem("lat_r"), sem("lat_sq"), sem("lat_ss")
        ml_abs, ml_bc, ml_cols, ml_evac, ml_exp = sem("ml_abs"), sem("ml_bc"), sem("ml_cols"), sem("ml_evac"), sem("ml_exp")
        ml_exps, ml_gate_t, ml_h, ml_masked, ml_out = sem("ml_exps"), sem("ml_gate_t"), sem("ml_h"), sem("ml_masked"), sem("ml_out")
        ml_prod, ml_rstd, ml_scan, ml_st, ml_var = sem("ml_prod"), sem("ml_rstd"), sem("ml_scan"), sem("ml_st"), sem("ml_var")
        moe_act, moe_add, moe_down = sem("moe_act"), sem("moe_add"), sem("moe_down")
        moe_up = sem("moe_up")
        oa_copied, oa_t = sem("oa_copied"), sem("oa_t")
        out_ready, out_t, out_written = sem("out_ready"), sem("out_t"), sem("out_written")
        pos_in = sem("pos_in")
        rope_arg, rope_ready = sem("rope_arg"), sem("rope_ready")
        route_arg, route_exp = sem("route_arg"), sem("route_exp")
        row_in = sem("row_in")
        sb_a, sb_ln, sb_out, sb_r, sb_sp = sem("sb_a"), sem("sb_ln"), sem("sb_out"), sem("sb_r"), sem("sb_sp")
        sb_y, sb_z = sem("sb_y"), sem("sb_z")
        tok_copied, tok_done = sem("tok_copied"), sem("tok_done")
        unit_act_done, unit_dve_done, unit_pe_done = sem("unit_act_done"), sem("unit_dve_done"), sem("unit_pe_done")
        wt_done, wt_ready = sem("wt_done"), sem("wt_ready")
        hnt_done, hnt_copied, picked, ranked, blk_ready = (
            sem("hnt_done"), sem("hnt_copied"), sem("picked"), sem("ranked"), sem("blk_ready"))
        sel_ready, table_ready, hn_out, gather_go = sem("sel_ready"), sem("table_ready"), sem("hn_out"), sem("gather_go")
        moe_xt, moe_xc, moe_sg, moe_yb, moe_sum, moe_back = (
            sem("moe_xt"), sem("moe_xc"), sem("moe_sg"), sem("moe_yb"), sem("moe_sum"), sem("moe_back"))
        idx_loaded, gathered, y_written = ([sem(f"{n}{j}") for j in range(2)] for n in ("idx_loaded", "gathered", "y_written"))
        y_gathered = [sem(f"y_gathered{t}") for t in range(NT)]
        block = ctx.enter_context(nc.Block())

        def load(sp, n, it, parts, after):
            if after is not None:
                sp.wait_ge(*after)
            for dst, src in parts:
                sp.dma_start(dst, src).then_inc(w_loaded[n % RING], 32 // len(parts))

        def arrived(eng, n, it):
            v = n // RING * 32 + 32
            eng.wait_ge(w_loaded[n % RING], v if it is None else it[0] * (it[1] // RING * 32) + v)

        def slot(n, kt=KC, cols=512):
            return W[n % RING][:, 0:kt * cols].rearrange("p (k n) -> p k n", n=cols)

        def rows(w, c0, cols):
            return w[:, c0:c0 + cols].rearrange("(k p) n -> p k n", p=P)

        X = ar(0, NT, D)
        PACK1 = [("norm_mix_g", 0, V_GMIX, 8), ("norm_ffn_g", 0, V_GFFN, 8), ("final_norm_g", 0, V_GFIN, 8),
                 ("ada_b", 0, V_ADAB, 48), ("c", 0, V_C, 8), ("mlstm_conv_w", 0, V_BCONV, 40), ("gdn_conv_w", 1, 0, 60)]

        def setup_pool(pool):
            own = Own(pool, pool_own)
            n = 0
            for name, dst in (("masks", MK[:, :, :].rearrange("p m f -> p (m f)")), ("freq", FREQ[:, :])):
                pool.dma_start(dst, a[name]).then_inc(consts_in, 16)
                n += 16
            own(pool.memset(PACK[:, :, :], 0.0))
            for name, pk, r0, nr in PACK1:
                v = a[name]
                flat = {1: "(r c) -> r c", 2: "o (r c) -> (o r) c", 3: "o t (r c) -> (o t r) c"}[len(v.shape)]
                pool.dma_start(PACK[r0:r0 + nr, pk, :], v.rearrange(flat, c=P)).then_inc(pack_in, 16)
            pool.dma_start(GW[:, :, 0:32], rows(a["w_in"][0], 2048, 32)).then_inc(consts_in, 16)
            pool.dma_start(GW[:, :, 32:64], rows(a["w_in"][0], 4128, 32)).then_inc(consts_in, 16)
            pool.dma_start(RW[:, :, 0:NG], rows(a["router_group"][0], 0, NG)).then_inc(consts_in, 16)
            pool.dma_start(RW[:, :, NG:NG + NE], rows(a["router_expert"][0], 0, NE)).then_inc(consts_in, 16)
            for c0, name, w in ((0, "gdn_a_log", 16), (16, "gdn_dt_bias", 16)):
                pool.dma_start(BC[:, c0:c0 + w], a[name].rearrange("o d h -> o (d h)").to_broadcast([P, w])
                               ).then_inc(consts_in, 16)
            for c0, name, w in ((32, "gdn_norm_g", HD), (32 + HD, "mlstm_norm_g", WA)):
                pool.dma_start(BC[:, c0:c0 + w], a[name].to_broadcast([P, w])).then_inc(consts_in, 16)
            for c0, name in ((0, "mlstm_i_bias"), (2, "mlstm_f_bias")):
                pool.dma_start(IFB[:, c0:c0 + 2], a[name].rearrange("o d h -> h (o d)"),
                               allow_slow_non_contiguous=True).then_inc(consts_in, 16)
            for c, v in enumerate((EPS, 1.0, -2.0794415416798357, 0.0)):
                pool.memset(EPSC[:, c:c + 1], v).then_inc(filled, 1)

        N_CONST, N_PACK1 = 12 * 16, 16 * len(PACK1)

        def setup_pe(pe):
            pe.wait_ge(consts_in, N_CONST)
            pe.wait_ge(pack_in, N_PACK1)
            for k in range(2):
                pe.transpose(PS[k][:, 0:P], PACK[:, k, :], ident).then_inc(cols_done, 1)
            pe.wait_ge(x_in, 16)
            for c in range(KC):
                if c >= 6:
                    pe.wait_ge(cols_ready, c - 5)
                for t in range(NT):
                    mm = pe.transpose(PS[(c + 2) % 8][:, t * P:(t + 1) * P], X[:, t, c * P:(c + 1) * P], ident)
                mm.then_inc(xt_done, 1)

        def setup_act(act):
            for k in range(2):
                act.wait_ge(cols_done, k + 1)
                act.activation(VEC[:, k, :], PS[k][:, 0:P], ACT.Copy).then_inc(cols_ready, 1)
            for c in range(KC):
                act.wait_ge(xt_done, c + 1)
                act.activation(H[:, c, :], PS[(c + 2) % 8][:, :], ACT.Copy).then_inc(h_ready, 1)
            act.wait_ge(cols_ready, 2)
            act.activation(CACT[:, :], VEC[:, 0, V_C:V_C + KC], ACT.Silu).then_inc(cact_ready, 1)

        ADA = TMP

        def ada_dve(dve, own, q, n0, it, bias):
            dve.wait_ge(cact_ready, q + 1)
            for b in range(N_ADA):
                n = n0 + b
                arrived(dve, n, it)
                if b >= 2:
                    dve.wait_ge(ada_sum, q * N_ADA + b - 1)
                w = slot(n)
                acc = ADA[:, b % 2, :]
                own(dve.tensor_scalar(acc, w[:, 0, :], CACT[:, 0:1], None, ALU.mult))
                for k in range(1, KC):
                    ins = dve.scalar_tensor_tensor(acc, w[:, k, :], CACT[:, k:k + 1], acc, ALU.mult, ALU.add)
                    own(ins) if k < KC - 1 else ins.then_inc(ada_acc, 1)
            dve.wait_ge(ada_sum, q * N_ADA + N_ADA)
            own(dve.tensor_tensor(MOD[:, :], PS[7][:, 0:NMOD], bias, ALU.add))

        def gains_dve(dve, own, q, g1, g2):
            for j, (g, c0) in enumerate(((g1, KC), (g2, 4 * KC))):
                ins = dve.scalar_tensor_tensor(GAIN[:, j, :], MOD[:, c0:c0 + KC], 1.0, g, ALU.add, ALU.mult)
                own(ins) if j == 0 else ins.then_inc(mod_ready, 1)
            dve.wait_ge(mod_ready, q + 1)

        def ada_pe(pe, q):
            for b in range(N_ADA):
                pe.wait_ge(ada_acc, q * N_ADA + b + 1)
                for j in range(4):
                    mm = pe.matmul(PS[7][:, 4 * b + j:4 * b + j + 1], ADA[:, b % 2, j * P:(j + 1) * P], ones[:, 0:1],
                                   start=True, stop=True)
                mm.then_inc(ada_sum, 1)

        def norm_act(act, own, k):
            for c in range(KC):
                if c >= 2:
                    act.wait_ge(ss_done, k * KC + c - 1)
                act.activation(SQ[:, c % 2, :], H[:, c, :], ACT.Square).then_inc(sq_ready, 1)
            act.wait_ge(ss_done, k * KC + KC)
            own(act.activation(RSTD[:, :], PS[6][:, :], ACT.Ln, scale=1.0 / D, bias=EPSC[:, 0:1]))
            act.activation(RSTD[:, :], RSTD[:, :], ACT.Exp, scale=-0.5).then_inc(rstd_ready, 1)

        def norm_pe(pe, k):
            for c in range(KC):
                pe.wait_ge(sq_ready, k * KC + c + 1)
                pe.matmul(PS[6][:, :], ones, SQ[:, c % 2, :], start=(c == 0), stop=(c == KC - 1)).then_inc(ss_done, 1)

        def norm_dve(dve, own, k, j):
            dve.wait_ge(rstd_ready, k + 1)
            for c in range(KC):
                own(dve.scalar_tensor_tensor(TMP[:, c % 2, :], H[:, c, :], GAIN[:, j, c:c + 1], RSTD[:, :],
                                             ALU.mult, ALU.mult))
                sh = 3 * j * KC + c
                dve.tensor_scalar(HN[:, c, :], TMP[:, c % 2, :], MOD[:, sh:sh + 1], None, ALU.add).then_inc(hn_ready, 1)

        def group(pe, g, it, products):
            v = g if it is None else it[0] * it[1] + g
            if it is not None or g >= 4:
                pe.wait_ge(proj_taken, v - 3)
            for i, (l, r) in enumerate(products):
                m, n = l.shape[-1], 1
                for s in r.shape[1:]:
                    n *= s
                o = PS[g % 4][0:m, 0:n]
                if len(r.shape) == 3:
                    o = o.rearrange("p (a b) -> p a b", b=r.shape[2])
                mm = pe.matmul(o, l, r, start=(i == 0), stop=(i == len(products) - 1))
            mm.then_inc(proj_done, 1)
            return mm

        def take(act, g, it):
            act.wait_ge(proj_done, (g if it is None else it[0] * it[1] + g) + 1)
            return PS[g % 4]

        def channel_products(w, m, rhs, kt=KC, width=P):
            return [(w[:, k, m * P:m * P + width], rhs[:, k, :]) for k in range(kt)]

        def token_products(w, t, lhs, kt=KC):
            return [(lhs[:, k, t * P:(t + 1) * P], w[:, k, :]) for k in range(kt)]

        MG = ar(0, 2, 4, S)
        YT = ar(4096, KC, S)

        def merge_pe(pe, n0, g0, it, gi, left, right):
            for hf in range(2):
                n = n0 + 3 * hf
                for b in range(3):
                    arrived(pe, n + b, it)
                wa = W[(n + 2) % RING][:, 0:2048].rearrange("p (k n) -> p k n", n=512)
                wb = W[(n + 2) % RING][:, 2048:4096].rearrange("p (k n) -> p k n", n=512)
                for m in range(4):
                    g = g0 + 16 * hf + 4 * m
                    group(pe, g, gi, channel_products(slot(n), m, HN))
                    group(pe, g + 1, gi, channel_products(slot(n + 1), m, HN))
                    group(pe, g + 2, gi, channel_products(wa, m, left, 4))
                    group(pe, g + 3, gi, channel_products(wb, m, right, 4))

        def merge_act(act, q, g0, it, bias):
            for c in range(KC):
                if c >= 2:
                    act.wait_ge(merged, q * KC + c - 1)
                for j in range(4):
                    b = take(act, g0 + 4 * c + j, it)
                    if j < 2:
                        kw = {} if bias is None else {"bias": bias[j][:, c:c + 1]}
                        act.activation(MG[:, c % 2, j, :], b[:, :], ACT.Sigmoid, **kw).then_inc(proj_taken, 1)
                    else:
                        act.activation(MG[:, c % 2, j, :], b[:, :], ACT.Copy).then_inc(proj_taken, 1)

        def merge_dve(dve, own, q, g0, it):
            for c in range(KC):
                v = g0 + 4 * c + 4
                dve.wait_ge(proj_taken, v if it is None else it[0] * it[1] + v)
                m = MG[:, c % 2, :, :]
                own(dve.tensor_tensor(m[:, 0:2, :], m[:, 0:2, :], m[:, 2:4, :], ALU.mult))
                dve.tensor_tensor(YT[:, c, :], m[:, 0, :], m[:, 1, :], ALU.add).then_inc(merged, 1)

        def residual_act(act, q, g0, it, gate):
            for c in range(KC):
                if c >= 2:
                    act.wait_ge(res_added, q * KC + c - 1)
                b = take(act, g0 + c, it)
                act.activation(TMP[:, c % 2, :], b[:, :], ACT.Copy, scale=MOD[:, gate + c:gate + c + 1]
                               ).then_inc(proj_taken, 1)

        def residual_dve(dve, q, g0, it):
            for c in range(KC):
                v = g0 + c + 1
                dve.wait_ge(proj_taken, v if it is None else it[0] * it[1] + v)
                dve.tensor_tensor(H[:, c, :], H[:, c, :], TMP[:, c % 2, :], ALU.add).then_inc(res_added, 1)

        def out_pe(pe, q, n0, g0, it, gi):
            pe.wait_ge(merged, q * KC + KC)
            for hf in range(2):
                arrived(pe, n0 + hf, it)
                for m in range(4):
                    group(pe, g0 + 4 * hf + m, gi, channel_products(slot(n0 + hf), m, YT))

        def pad(i, width):
            return CPAD[:, (i % 2) * (S + 4):(i % 2) * (S + 4) + width]

        def conv_pads(pool):
            for i in range(2):
                pool.memset(pad(i, 2), 0.0).then_inc(filled, 1)
                pool.memset(pad(i, S + 4)[:, S + 2:S + 4], 0.0).then_inc(filled, 1)

        def conv_act(act, tiles, idx0, g0, dst):
            def silu(m):
                act.wait_ge(conv_done, idx0 + m + 1)
                act.activation(dst[:, m, :], TMP[:, (idx0 + m) % 2, :], ACT.Silu).then_inc(conv_out, 1)
            for m in range(tiles):
                i = idx0 + m
                b = take(act, g0 + m, None)
                if i >= 2:
                    act.wait_ge(conv_done, i - 1)
                act.activation(pad(i, S + 2)[:, 2:S + 2], b[:, :], ACT.Copy).then_inc(proj_taken, 1)
                if m >= 1:
                    silu(m - 1)
            silu(tiles - 1)

        def conv_dve(dve, own, tiles, idx0, g0, wcol):
            for m in range(tiles):
                i = idx0 + m
                dve.wait_ge(proj_taken, g0 + m + 1)
                if i >= 2:
                    dve.wait_ge(conv_out, i - 1)
                acc, x = TMP[:, i % 2, :], pad(i, S + 4)
                own(dve.tensor_scalar(acc, x[:, 0:S], wcol(0, m), None, ALU.mult))
                for k in range(1, TAPS):
                    ins = dve.scalar_tensor_tensor(acc, x[:, k:k + S], wcol(k, m), acc, ALU.mult, ALU.add)
                    own(ins) if k < TAPS - 1 else ins.then_inc(conv_done, 1)
                dve.wait_ge(conv_done, i + 1)

        BQK = ar(0, KC, S)
        BV = ar(4096, NT, NH, HD + 1)
        EW = ar(6176, 2, 2, NT, S)
        HACC = ar(14368, NT, WA)
        ML = ar(16416, 2, 4, S)
        MD = SQ
        MLC = SM[:, 0:128].rearrange("p (d w t h) -> p d w t h", d=2, w=2, t=NT)
        DEN = SM[:, 128:136]
        LNS = SM[:, 136:136 + 64]
        BO = ar(6176, NT, WA)
        HSQ = ar(8224, NT, WA)

        def span(d, s):
            return slice(s * P, S) if d == 0 else slice(0, (s + 1) * P)

        def ml_gates_pe(pe):
            pe.wait_ge(proj_taken, 4)
            for kind in range(2):
                for d in range(2):
                    for t in range(NT):
                        c = 32 + 16 * d + 8 * kind
                        mm = pe.transpose(PS[4 + 2 * kind + d][0:NH, t * P:(t + 1) * P], GT[:, t, c:c + NH], ident)
            mm.then_inc(ml_gate_t, 1)
            pe.wait_ge(ml_scan, 1)
            pe.wait_ge(ml_exp, 2)
            for d in range(2):
                for w in range(2):
                    for t in range(NT):
                        c = ((d * 2 + w) * NT + t) * NH
                        mm = pe.transpose(PS[7][:, c:c + NH], ML[0:NH, d, w, t * P:(t + 1) * P], ident[0:NH, 0:NH])
            mm.then_inc(ml_gate_t, 1)

        def ml_gates_dve(dve, own):
            dve.wait_ge(ml_gate_t, 1)
            dve.wait_ge(consts_in, N_CONST)
            one = EPSC[0:NH, 1:2].to_broadcast([NH, S])
            for d in range(2):
                a_, b_, m_, t_ = (ML[0:NH, d, j, :] for j in range(4))
                own(dve.tensor_scalar(b_, PS[6 + d][0:NH, :], IFB[:, 2 + d:3 + d], None, ALU.add))
                dve.scalar_tensor_tensor(t_, b_, -1.0, b_, ALU.mult, ALU.max).then_inc(ml_abs, 1)
            for d in range(2):
                a_, b_, m_, t_ = (ML[0:NH, d, j, :] for j in range(4))
                rev = (lambda v: v) if d == 0 else (lambda v: v[:, ::-1])
                dve.wait_ge(ml_exp, d + 1)
                own(dve.scalar_tensor_tensor(b_, b_, 0.0, t_, ALU.min, ALU.subtract))
                own(dve.tensor_tensor_scan(rev(t_), one, rev(b_), 0.0, ALU.mult, ALU.add))
                own(dve.scalar_tensor_tensor(a_, PS[4 + d][0:NH, :], IFB[:, d:d + 1], t_, ALU.add, ALU.subtract))
                own(dve.tensor_tensor_scan(rev(m_), rev(a_), rev(a_), 0.0, ALU.max, ALU.max))
                own(dve.scalar_tensor_tensor(b_, t_, -1.0, m_, ALU.mult, ALU.subtract))
                ins = dve.tensor_scalar(m_, m_, -1.0, None, ALU.mult)
                own(ins) if d == 0 else ins.then_inc(ml_scan, 1)

        def ml_gates_act(act, own):
            for d in range(2):
                t_ = ML[0:NH, d, 3, :]
                act.wait_ge(ml_abs, d + 1)
                own(act.activation(t_, t_, ACT.Exp, scale=-1.0))
                act.activation(t_, t_, ACT.Ln, bias=EPSC[0:NH, 1:2]).then_inc(ml_exp, 1)
            act.wait_ge(ml_gate_t, 2)
            own(act.activation(SM[:, 0:128], PS[7][:, 0:128], ACT.Copy))
            for d in range(2):
                own(act.activation(MLC[:, d, 1, :, :], MLC[:, d, 1, :, :], ACT.Exp))
            act.sem_inc(ml_cols, 1)

        def ml_pe(pe):
            def weigh(h):
                pe.wait_ge(ml_prod, 4 * h + 4)
                if h >= 2:
                    pe.wait_ge(ml_evac, 2 * (h - 2) + 2)
                for d in range(2):
                    o = PS[4 + 2 * (h % 2) + d]
                    for t in range(NT):
                        keys = range(t + 1) if d == 0 else range(t, NT)
                        for s in keys:
                            mm = pe.matmul(o[:, t * (HD + 1):(t + 1) * (HD + 1)], EW[:, h % 2, d, s, t * P:(t + 1) * P],
                                           BV[:, s, h, :], start=(s == keys[0]), stop=(s == keys[-1]))
                    mm.then_inc(ml_out, 1)
            pe.wait_ge(conv_out, 8)
            pe.wait_ge(ml_cols, 1)
            for h in range(NH):
                r = slice(HD * (h % 2), HD * (h % 2) + HD)
                if h >= 1:
                    pe.wait_ge(ml_exps, 2 * h)
                for d in range(2):
                    pe.matmul(PS[2 + d][:, :], ident[0:NH, h:h + 1].to_broadcast([NH, P]), ML[0:NH, d, 2, :],
                              start=True, stop=True).then_inc(ml_bc, 1)
                for s in range(NT):
                    if 4 * h + s >= 2:
                        pe.wait_ge(ml_prod, 4 * h + s - 1)
                    pe.matmul(PS[s % 2][:, :], BQK[r, 4 + h // 2, s * P:(s + 1) * P], BQK[r, h // 2, :],
                              start=True, stop=True).then_inc(ml_st, 1)
                    if s == 1 and h >= 1:
                        weigh(h - 1)
            weigh(NH - 1)

        def ml_act(act):
            for h in range(NH):
                if h >= 2:
                    act.wait_ge(ml_out, 2 * (h - 2) + 2)
                for d in range(2):
                    act.wait_ge(ml_masked, 2 * h + d + 1)
                    for s in range(NT):
                        o = slice((s + 1) * P, S) if d == 0 else slice(0, s * P)
                        if o.stop > o.start:
                            act.activation(EW[:, h % 2, d, s, o], PS[2 + d][:, o], ACT.Exp, bias=MLC[:, d, 0, s, h:h + 1])
                    for s in range(NT):
                        o = slice(s * P, (s + 1) * P)
                        ins = act.activation(EW[:, h % 2, d, s, o], MD[:, d, o], ACT.Exp, bias=MLC[:, d, 0, s, h:h + 1])
                    ins.then_inc(ml_exps, 1)

        def ml_dve(dve, own):
            hv = HACC.rearrange("p t (h c) -> p t h c", c=HD)

            def evac(h):
                for d in range(2):
                    dve.wait_ge(ml_out, 2 * h + d + 1)
                    o = PS[4 + 2 * (h % 2) + d][:, 0:NT * (HD + 1)].rearrange("p (t c) -> p t c", c=HD + 1)
                    den = DEN[:, 4 * d:4 * d + 4]
                    own(dve.scalar_tensor_tensor(den, o[:, :, HD], -1.0, MLC[:, d, 1, :, h], ALU.mult, ALU.max))
                    own(dve.tensor_tensor(den, o[:, :, HD], den, ALU.max))
                    own(dve.reciprocal(den, den))
                    dst = hv[:, :, h, :] if d == 0 else TMP[:, 0, 0:NT * HD].rearrange("p (t c) -> p t c", c=HD)
                    dve.tensor_tensor(dst, o[:, :, 0:HD], den.unsqueeze(2).to_broadcast([P, NT, HD]), ALU.mult
                                      ).then_inc(ml_evac, 1)
                    dve.wait_ge(ml_evac, 2 * h + d + 1)
                own(dve.tensor_tensor(hv[:, :, h, :], hv[:, :, h, :], dst, ALU.add))

            dve.wait_ge(ml_cols, 1)
            for h in range(NH):
                for d in range(2):
                    dve.wait_ge(ml_bc, 2 * h + d + 1)
                    if h >= 1:
                        dve.wait_ge(ml_exps, 2 * (h - 1) + d + 1)
                    dve.tensor_tensor(MD[:, d, :].rearrange("p (t c) -> p t c", c=P),
                                      PS[2 + d][:, :].rearrange("p (t c) -> p t c", c=P),
                                      mask[f"nml{d}"].unsqueeze(1).to_broadcast([P, NT, P]), ALU.add).then_inc(ml_masked, 1)
                dve.wait_ge(ml_exps, 2 * h + 2)
                for s in range(NT):
                    dve.wait_ge(ml_st, 4 * h + s + 1)
                    for d in range(2):
                        o = span(d, s)
                        e = EW[:, h % 2, d, s, o]
                        ins = dve.scalar_tensor_tensor(e, PS[s % 2][:, o], HD ** -0.5, e, ALU.mult, ALU.mult)
                    ins.then_inc(ml_prod, 1)
                if h >= 1:
                    evac(h - 1)
            evac(NH - 1)
            h32 = HACC.rearrange("p t (h c) -> p (t h) c", c=HD)
            q32 = HSQ.rearrange("p t (h c) -> p (t h) c", c=HD)
            mu, var = LNS[:, 0:32], LNS[:, 32:64]
            wide = lambda v: v.unsqueeze(2).to_broadcast([P, 32, HD])
            own(dve.tensor_reduce(mu, h32, AX_X, ALU.add))
            own(dve.tensor_scalar(mu, mu, -1.0 / HD, None, ALU.mult))
            own(dve.tensor_tensor(h32, h32, wide(mu), ALU.add))
            own(dve.tensor_tensor(HSQ[:, :, :], HACC[:, :, :], HACC[:, :, :], ALU.mult))
            dve.tensor_reduce(var, q32, AX_X, ALU.add).then_inc(ml_var, 1)
            dve.wait_ge(ml_rstd, 1)
            own(dve.tensor_tensor(h32, h32, wide(var), ALU.mult))
            own(dve.tensor_tensor(HACC[:, :, :], HACC[:, :, :],
                                  BC[:, 32 + HD:32 + HD + WA].unsqueeze(1).to_broadcast([P, NT, WA]), ALU.mult))
            dve.wait_ge(proj_taken, 20)
            dve.tensor_tensor(HACC[:, :, :], HACC[:, :, :], BO[:, :, :], ALU.mult).then_inc(ml_h, 1)

        def ml_post_act(act, own):
            act.wait_ge(ml_var, 1)
            var = LNS[:, 32:64]
            own(act.activation(var, var, ACT.Ln, scale=1.0 / HD, bias=EPSC[:, 0:1]))
            act.activation(var, var, ACT.Exp, scale=-0.5).then_inc(ml_rstd, 1)

        def to_channels_pe(pe, src, banks, done):
            for c in range(4):
                for t in range(NT):
                    mm = pe.transpose(banks[c][:, t * P:(t + 1) * P], src[:, t, c * P:(c + 1) * P], ident)
                mm.then_inc(done, 1)

        def to_channels_act(act, dst, banks, done, copied):
            for c in range(4):
                act.wait_ge(done, c + 1)
                act.activation(dst[:, c, :], banks[c][:, :], ACT.Copy).then_inc(copied, 1)

        def bv_act(act):
            for t in range(NT):
                act.activation(BV[:, t, :, 0:HD], take(act, 12 + t, None)[:, :].rearrange("p (h c) -> p h c", c=HD),
                               ACT.Copy).then_inc(proj_taken, 1)

        QKV = ar(0, 12, S)
        KD = ar(4096, 2, WA)
        U = ar(5120, 2, WA)
        KTOK = ar(6144, NT, WA)
        VTOK = ar(8192, NT, WA)
        O = ar(10240, NT, WA)
        WT = ar(12288, 2, 4, P)
        AT = ar(13312, 2, NH, P)
        ST = ar(15360, 2, 4, P)
        WTOK = ar(16384, WA)
        LT = ar(16896, 4, P)
        PA, PAT, PB, PBT = (ar(17408 + 512 * j, 4, P) for j in range(4))
        XR = ar(19456, 4, 2 * P)
        RT = ar(20480, 2, WA)
        Z = ar(6144, NT, WA)
        OSQ = ar(0, NT, WA)
        SPG = SQ[:, 0, 0:128]
        ABG = SQ[:, 0, 128:256]
        NEA = SQ[:, 0, 256:272]
        SUMS = [CPAD[:, 64 * j:64 * j + 64].rearrange("p (t d h) -> p t d h", t=NT, d=2) for j in range(8)]
        GG, LNB, GC, GCB, NGC, EGC, BEG, BETA = SUMS
        KE = CPAD[:, 512:576].rearrange("p (t d h) -> p t d h", t=NT, d=2)
        CD = CPAD[:, 576:640].rearrange("p (c d h) -> p c d h", c=8, d=2)
        ROUNDS = NT
        OTV = ar(8192, NT, S)

        def l2_act(act, own):
            def rstd(m):
                act.wait_ge(l2_ss, m + 1)
                r = TMP[:, m % 2, :]
                if m >= 2:
                    act.wait_ge(l2_done, m - 1)
                own(act.activation(r, PS[4 + m % 2][:, :], ACT.Ln, bias=EPSC[:, 0:1]))
                bias = EPSC[:, 2:3] if m < 4 else EPSC[:, 3:4]
                act.activation(r, r, ACT.Exp, scale=-0.5, bias=bias).then_inc(l2_r, 1)
            for m in range(8):
                if m >= 2:
                    act.wait_ge(l2_ss, m - 1)
                if m == 0:
                    act.wait_ge(conv_out, 20)
                act.activation(SQ[:, m % 2, :], QKV[:, m, :], ACT.Square).then_inc(l2_sq, 1)
                if m >= 1:
                    rstd(m - 1)
            rstd(7)

        def l2_pe(pe):
            for m in range(8):
                pe.wait_ge(l2_sq, m + 1)
                if m >= 2:
                    pe.wait_ge(l2_r, m - 1)
                pe.matmul(PS[4 + m % 2][:, :], mask["blk64"], SQ[:, m % 2, :], start=True, stop=True).then_inc(l2_ss, 1)
            for j, m in enumerate((8, 9, 10, 11, 4, 5, 6, 7)):
                if m < 8:
                    pe.wait_ge(l2_done, m + 1)
                if j >= 4:
                    pe.wait_ge(tok_copied, j - 3)
                for t in range(NT):
                    mm = pe.transpose(PS[j % 4][:, t * P:(t + 1) * P], QKV[:, m, t * P:(t + 1) * P], ident)
                mm.then_inc(tok_done, 1)

        def l2_dve(dve):
            for m in range(8):
                dve.wait_ge(l2_r, m + 1)
                dve.tensor_tensor(QKV[:, m, :], QKV[:, m, :], TMP[:, m % 2, :], ALU.mult).then_inc(l2_done, 1)

        def tok_act(act):
            for j, m in enumerate((8, 9, 10, 11, 4, 5, 6, 7)):
                act.wait_ge(tok_done, j + 1)
                dst = VTOK if m >= 8 else KTOK
                act.activation(dst[:, :, (m % 4) * P:(m % 4 + 1) * P], PS[j % 4][:, :].rearrange("p (t c) -> p t c", c=P),
                               ACT.Copy).then_inc(tok_copied, 1)

        def gdn_gates_dve(dve, own):
            v5 = lambda x: x.rearrange("p (t d k h) -> p t d k h", t=NT, d=2, k=2)
            gt = GT[:, :, 0:32].rearrange("p t (d k h) -> p t d k h", d=2, k=2)
            sp, ab = v5(SPG), v5(ABG)
            dt_bias = BC[:, 16:32].rearrange("p (d h) -> p d h", d=2).unsqueeze(1).to_broadcast([P, NT, 2, NH])
            dve.wait_ge(l2_ss, 8)
            own(dve.tensor_tensor(sp[:, :, :, 0, :], gt[:, :, :, 0, :], dt_bias, ALU.add))
            own(dve.tensor_scalar(sp[:, :, :, 1, :], gt[:, :, :, 1, :], -1.0, None, ALU.mult))
            dve.scalar_tensor_tensor(ABG, SPG, -1.0, SPG, ALU.mult, ALU.max).then_inc(gg_abs, 1)
            dve.wait_ge(gg_ln, 1)
            own(dve.scalar_tensor_tensor(SPG, SPG, 0.0, ABG, ALU.max, ALU.add))
            own(dve.tensor_scalar(NEA, NEA, -1.0, None, ALU.mult))
            own(dve.tensor_scalar(LNB, sp[:, :, :, 1, :], -1.0, None, ALU.mult))
            nea = NEA.rearrange("p (d h) -> p d h", d=2).unsqueeze(1).to_broadcast([P, NT, 2, NH])
            dve.tensor_tensor(GG, sp[:, :, :, 0, :], nea, ALU.mult).then_inc(gg_ready, 1)
            dve.wait_ge(gg_sum, 1)
            ps = lambda k: PS[4 + k][:, 0:64].rearrange("p (t d h) -> p t d h", t=NT, d=2)
            own(dve.tensor_copy(GC, ps(0)))
            own(dve.tensor_tensor(GCB, GC, LNB, ALU.add))
            own(dve.tensor_scalar(NGC, GC, -1.0, None, ALU.mult))
            dve.tensor_tensor(KE, ps(1), NGC, ALU.add).then_inc(gg_cum, 1)
            dve.wait_ge(gg_exp, 1)

        def gdn_gates_act(act, own):
            act.wait_ge(gg_abs, 1)
            own(act.activation(ABG, ABG, ACT.Exp, scale=-1.0))
            own(act.activation(NEA, BC[:, 0:16], ACT.Exp))
            act.activation(ABG, ABG, ACT.Ln, bias=EPSC[:, 1:2]).then_inc(gg_ln, 1)
            act.wait_ge(gg_cum, 1)
            act.activation(EGC, GC, ACT.Exp)
            act.activation(BEG, GCB, ACT.Exp)
            act.activation(BETA, LNB, ACT.Exp)
            act.activation(KE, KE, ACT.Exp)
            for par in range(2):
                r = slice(64 * par, 64 * par + 64)
                ends = PS[6][r, 0:P].rearrange("p (c d j q) -> p c d j q", c=8, d=2, q=2)
                ins = act.activation(CD[r, :, :, 0:4], ends[:, :, :, :, par], ACT.Exp)
            ins.then_inc(gg_exp, 1)

        def gdn_gates_pe(pe):
            pe.wait_ge(gg_ready, 1)
            for t in range(NT):
                for d in range(2):
                    c = (t * 2 + d) * NH
                    pe.matmul(PS[4][:, c:c + NH], mask[f"cum{d}"], GG[:, t, d, :], start=True, stop=True)
                g2 = GG[:, t, :, :].rearrange("p d h -> p (d h)")
                pe.matmul(PS[5][:, 16 * t:16 * t + 16], mask["blk64"], g2, start=True, stop=True)
                for hf in range(2):
                    c = 16 * (2 * t + hf)
                    mm = pe.matmul(PS[6][:, c:c + 16], mask["blk64"][:, 64 * hf:64 * hf + 1].to_broadcast([P, P]), g2,
                                   start=True, stop=True)
            mm.then_inc(gg_sum, 1)

        PE_STEPS = ["spread", "raw", "lower", "fold0", "fold1", "fold2", "fold3", "zt", "zy", "zzy", "zy1"]
        ACT_STEPS = ["decay_l", "decay_a", "square0", "square1", "square2", "zt", "zy"]
        DVE_STEPS = ["mask_l", "mask_a", "lower", "scores", "split", "add0", "add1", "add2", "add3", "y1", "y2"]

        def units():
            for r in range(ROUNDS):
                for d in range(2):
                    for par in range(2):
                        yield r, d, (r if d == 0 else NT - 1 - r), par

        def after(steps, name, u):
            return u * len(steps) + steps.index(name) + 1

        def by_parity(x, par):
            return x.rearrange("p (j q) c -> p j q c", q=2)[:, :, par, :]

        def unit_pe(pe, u, r, d, t, par):
            rows_, cols = slice(64 * par, 64 * par + 64), slice(t * P, (t + 1) * P)
            step = lambda ins: ins.then_inc(unit_pe_done, 1)
            dve_at = lambda name: pe.wait_ge(unit_dve_done, after(DVE_STEPS, name, u))
            act_at = lambda name: pe.wait_ge(unit_act_done, after(ACT_STEPS, name, u))
            hs = [slice(j * P, (j + 1) * P) for j in range(4)]
            if u > 0:
                pe.wait_ge(unit_dve_done, after(DVE_STEPS, "y2", u - 1))
            for b, src in ((0, GCB), (1, GC)):
                for j in range(4):
                    h = 2 * j + par
                    mm = pe.matmul(PS[b][:, hs[j]], src[:, t, d, h:h + 1].to_broadcast([P, P]), ident, start=True, stop=True)
            step(mm)
            if u % 4 == 2:
                pe.wait_ge(wt_ready, u // 2)
            for b, m0 in ((2, 4), (3, 0)):
                for j in range(4):
                    mm = pe.matmul(PS[b][:, hs[j]], QKV[rows_, 4 + j, cols], QKV[rows_, m0 + j, cols], start=True, stop=True)
            step(mm)
            dve_at("lower")
            for j in range(4):
                mm = pe.transpose(PS[4][:, hs[j]], LT[:, j, :], ident)
            step(mm)

            def apply(banks, left):
                for j in range(4):
                    mm = pe.matmul(PS[banks[j // 2]][:, (j % 2) * 256:(j % 2) * 256 + 256], left[:, j, :], XR[:, j, :],
                                   start=True, stop=True)
                return mm

            def square(bank, left, right):
                for j in range(4):
                    mm = pe.matmul(PS[bank][:, hs[j]], left[:, j, :], right[:, j, :], start=True, stop=True)
                return mm

            dve_at("split")
            apply((0, 1), PAT)
            square(2, PAT, PA)
            step(square(3, PA, PAT))
            act_at("square0")
            dve_at("add0")
            apply((4, 5), PBT)
            square(6, PBT, PB)
            step(square(7, PB, PBT))
            act_at("square1")
            dve_at("add1")
            apply((0, 1), PAT)
            step(square(2, PA, PAT))
            act_at("square2")
            dve_at("add2")
            step(apply((4, 5), PBT))
            dve_at("add3")
            for j in range(4):
                mm = pe.transpose(PS[6][:, hs[j]], XR[:, j, 0:P], ident)
            step(mm)
            act_at("zt")
            for j in range(4):
                mm = pe.matmul(PS[7][:, hs[j]], LT[:, j, :], XR[:, j, P:2 * P], start=True, stop=True)
            step(mm)
            act_at("zy")
            step(square(0, LT, PA))
            dve_at("y1")
            step(square(1, LT, PAT))

        def unit_act(act, u, r, d, t, par):
            step = lambda ins: ins.then_inc(unit_act_done, 1)
            dve_at = lambda name: act.wait_ge(unit_dve_done, after(DVE_STEPS, name, u))
            pe_at = lambda name: act.wait_ge(unit_pe_done, after(PE_STEPS, name, u))
            flat = lambda x: x.rearrange("p a b -> p (a b)")
            at = by_parity(AT[:, d, :, :], par)
            dve_at("mask_l")
            step(act.activation(flat(LT), flat(LT), ACT.Exp))
            dve_at("mask_a")
            step(act.activation(at, at, ACT.Exp))
            for k, (l, lt, b) in enumerate(((PB, PBT, 2), (PA, PAT, 6))):
                pe_at(f"fold{k}")
                act.activation(flat(l), PS[b][:, :], ACT.Copy)
                step(act.activation(flat(lt), PS[b + 1][:, :], ACT.Copy))
            pe_at("fold2")
            step(act.activation(flat(PBT), PS[2][:, :], ACT.Copy))
            pe_at("zt")
            step(act.activation(flat(LT), PS[6][:, :], ACT.Copy))
            pe_at("zy")
            step(act.activation(flat(PA), PS[7][:, :], ACT.Copy))

        def unit_dve(dve, u, r, d, t, par):
            n = len(DVE_STEPS)
            count = [u * n]

            def step(ins):
                count[0] += 1
                ins.then_inc(unit_dve_done, 1)

            def done(name):
                dve.wait_ge(unit_dve_done, after(DVE_STEPS, name, u))
            pe_at = lambda name: dve.wait_ge(unit_pe_done, after(PE_STEPS, name, u))
            act_at = lambda name: dve.wait_ge(unit_act_done, after(ACT_STEPS, name, u))
            v4 = lambda b: PS[b][:, :].rearrange("p (j c) -> p j c", c=P)
            at = by_parity(AT[:, d, :, :], par)
            over = lambda m: m.unsqueeze(1).to_broadcast([P, 4, P])
            heads = lambda x, w: x[:, t, d, par::2].unsqueeze(2).to_broadcast([P, 4, w])
            pe_at("spread")
            for b, dst, m in ((0, LT, f"nstr{d}"), (1, at, f"ninc{d}")):
                for j in range(4):
                    h = 2 * j + par
                    ins = dve.scalar_tensor_tensor(dst[:, j, :], v4(b)[:, j, :], NGC[:, t, d, h:h + 1], mask[m], ALU.add, ALU.add)
                step(ins)
            pe_at("raw")
            act_at("decay_l")
            step(dve.tensor_tensor(LT, LT, v4(2), ALU.mult))
            act_at("decay_a")
            step(dve.tensor_tensor(at, at, v4(3), ALU.mult))
            by_head = lambda x: by_parity(x[:, t, :].rearrange("p (h c) -> p h c", c=HD), par)
            dve.tensor_tensor(XR[:, :, P:P + HD], by_head(VTOK), heads(BETA, HD), ALU.mult)
            dve.tensor_tensor(XR[:, :, P + HD:2 * P], by_head(KTOK), heads(BEG, HD), ALU.mult)
            done("lower")
            dve.tensor_tensor(PAT, LT, over(mask["b16n"]), ALU.mult)
            pe_at("lower")
            dve.tensor_tensor(PA, v4(4), over(mask["b16n"]), ALU.mult)
            step(dve.tensor_tensor(XR[:, :, 0:P], v4(4), over(mask["off16"]), ALU.mult))
            done("split")
            for k, b in enumerate((0, 4, 0, 4)):
                pe_at(f"fold{k}")
                for i in range(2):
                    x = XR[:, 2 * i:2 * i + 2, :]
                    ins = dve.tensor_tensor(x, x, PS[b + i][:, :].rearrange("p (j c) -> p j c", c=2 * P), ALU.add)
                step(ins)
                done(f"add{k}")
            pe_at("zzy")
            step(dve.tensor_tensor(PAT, XR[:, :, P:2 * P], v4(0), ALU.add))
            done("y1")
            pe_at("zy1")
            uv = by_parity(U[:, d, :].rearrange("p (h c) -> p h c", c=HD), par)
            wv = by_parity(WTOK.rearrange("p (h c) -> p h c", c=HD), par)
            dve.tensor_tensor(uv, PAT[:, :, 0:HD], v4(1)[:, :, 0:HD], ALU.subtract)
            step(dve.tensor_tensor(wv, PAT[:, :, HD:P], v4(1)[:, :, HD:P], ALU.subtract))

        def turn_w_pe(pe, r, d):
            pe.wait_ge(unit_dve_done, after(DVE_STEPS, "y2", 4 * r + 2 * d + 1))
            for j in range(4):
                mm = pe.transpose(PS[2][:, j * P:(j + 1) * P], WTOK[:, j * P:(j + 1) * P], ident)
            mm.then_inc(wt_done, 1)

        def turn_w_act(act, r, d):
            act.wait_ge(wt_done, 2 * r + d + 1)
            act.activation(WT[:, d, :, :].rearrange("p a b -> p (a b)"), PS[2][:, :], ACT.Copy).then_inc(wt_ready, 1)

        def steps_of(r):
            for s in range(2):
                for d in range(2):
                    yield 4 * r + 2 * s + d, s, d, (r if d == 0 else NT - 1 - r), (s if d == 0 else 1 - s)

        def recur_pe(pe, r):
            pe.wait_ge(wt_ready, 2 * r + 2)
            pe.wait_ge(kd_ready, 2 * r + 2)
            for pair in range(2):
                two = list(steps_of(r))[2 * pair:2 * pair + 2]
                for n, s, d, t, hf in two:
                    if n >= 2:
                        pe.wait_ge(gd_state, n - 1)
                    rw = slice(64 * hf, 64 * hf + 64)
                    for j in range(4):
                        pe.matmul(PS[d][rw, j * P:(j + 1) * P], WT[:, d, j, rw], ST[:, d, j, :], start=True, stop=True)
                    for j in range(4):
                        c0 = t * P + 64 * hf
                        mm = pe.matmul(PS[2 + d][rw, j * P:(j + 1) * P], QKV[:, j, c0:c0 + 64], ST[:, d, j, :],
                                       start=True, stop=True)
                    mm.then_inc(gd_read, 1)
                for n, s, d, t, hf in two:
                    pe.wait_ge(gd_vnew, n + 1)
                    rw = slice(64 * hf, 64 * hf + 64)
                    for j in range(4):
                        js = slice(j * P, (j + 1) * P)
                        mm = pe.matmul(PS[4 + d][:, js], KD[rw, d, js], U[rw, d, js], start=True, stop=True)
                    mm.then_inc(gd_kv, 1)
            for d in range(2):
                for h in range(NH):
                    hs = slice(h * HD, (h + 1) * HD)
                    mm = pe.matmul(PS[6 + d][:, hs], AT[:, d, h, :], U[:, d, hs], start=True, stop=True)
                mm.then_inc(gd_intra, 1)

        def recur_dve(dve, own, r):
            v8 = lambda x: x.rearrange("p (h c) -> p h c", c=HD)
            for pair in range(2):
                two = list(steps_of(r))[2 * pair:2 * pair + 2]
                for n, s, d, t, hf in two:
                    rw = slice(64 * hf, 64 * hf + 64)
                    dve.wait_ge(gd_read, n + 1)
                    dve.tensor_tensor(U[rw, d, :], U[rw, d, :], PS[d][rw, :], ALU.subtract).then_inc(gd_vnew, 1)
                for n, s, d, t, hf in two:
                    rw = slice(64 * hf, 64 * hf + 64)
                    own(dve.tensor_tensor(v8(RT[rw, d, :]), v8(PS[2 + d][rw, :]),
                                          EGC[rw, t, d, :].unsqueeze(2).to_broadcast([64, NH, HD]), ALU.mult))
                    own(dve.tensor_tensor(O[rw, t, :], O[rw, t, :], RT[rw, d, :], ALU.add))
                    dve.wait_ge(gd_kv, n + 1)
                    r4 = RT[:, d, :].rearrange("p (j c) -> p j c", c=P)
                    own(dve.tensor_tensor(r4, PS[4 + d][:, :].rearrange("p (j c) -> p j c", c=P),
                                          mask["blk64"].unsqueeze(1).to_broadcast([P, 4, P]), ALU.mult))
                    for j in range(4):
                        ins = dve.scalar_tensor_tensor(ST[:, d, j, :], ST[:, d, j, :], CD[:, 2 * t + hf, d, j:j + 1], r4[:, j, :],
                                                       ALU.mult, ALU.add)
                    ins.then_inc(gd_state, 1)
                    dve.wait_ge(gd_state, n + 1)
            for d in range(2):
                t = r if d == 0 else NT - 1 - r
                dve.wait_ge(gd_intra, 2 * r + d + 1)
                own(dve.tensor_tensor(O[:, t, :], O[:, t, :], PS[6 + d][:, :], ALU.add))

        def gdn_fill_pool(pool):
            pool.wait_ge(ml_h, 1)
            pool.wait_ge(hb_copied, 4)
            pool.memset(O[:, :, :], 0.0).then_inc(gd_zero, 1)
            pool.memset(ST[:, :, :, :], 0.0).then_inc(gd_zero, 1)

        def gdn_kd_pool(pool):
            pool.wait_ge(gg_exp, 1)
            pool.wait_ge(tok_copied, 8)
            for r in range(ROUNDS):
                for d in range(2):
                    t = r if d == 0 else NT - 1 - r
                    if r >= 1:
                        pool.wait_ge(gd_kv, 4 * (r - 1) + 2 + d + 1)
                    v8 = lambda x: x.rearrange("p (h c) -> p h c", c=HD)
                    pool.tensor_tensor(v8(KD[:, d, :]), v8(KTOK[:, t, :]),
                                       KE[:, t, d, :].unsqueeze(2).to_broadcast([P, NH, HD]), ALU.mult).then_inc(kd_ready, 1)

        def gdn_pe(pe):
            pe.wait_ge(gg_exp, 1)
            pe.wait_ge(tok_copied, 8)
            pe.wait_ge(gd_zero, 2)
            for u, (r, d, t, par) in enumerate(units()):
                if u % 4 == 0 and r >= 1:
                    pe.wait_ge(gd_out, r)
                unit_pe(pe, u, r, d, t, par)
                if par == 1:
                    turn_w_pe(pe, r, d)
                if u % 4 == 3:
                    recur_pe(pe, r)

        def gdn_act(act):
            for u, (r, d, t, par) in enumerate(units()):
                unit_act(act, u, r, d, t, par)
                if par == 1:
                    turn_w_act(act, r, d)

        def gdn_dve(dve, own):
            dve.wait_ge(gd_zero, 2)
            dve.wait_ge(tok_copied, 8)
            for u, (r, d, t, par) in enumerate(units()):
                if par == 0 and u >= 1:
                    dve.wait_ge(wt_done, u // 2)
                unit_dve(dve, u, r, d, t, par)
                if u % 4 == 3:
                    recur_dve(dve, own, r)
                    dve.sem_inc(gd_out, 1)
            o32 = O.rearrange("p t (h c) -> p (t h) c", c=HD)
            q32 = OSQ.rearrange("p t (h c) -> p (t h) c", c=HD)
            var = LNS[:, 0:32]
            own(dve.tensor_tensor(OSQ[:, :, :], O[:, :, :], O[:, :, :], ALU.mult))
            dve.tensor_reduce(var, q32, AX_X, ALU.add).then_inc(gd_var, 1)
            dve.wait_ge(gd_rstd, 1)
            own(dve.tensor_tensor(o32, o32, var.unsqueeze(2).to_broadcast([P, 32, HD]), ALU.mult))
            own(dve.tensor_tensor(o32, o32, BC[:, 32:32 + HD].unsqueeze(1).to_broadcast([P, 32, HD]), ALU.mult))
            dve.wait_ge(proj_taken, 36)
            dve.tensor_tensor(O[:, :, :], O[:, :, :], Z[:, :, :], ALU.mult).then_inc(gd_o, 1)

        def gdn_post_act(act, own):
            act.wait_ge(gd_var, 1)
            var = LNS[:, 0:32]
            own(act.activation(var, var, ACT.Ln, scale=1.0 / HD, bias=EPSC[:, 0:1]))
            act.activation(var, var, ACT.Exp, scale=-0.5).then_inc(gd_rstd, 1)

        def at_route(off, *shape):
            return ar(ROUTE + off, *shape)

        ROUTE = 16384
        RL = at_route(0, NT, NG + NE)
        EL, OH1, OH2, HOT, PICK, POS, BK = (at_route(144 + NT * NE * j, NT, NE) for j in range(7))
        GEX, HIDE, GPICK = (at_route(1040 + NT * NG * j, NT, NG) for j in range(3))
        GMAX, GPROB, GIDX, V1, V2_, IDX1, DENR, WT1, WT2, BK1, BK2, POS1, POS2, TOKID = (
            at_route(1088 + NT * j, NT) for j in range(14))
        BLK = at_route(1152, P)[0:NE, :]
        LE = at_route(1280, MOE_SLOTS)[0:NE, :]
        SEL = at_route(1344, 2 * NT, P)
        BSEL = at_route(2368, 2 * NT, MOE_SLOTS)
        IDXR = at_route(2688, P)[0:MOE_SLOTS, :].bitcast(U32)
        EXPT = at_route(2816, MOE_SLOTS)[0:1, :].bitcast(I32)
        SLU = at_route(2880, 2 * NT).bitcast(U32)
        IDXB = at_route(2896, 2).bitcast(U32)
        IOTA_TMP = at_route(2944, P)
        HNT = ar(12288, NT, D)
        ROUTE_G = 76
        ROUND = 12582912.0

        def router_pe(pe):
            pe.wait_ge(hn_ready, 2 * KC)
            for t in range(NT):
                group(pe, ROUTE_G + t, None, token_products(RW, t, HN))
            for t in range(NT):
                for hf in range(2):
                    if t == 2 and hf == 0:
                        pe.wait_ge(proj_taken, ROUTE_G + NT)
                    for j in range(4):
                        mm = pe.transpose(PS[(2 * t + hf + 4) % 8][:, j * P:(j + 1) * P], HN[:, 4 * hf + j, t * P:(t + 1) * P],
                                          ident)
                    mm.then_inc(hnt_done, 1)
            pe.wait_ge(hnt_copied, 2 * NT)
            pe.wait_ge(picked, 1)
            for t in range(NT):
                for s in range(t + 1):
                    mm = pe.matmul(PS[4][:, t * NE:(t + 1) * NE], mask["sbpast"] if s == t else ones, HOT[:, s, :],
                                   start=(s == 0), stop=(s == t))
            for t in range(NT):
                mm = pe.matmul(PS[5][0:NE, 0:P], HOT[:, t, :], ones, start=(t == 0), stop=(t == NT - 1))
            mm.then_inc(ranked, 1)
            pe.wait_ge(blk_ready, 1)
            pe.matmul(PS[6][:, 0:NE], BLK, mask["sbpast"][0:NE, 0:NE], start=True, stop=True)
            pe.matmul(PS[7][0:NE, 0:P], mask["cum0"][0:NE, 0:NE], BLK, start=True, stop=True).then_inc(ranked, 1)
            pe.wait_ge(sel_ready, 1)
            for j in range(2 * NT):
                mm = pe.matmul(PS[5][0:MOE_SLOTS, 0:P], BSEL[:, j, :], SEL[:, j, :], start=(j == 0), stop=(j == 2 * NT - 1))
            mm = pe.matmul(PS[3][0:1, 0:MOE_SLOTS], ones[0:NE, 0:1], LE, start=True, stop=True)
            mm.then_inc(ranked, 1)

        def router_act(act, own):
            for t in range(NT):
                b = take(act, ROUTE_G + t, None)
                act.activation(RL[:, t, :], b[:, 0:NG + NE], ACT.Copy).then_inc(proj_taken, 1)
            act.wait_ge(route_arg, 1)
            act.activation(GEX, GEX, ACT.Exp).then_inc(route_exp, 1)
            for t in range(NT):
                for hf in range(2):
                    act.wait_ge(hnt_done, 2 * t + hf + 1)
                    act.activation(HNT[:, t, hf * 512:(hf + 1) * 512], PS[(2 * t + hf + 4) % 8][:, :], ACT.Copy).then_inc(hnt_copied, 1)
            act.wait_ge(route_arg, 2)
            act.activation(DENR, DENR, ACT.Exp).then_inc(route_exp, 1)

        def router_dve(dve, own):
            iota = mask["iota"]
            bc = lambda v, n: v.unsqueeze(2).to_broadcast([P, NT, n])
            counts = lambda n: iota[:, 0:n].unsqueeze(1).to_broadcast([P, NT, n])

            def first(hot, pick, low, n):
                own(dve.scalar_tensor_tensor(pick, hot, -100.0, counts(n), ALU.mult, ALU.add))
                own(dve.tensor_reduce(low, pick, AX_X, ALU.min))
                own(dve.tensor_tensor(hot, pick, bc(low, n), ALU.is_equal))

            own(dve.tensor_tensor(IOTA_TMP, ident, iota, ALU.mult))
            own(dve.tensor_reduce(TOKID[:, 0:1], IOTA_TMP, AX_X, ALU.add))
            for t in range(1, NT):
                dve.tensor_scalar(TOKID[:, t:t + 1], TOKID[:, 0:1], float(t * P), None, ALU.add)
            dve.wait_ge(proj_taken, ROUTE_G + NT)
            gl, el = RL[:, :, 0:NG], RL[:, :, NG:NG + NE]
            own(dve.tensor_reduce(GMAX, gl, AX_X, ALU.max))
            dve.tensor_tensor(GEX, gl, bc(GMAX, NG), ALU.subtract).then_inc(route_arg, 1)
            own(dve.tensor_tensor(HIDE, gl, bc(GMAX, NG), ALU.is_equal))
            first(HIDE, GPICK, GIDX, NG)
            own(dve.tensor_scalar(HIDE, HIDE, -NEG, NEG, ALU.mult, ALU.add))
            e4 = lambda v: v.rearrange("p t (g e) -> p t g e", g=NG)
            own(dve.tensor_tensor(e4(EL), e4(el), HIDE.unsqueeze(3).to_broadcast([P, NT, NG, NE // NG]), ALU.add))
            for v, hot in ((V1, OH1), (V2_, OH2)):
                own(dve.tensor_reduce(v, EL, AX_X, ALU.max))
                own(dve.tensor_tensor(hot, EL, bc(v, NE), ALU.is_equal))
                first(hot, PICK, IDX1, NE)
                if hot is OH1:
                    own(dve.scalar_tensor_tensor(EL, OH1, 3.0 * NEG, EL, ALU.mult, ALU.add))
            dve.tensor_tensor(HOT, OH1, OH2, ALU.add).then_inc(picked, 1)
            dve.tensor_tensor(DENR, V2_, V1, ALU.subtract).then_inc(route_arg, 1)
            dve.wait_ge(ranked, 1)
            own(dve.tensor_scalar(BLK, PS[5][0:NE, 0:P], 1.0 / P, 127.0 / 256.0, ALU.mult, ALU.add))
            own(dve.tensor_scalar(BLK, BLK, ROUND, None, ALU.add))
            dve.tensor_scalar(BLK, BLK, -ROUND, None, ALU.add).then_inc(blk_ready, 1)
            rank = PS[4][:, 0:NT * NE].rearrange("p (t e) -> p t e", t=NT)
            own(dve.tensor_scalar(BK, rank, 1.0 / P, -127.0 / 256.0, ALU.mult, ALU.add))
            own(dve.tensor_scalar(BK, BK, ROUND, None, ALU.add))
            own(dve.tensor_scalar(BK, BK, -ROUND, None, ALU.add))
            own(dve.scalar_tensor_tensor(POS, BK, -float(P), rank, ALU.mult, ALU.add))
            dve.wait_ge(ranked, 2)
            own(dve.tensor_tensor(BK, BK, PS[6][:, 0:NE].unsqueeze(1).to_broadcast([P, NT, NE]), ALU.add))
            dve.tensor_tensor(LE, PS[7][0:NE, 0:MOE_SLOTS], iota[0:NE, 0:MOE_SLOTS], ALU.is_le)
            for hot, bk, pos in ((OH1, BK1, POS1), (OH2, BK2, POS2)):
                own(dve.tensor_tensor(PICK, hot, BK, ALU.mult))
                own(dve.tensor_reduce(bk, PICK, AX_X, ALU.add))
                own(dve.tensor_tensor(PICK, hot, POS, ALU.mult))
                own(dve.tensor_reduce(pos, PICK, AX_X, ALU.add))
            for k, (bk, pos) in enumerate(((BK1, POS1), (BK2, POS2))):
                for t in range(NT):
                    dve.tensor_scalar(SEL[:, NT * k + t, :], iota, pos[:, t:t + 1], None, ALU.is_equal)
                    ins = dve.tensor_scalar(BSEL[:, NT * k + t, :], iota[:, 0:MOE_SLOTS], bk[:, t:t + 1], TOKID[:, t:t + 1],
                                            ALU.is_equal, ALU.mult)
                own(dve.scalar_tensor_tensor(SLU[:, NT * k:NT * k + NT], bk, float(P), pos, ALU.mult, ALU.add))
            dve.sem_inc(sel_ready, 1)
            dve.wait_ge(route_exp, 2)
            own(dve.tensor_reduce(GPROB, GEX, AX_X, ALU.add))
            own(dve.tensor_scalar(WT1, DENR, 1.0, None, ALU.add))
            own(dve.tensor_tensor(WT1, WT1, GPROB, ALU.mult))
            own(dve.reciprocal(WT1, WT1))
            own(dve.tensor_tensor(WT2, WT1, DENR, ALU.mult))
            dve.wait_ge(ranked, 3)
            own(dve.tensor_copy(IDXR, PS[5][0:MOE_SLOTS, 0:P]))
            dve.tensor_scalar(EXPT, PS[3][0:1, 0:MOE_SLOTS], float(NE - 1), None, ALU.min).then_inc(table_ready, 1)

        XG = ar(0, 2, D)
        XT = ar(2048, 2, KC, P)
        SG = ar(4096, 2, 2 * P)
        ACTT = ar(4608, 2, 2, P)
        YB = ar(5120, 2, D)
        YG = ar(8192, NT, 2, D)
        XT_CREDIT, ACT_CREDIT, DOWN_CREDIT, YB_CREDIT, Y_CREDIT = 2, 2, 4, 4, 16

        def expert_slots(j):
            up = W[(MOE_AT + j) % RING]
            down = W[(MOE_AT + 2) % RING][:, 2048 * j:2048 * j + 2048].rearrange("p (k n) -> p k n", k=2)
            return [up[:, 2048 * x:2048 * x + 2048].rearrange("p (k n) -> p k n", k=KC) for x in range(2)], down

        def expert_parts(experts, j):
            rows_of = lambda name, e: a[name][0, bass.ds(e, 1)].rearrange("o (k p) n -> p (o k) n", p=P)
            if j < 2:
                dst, _ = expert_slots(j)
                return [(dst[x], rows_of(name, experts[j])) for x, name in ((0, "w_gate"), (1, "w_up"))]
            return [(expert_slots(x)[1], rows_of("w_down", experts[x])) for x in range(2)]

        def experts_of(sp, first_block):
            return [sp.value_load(EXPT[0:1, bass.ds(first_block + x, 1)], min_val=0, max_val=NE - 1) for x in range(2)]

        def moe_pool(pool):
            pool.wait_ge(hnt_copied, 2 * NT)
            pool.dma_start(hn_rows.rearrange("(t p) d -> p t d", p=P), HNT[:, :, :]).then_inc(hn_out, 16)
            pool.wait_ge(table_ready, 1)
            pool.dma_start(idx_rows, IDXR).then_inc(hn_out, 16)
            pool.wait_ge(hn_out, 32)
            with pool.Fori(0, MOE_TRIPS) as i:
                for j in range(2):
                    pool.wait_ge(moe_xt, i * 2 + (j - 1 + XT_CREDIT))
                    pool.dma_start(IDXB[:, j:j + 1], idx_rows[bass.ds(i * 2 + j, 1), :].rearrange("o p -> p o")
                                   ).then_inc(idx_loaded[j], 16)
                    pool.wait_ge(idx_loaded[j], i * 16 + 16)
                    pool.sem_inc(gather_go, 1)
                    pool.indirect_dma_start(XG[:, j, :], None, hn_rows, bass.IndirectOffsetOnAxis(IDXB[:, j:j + 1], 0)
                                            ).then_inc(gathered[j], 16)
            for j in range(2):
                pool.wait_ge(y_written[j], MOE_TRIPS * 16 + Y_CREDIT)
            for t in range(NT):
                for k in range(2):
                    c = NT * k + t
                    pool.indirect_dma_start(YG[:, t, k, :], None, y_rows, bass.IndirectOffsetOnAxis(SLU[:, c:c + 1], 0)
                                            ).then_inc(y_gathered[t], 16)

        def moe_pe(pe):
            pe.sem_inc(moe_xt, XT_CREDIT)
            pe.sem_inc(moe_down, DOWN_CREDIT)
            pe.wait_ge(table_ready, 1)
            with pe.Fori(0, MOE_TRIPS) as i:
                for j in range(2):
                    pe.wait_ge(gathered[j], i * 16 + 16)
                    for c in range(KC):
                        mm = pe.transpose(PS[2 * j + c // 4][:, (c % 4) * P:(c % 4 + 1) * P], XG[:, j, c * P:(c + 1) * P], ident)
                    mm.then_inc(moe_xt, 1)
                for j in range(2):
                    arrived(pe, MOE_AT + j, (i, MOE_BLOCKS))
                    pe.wait_ge(moe_xc, i * 4 + (2 * j + 2))
                    pe.wait_ge(moe_yb, i * 4 + YB_CREDIT)
                    ups, _ = expert_slots(j)
                    for x, bank in ((0, 4 + j), (1, 2 * j)):
                        for f in range(2):
                            fs = slice(f * P, (f + 1) * P)
                            for k in range(KC):
                                mm = pe.matmul(PS[bank][:, fs], ups[x][:, k, fs], XT[:, j, k, :], start=(k == 0), stop=(k == KC - 1))
                        mm.then_inc(moe_up, 1)
                arrived(pe, MOE_AT + 2, (i, MOE_BLOCKS))
                for j in range(2):
                    _, down = expert_slots(j)
                    pe.wait_ge(moe_act, i * 2 + (j + 1 + ACT_CREDIT))
                    for hf in range(2):
                        for f in range(2):
                            mm = pe.matmul(PS[6 - 2 * j + hf][:, :], ACTT[:, j, f, :], down[:, f, hf * 512:(hf + 1) * 512],
                                           start=(f == 0), stop=(f == 1))
                        mm.then_inc(moe_down, 1)
            pe.wait_ge(moe_yb, MOE_SLOTS * 2 + YB_CREDIT)
            for t in range(NT):
                pe.wait_ge(moe_sum, t + 1)
                for c in range(KC):
                    mm = pe.transpose(PS[c][:, t * P:(t + 1) * P], YG[:, t, 0, c * P:(c + 1) * P], ident)
                    if t == NT - 1:
                        mm.then_inc(moe_back, 1)

        def moe_act_(act):
            act.sem_inc(moe_yb, YB_CREDIT)
            for j in range(2):
                act.sem_inc(y_written[j], Y_CREDIT)
            with act.Fori(0, MOE_TRIPS) as i:
                for j in range(2):
                    act.wait_ge(moe_up, i * 4 + (2 * j + 1))
                    act.wait_ge(moe_act, i * 2 + (j - 1 + ACT_CREDIT))
                    act.activation(SG[:, j, :], PS[4 + j][:, 0:2 * P], ACT.Silu).then_inc(moe_sg, 1)
                for j in range(2):
                    act.wait_ge(y_written[j], i * 16 + 16)
                    for hf in range(2):
                        act.wait_ge(moe_down, i * 4 + (2 * j + hf + 1 + DOWN_CREDIT))
                        act.activation(YB[:, j, hf * 512:(hf + 1) * 512], PS[6 - 2 * j + hf][:, :], ACT.Copy).then_inc(moe_yb, 1)

        def moe_dve(dve):
            dve.sem_inc(moe_act, ACT_CREDIT)
            with dve.Fori(0, MOE_TRIPS) as i:
                for j in range(2):
                    dve.wait_ge(moe_xt, i * 2 + (j + 1 + XT_CREDIT))
                    for hf in range(2):
                        dve.tensor_copy(XT[:, j, 4 * hf:4 * hf + 4, :], PS[2 * j + hf][:, :].rearrange("p (k n) -> p k n", n=P)
                                        ).then_inc(moe_xc, 1)
                for j in range(2):
                    dve.wait_ge(moe_up, i * 4 + (2 * j + 2))
                    dve.wait_ge(moe_sg, i * 2 + (j + 1))
                    dve.wait_ge(moe_down, i * 4 + (2 * j - 2 + DOWN_CREDIT))
                    dve.tensor_tensor(ACTT[:, j, :, :].rearrange("p f n -> p (f n)"), PS[2 * j][:, 0:2 * P], SG[:, j, :],
                                      ALU.mult).then_inc(moe_act, 1)

        def moe_sum_dve(dve, own):
            for t in range(NT):
                dve.wait_ge(y_gathered[t], 32)
                own(dve.tensor_scalar(YG[:, t, 0, :], YG[:, t, 0, :], WT1[:, t:t + 1], None, ALU.mult))
                dve.scalar_tensor_tensor(YG[:, t, 0, :], YG[:, t, 1, :], WT2[:, t:t + 1], YG[:, t, 0, :], ALU.mult, ALU.add
                                         ).then_inc(moe_sum, 1)
            for c in range(KC):
                dve.wait_ge(moe_back, c + 1)
                dve.scalar_tensor_tensor(H[:, c, :], PS[c][:, :], MOD[:, 5 * KC + c:5 * KC + c + 1], H[:, c, :],
                                         ALU.mult, ALU.add).then_inc(moe_add, 1)

        def final_norm_dve(dve):
            dve.wait_ge(rstd_ready, 3)
            for c in range(KC):
                dve.scalar_tensor_tensor(H[:, c, :], H[:, c, :], VEC[:, 0, V_GFIN + c:V_GFIN + c + 1], RSTD[:, :],
                                         ALU.mult, ALU.mult).then_inc(hn_ready, 1)

        def rope_tables_pool(pool):
            pool.wait_ge(merged, KC)
            pool.wait_ge(proj_done, 68)
            pool.dma_start(COS.bitcast(I32), a["positions_2"].to_broadcast([ROPE, S])).then_inc(pos_in, 16)

        def rope_tables_dve(dve, own):
            dve.wait_ge(pos_in, 16)
            dve.wait_ge(consts_in, N_CONST)
            ang, k, r = (TMP[0:ROPE, 0, :], TMP[0:ROPE, 1, :], SQ[0:ROPE, 0, :])
            dve.wait_ge(res_added, KC)
            own(dve.tensor_copy(ang, COS.bitcast(I32)))
            own(dve.tensor_scalar(ang, ang, FREQ[:, 0:1], None, ALU.mult))
            for j, (dst, quarter) in enumerate(((SIN, 0.0), (COS, 0.25))):
                own(dve.tensor_scalar(k, ang, 1.0 / PI2, quarter, ALU.mult, ALU.add))
                own(dve.tensor_scalar(k, k, 12582912.0, None, ALU.add))
                own(dve.tensor_scalar(k, k, -12582912.0, None, ALU.add))
                own(dve.scalar_tensor_tensor(dst, k, -6.28125, ang, ALU.mult, ALU.add))
                own(dve.scalar_tensor_tensor(dst, k, -0.0019350051879882812, dst, ALU.mult, ALU.add))
                own(dve.scalar_tensor_tensor(dst, k, -3.019916050561733e-07, dst, ALU.mult, ALU.add))
                own(dve.tensor_scalar(dst, dst, quarter * PI2, None, ALU.add))
                own(dve.tensor_scalar(dst, dst, 3.1415925, -3.1415925, ALU.min, ALU.max))
            dve.sem_inc(rope_arg, 1)

        def rope_tables_act(act):
            act.wait_ge(rope_arg, 1)
            act.activation(SIN, SIN, ACT.Sin)
            act.activation(COS, COS, ACT.Sin).then_inc(rope_ready, 1)

        QLAT, KVLAT, KROPE = ar(18432, 2, S), ar(19456, S), ar(19968, S)[0:ROPE, :]
        SMB = SM[:, 200:204]
        QSB, KSB, VSB = ar(12288, MH, S), ar(14336, MH, S), ar(16384, NT, WA)
        SPB, ABSZ, ATT = ar(0, NT, S), ar(2048, NT, S), ar(4096, NT, S)
        YM, YS = ar(8192, MH, S), ar(10240, MH, S)
        QN, QR, KN, KR = ar(0, MH, S), ar(2048, MH, S)[0:ROPE], ar(4096, MH, S), ar(6144, MH, S)[0:ROPE]
        VM, PT, PX = ar(12288, NT, WA), ar(14336, NT, S), ar(16384, 2, S)
        RTM = ar(17408, S)[0:ROPE, :]
        NMX, PSUM_ = SM[:, 0:16], SM[:, 16:32]
        FF, FP, FA = ar(0, FT, S), ar(11264, 4, S + 2), ar(13320, 4, S)
        V2 = {"b_ada": 0, "g_norm1": 48, "g_norm2": 56, "g_q_lat": 64, "g_kv_lat": 66, "c": 67, "b_lat": 75, "b_rope": 78,
              "b_qsb": 79, "b_ksb": 83, "b_gate": 87, "gq": 103, "gq_rope": 104, "gk": 105, "gk_rope": 106}
        LB = L_AT
        LG = B1_GROUPS
        GL = {"lat": 0, "qsb": 4, "ksb": 8, "vsb": 12, "qn": 16, "qr": 20, "kn": 24, "vm": 28, "merge": 32, "out": 64,
              "up": 72, "down": 116}
        vec = lambda name, i=0: VEC[:, 0, V2[name] + i:V2[name] + i + 1]
        conv_col = lambda k, m: VEC[:, 1 + k // 2, 44 * (k % 2) + m:44 * (k % 2) + m + 1]
        conv_bias = lambda m: VEC[:, 2, 44 + m:44 + m + 1]
        lay = lambda L, w: w[bass.ds(L, 1)]

        def layer_pack_pool(pool, L):
            pool.wait_ge(hn_ready, 3 * KC)
            pool.wait_ge(res_added, L * 16 + 8)
            def vrows(name, r0, c0, n):
                src = lay(L, a[name + "_2"])[:, c0:c0 + n * P].rearrange("o (r c) -> (o r) c", c=P)
                pool.dma_start(PACK[r0:r0 + n, 0, :], src).then_inc(pack_in, 16)
            def half(name, r0, c0):
                pool.dma_start(PACK[r0:r0 + 1, 0, 0:ROPE], lay(L, a[name + "_2"])[:, c0:c0 + ROPE]).then_inc(pack_in, 16)
            vrows("b_ada", V2["b_ada"], 0, 48)
            vrows("g_norm1", V2["g_norm1"], 0, 8)
            vrows("g_norm2", V2["g_norm2"], 0, 8)
            vrows("g_q_lat", V2["g_q_lat"], 0, 2)
            vrows("g_kv_lat", V2["g_kv_lat"], 0, 1)
            pool.dma_start(PACK[V2["c"]:V2["c"] + KC, 0, :], a["c_2"].rearrange("o (r c) -> (o r) c", c=P)).then_inc(pack_in, 16)
            vrows("b_in", V2["b_lat"], 0, 3)
            half("b_in", V2["b_rope"], 384)
            vrows("b_in", V2["b_qsb"], 448, 8)
            vrows("b_in", V2["b_gate"], 1984, 16)
            for name, r0 in (("g_q_head", V2["gq"]), ("g_k_head", V2["gk"])):
                vrows(name, r0, 0, 1)
                half(name, r0 + 1, NOPE)
            for k in range(3):
                src = lay(L, a["w_conv_2"])[:, k, :].rearrange("o (r c) -> (o r) c", c=P)
                pool.dma_start(PACK[44 * (k % 2):44 * (k % 2) + 44, 1 + k // 2, :], src).then_inc(pack_in, 16)
            pool.dma_start(PACK[44:88, 2, :], lay(L, a["b_conv_2"]).rearrange("o (r c) -> (o r) c", c=P)).then_inc(pack_in, 16)
            pool.dma_start(ROW, lay(L, a["b_in_2"])[:, 1472:1984]).then_inc(row_in, 16)

        N_PACK2 = 18 * 16

        def layer_pack_pe(pe, L):
            pe.wait_ge(pack_in, L * N_PACK2 + (N_PACK1 + N_PACK2))
            for k in range(3):
                pe.transpose(PS[3 + k][:, 0:P], PACK[:, k, :], ident).then_inc(cols_done, 1)

        def layer_pack_act(act, own, L):
            for k in range(3):
                act.wait_ge(cols_done, L * 3 + (2 + k + 1))
                act.activation(VEC[:, k, :], PS[3 + k][:, 0:P], ACT.Copy).then_inc(cols_ready, 1)
            act.wait_ge(cols_ready, L * 3 + 5)
            act.activation(SMB, VEC[:, 0, V2["b_qsb"]:V2["b_qsb"] + 4], ACT.Copy, scale=SB_SCALE)
            act.activation(CACT[:, :], VEC[:, 0, V2["c"]:V2["c"] + KC], ACT.Silu).then_inc(cact_ready, 1)

        def attn_proj_pe(pe, L):
            it, gi = (L, L_BLOCKS), (L, L_GROUPS)
            pe.wait_ge(hn_ready, L * 16 + 4 * KC)
            n = LB + N_ADA
            arrived(pe, n, it)
            w = slot(n, cols=448)
            for m in range(4):
                group(pe, LG + GL["lat"] + m, gi, channel_products(w, m, HN, width=P if m < 3 else ROPE))
            for b, name in ((1, "qsb"), (2, "ksb")):
                arrived(pe, n + b, it)
                for m in range(MH):
                    group(pe, LG + GL[name] + m, gi, channel_products(slot(n + b), m, HN))
            arrived(pe, n + 3, it)
            pe.wait_ge(row_in, L * 16 + 16)
            for t in range(NT):
                group(pe, LG + GL["vsb"] + t, gi, token_products(slot(n + 3), t, HN) + [(ones[0:1, :], ROW)])

        def attn_proj_act(act, L):
            gi = (L, L_GROUPS)
            act.wait_ge(cact_ready, L + 2)
            dst = [QLAT[:, 0, :], QLAT[:, 1, :], KVLAT, KROPE]
            for m in range(4):
                n = P if m < 3 else ROPE
                act.activation(dst[m], take(act, LG + m, gi)[0:n, :], ACT.Identity, bias=vec("b_lat", m)[0:n]).then_inc(proj_taken, 1)
            for m in range(MH):
                act.activation(QSB[:, m, :], take(act, LG + GL["qsb"] + m, gi)[:, :], ACT.Identity, scale=SB_SCALE,
                               bias=SMB[:, m:m + 1]).then_inc(proj_taken, 1)
            for m in range(MH):
                act.activation(KSB[:, m, :], take(act, LG + GL["ksb"] + m, gi)[:, :], ACT.Identity, bias=vec("b_ksb", m)
                               ).then_inc(proj_taken, 1)
            for t in range(NT):
                act.activation(VSB[:, t, :], take(act, LG + GL["vsb"] + t, gi)[:, :], ACT.Copy).then_inc(proj_taken, 1)

        def sb_pe(pe, L):
            pe.wait_ge(proj_taken, L * L_GROUPS + (LG + 16))
            for h in range(MH):
                if h >= 1:
                    pe.wait_ge(sb_a, L * 16 + 4 * h)
                hs = slice(h * P, (h + 1) * P)
                for j in range(NT):
                    pe.matmul(PS[j][:, j * P:S], KSB[:, h, j * P:(j + 1) * P], QSB[:, h, j * P:S],
                              start=True, stop=True).then_inc(sb_z, 1)
                for j in reversed(range(NT)):
                    pe.wait_ge(sb_sp, L * 16 + (4 * h + NT - j))
                    add = lambda l, r, o, last: pe.matmul(PS[j][:, o:o + r.shape[-1]], l, r, start=False, stop=last,
                                                          skip_group_check=True)
                    add(mask["trin"], SPB[:, j, j * P:S], j * P, False)
                    for i in range(j + 1, NT):
                        add(mask["negones"], SPB[:, i, i * P:S], i * P, False)
                    add(ident, mask["sbneg"], j * P, True).then_inc(sb_r, 1)
                if h >= 1:
                    pe.wait_ge(sb_out, L * 4 + h)
                for j in range(NT):
                    if j == 0:
                        pe.wait_ge(sb_a, L * 16 + (4 * h + 4))
                    mm = pe.matmul(PS[4][:, j * P:S], VSB[:, j, hs], ATT[:, j, j * P:S], start=(j == 0), stop=(j == NT - 1))
                mm.then_inc(sb_y, 1)

        def sb_act(act, own, L):
            for h in range(MH):
                for j in reversed(range(NT)):
                    act.wait_ge(sb_z, L * 16 + (4 * h + j + 1))
                    z = ABSZ[:, j, j * P:S]
                    if h >= 1:
                        act.wait_ge(sb_sp, L * 16 + (4 * (h - 1) + NT - j))
                    own(act.activation(z, PS[j][:, j * P:S], ACT.Abs))
                    own(act.activation(z, z, ACT.Exp, scale=-1.0))
                    act.activation(z, z, ACT.Ln, bias=EPSC[:, 1:2]).then_inc(sb_ln, 1)
                if h >= 1:
                    act.wait_ge(sb_y, L * 4 + h)
                for j in reversed(range(NT)):
                    act.wait_ge(sb_r, L * 16 + (4 * h + NT - j))
                    act.activation(ATT[:, j, j * P:S], PS[j][:, j * P:S], ACT.Exp).then_inc(sb_a, 1)
                act.wait_ge(sb_y, L * 4 + (h + 1))
                act.activation(YS[:, h, :], PS[4][:, :], ACT.Copy).then_inc(sb_out, 1)

        def sb_dve(dve, own, L):
            for h in range(MH):
                if h == 0:
                    dve.wait_ge(proj_taken, L * L_GROUPS + (LG + 16))
                for j in reversed(range(NT)):
                    dve.wait_ge(sb_ln, L * 16 + (4 * h + NT - j))
                    sp = SPB[:, j, j * P:S]
                    own(dve.scalar_tensor_tensor(sp, PS[j][:, j * P:S], 0.0, ABSZ[:, j, j * P:S], ALU.max, ALU.add))
                    sd = SPB[:, j, j * P:(j + 1) * P]
                    dve.tensor_tensor(sd, sd, mask["sbpast"], ALU.mult).then_inc(sb_sp, 1)

        def latent_act(act, own, L):
            act.wait_ge(ss_done, L * 16 + 4 * KC)
            for x, src in enumerate((QLAT[:, 0, :], QLAT[:, 1, :], KVLAT)):
                if x == 2:
                    act.wait_ge(lat_ss, L * 2 + 1)
                act.activation(SQ[:, x % 2, :], src, ACT.Square).then_inc(lat_sq, 1)
            for x, n in ((0, 256), (1, 128)):
                act.wait_ge(lat_ss, L * 2 + (x + 1))
                own(act.activation(TMP[:, x, :], PS[4 + x][:, :], ACT.Ln, scale=1.0 / n, bias=EPSC[:, 0:1]))
                act.activation(TMP[:, x, :], TMP[:, x, :], ACT.Exp, scale=-0.5).then_inc(lat_r, 1)

        def latent_pe(pe, L):
            pe.wait_ge(sb_out, L * 4 + 4)
            for x in range(3):
                pe.wait_ge(lat_sq, L * 3 + (x + 1))
                mm = pe.matmul(PS[4 + x // 2][:, :], ones, SQ[:, x % 2, :], start=(x != 1), stop=(x != 0))
                if x >= 1:
                    mm.then_inc(lat_ss, 1)

        def latent_dve(dve, L):
            for x, (dst, g) in enumerate(((QLAT[:, 0, :], vec("g_q_lat")), (QLAT[:, 1, :], vec("g_q_lat", 1)),
                                          (KVLAT, vec("g_kv_lat")))):
                dve.wait_ge(lat_r, L * 2 + (x // 2 + 1))
                dve.scalar_tensor_tensor(dst, dst, g, TMP[:, x // 2, :], ALU.mult, ALU.mult).then_inc(lat_n, 1)

        def heads_proj_pe(pe, L):
            it, gi = (L, L_BLOCKS), (L, L_GROUPS)
            n = LB + N_ADA + 4
            arrived(pe, n, it)
            wq = W[n % RING][:, 0:1536].rearrange("p (k n) -> p k n", k=2)
            wkv = W[n % RING][:, 1536:2560]
            pe.wait_ge(lat_n, L * 3 + 3)
            for name, c0, width in (("qn", 0, NOPE), ("qr", NOPE, ROPE)):
                for h in range(MH):
                    c = h * (NOPE + ROPE) + c0
                    group(pe, LG + GL[name] + h, gi, [(wq[:, k, c:c + width], QLAT[:, k, :]) for k in range(2)])
            for h in range(MH):
                group(pe, LG + GL["kn"] + h, gi, [(wkv[:, 256 * h:256 * h + NOPE], KVLAT)])
            wv = wkv.rearrange("p (h c) -> p h c", c=256)[:, :, NOPE:256]
            for t in range(NT):
                group(pe, LG + GL["vm"] + t, gi, [(KVLAT[:, t * P:(t + 1) * P], wv)])

        def heads_proj_act(act, L):
            gi = (L, L_GROUPS)
            for name, dst, n in (("qn", QN, NOPE), ("qr", QR, ROPE), ("kn", KN, NOPE), ("vm", VM, P)):
                for h in range(4):
                    act.activation(dst[:, h, :], take(act, LG + GL[name] + h, gi)[0:n, :], ACT.Copy).then_inc(proj_taken, 1)

        def head_of(i):
            return (QN[:, i, :], QR[:, i, :], QR[:, i, :], "gq") if i < MH else (KN[:, i - MH, :], KROPE, KR[:, i - MH, :], "gk")

        def heads_norm_act(act, own, L):
            act.wait_ge(proj_taken, L * L_GROUPS + (LG + GL["merge"]))
            for i in range(2 * MH):
                nope, raw, _, _ = head_of(i)
                if i >= 1:
                    act.wait_ge(hd_ss, L * 8 + i)
                act.activation(SQ[:, 0, :], nope, ACT.Square)
                act.activation(SQ[0:ROPE, 1, :], raw, ACT.Square).then_inc(hd_sq, 1)
                act.wait_ge(hd_ss, L * 8 + (i + 1))
                if i >= 2:
                    act.wait_ge(hd_n, L * 8 + (i - 1))
                r = TMP[:, i % 2, :]
                own(act.activation(r, PS[4 + i % 2][:, :], ACT.Ln, scale=1.0 / (NOPE + ROPE), bias=EPSC[:, 0:1]))
                act.activation(r, r, ACT.Exp, scale=-0.5).then_inc(hd_r, 1)

        def heads_norm_pe(pe, L):
            def rotate(i):
                pe.wait_ge(hd_n, L * 8 + (i + 1))
                if i >= 2:
                    pe.wait_ge(hd_done, L * 8 + (i - 1))
                pe.matmul(PS[6 + i % 2][:, :], mask["rot"][0:ROPE, :], head_of(i)[2], start=True, stop=True
                          ).then_inc(hd_rot, 1)
            for i in range(2 * MH):
                pe.wait_ge(hd_sq, L * 8 + (i + 1))
                if i >= 2:
                    pe.wait_ge(hd_r, L * 8 + (i - 1))
                pe.matmul(PS[4 + i % 2][:, :], ones, SQ[:, 0, :], start=True, stop=False)
                pe.matmul(PS[4 + i % 2][:, :], ones[0:ROPE, :], SQ[0:ROPE, 1, :], start=False, stop=True).then_inc(hd_ss, 1)
                if i >= 1:
                    rotate(i - 1)
            rotate(2 * MH - 1)

        def heads_norm_dve(dve, own, L):
            dve.wait_ge(rope_ready, 1)
            def rotate(i):
                dve.wait_ge(hd_rot, L * 8 + (i + 1))
                rope = head_of(i)[2]
                if i >= 1:
                    dve.wait_ge(hd_done, L * 8 + i)
                own(dve.tensor_tensor(RTM, PS[6 + i % 2][0:ROPE, :], SIN, ALU.mult))
                own(dve.tensor_tensor(rope, rope, COS, ALU.mult))
                dve.tensor_tensor(rope, rope, RTM, ALU.add).then_inc(hd_done, 1)
            for i in range(2 * MH):
                nope, raw, rope, g = head_of(i)
                dve.wait_ge(hd_r, L * 8 + (i + 1))
                r = TMP[:, i % 2, :]
                dve.scalar_tensor_tensor(nope, nope, vec(g), r, ALU.mult, ALU.mult)
                dve.scalar_tensor_tensor(rope, raw, vec(g + "_rope")[0:ROPE], r[0:ROPE, :], ALU.mult, ALU.mult).then_inc(hd_n, 1)
                if i >= 1:
                    rotate(i - 1)
            rotate(2 * MH - 1)

        def mla_pe(pe, L):
            pe.wait_ge(hd_done, L * 8 + 8)
            for h in range(MH):
                if h >= 1:
                    pe.wait_ge(la_out, L * 4 + h)
                for t in range(NT):
                    ts_, n = slice(t * P, (t + 1) * P), (t + 1) * P
                    pe.matmul(PS[t][:, 0:n], QN[:, h, ts_], KN[:, h, 0:n], start=True, stop=False)
                    pe.matmul(PS[t][:, 0:n], QR[:, h, ts_], KR[:, h, 0:n], start=False, stop=True)
                    pe.matmul(PS[t][:, t * P:n], ident, mask["ncaus"], start=False, stop=True, skip_group_check=True
                              ).then_inc(la_s, 1)
                for t in range(NT):
                    pe.wait_ge(la_p, L * 16 + (4 * h + t + 1))
                    for s in range(t + 1):
                        mm = pe.transpose(PS[4 + s][:, t * P:(t + 1) * P], PX[:, t % 2, s * P:(s + 1) * P], ident)
                    mm.then_inc(la_t, 1)
                for s in range(NT):
                    pe.wait_ge(la_pt, L * 16 + (4 * h + s + 1))
                    mm = pe.matmul(PS[0][:, s * P:S], VM[:, s, h * P:(h + 1) * P], PT[:, s, s * P:S], start=(s == 0), stop=(s == NT - 1))
                mm.then_inc(la_y, 1)

        def mla_act(act, L):
            for h in range(MH):
                for t in range(NT):
                    n, i = (t + 1) * P, 4 * h + t
                    act.wait_ge(la_max, L * 16 + (i + 1))
                    if i >= 2:
                        act.wait_ge(la_t, L * 16 + (i - 1))
                    act.activation(PX[:, t % 2, 0:n], PS[t][:, 0:n], ACT.Exp, scale=MLA_SCALE, bias=NMX[:, i:i + 1],
                                   accum_out=PSUM_[:, i:i + 1]).then_inc(la_e, 1)
                act.wait_ge(la_t, L * 16 + (4 * h + 4))
                for s in range(NT):
                    act.activation(PT[:, s, s * P:S], PS[4 + s][:, s * P:S], ACT.Copy).then_inc(la_pt, 1)
                act.wait_ge(la_y, L * 4 + (h + 1))
                act.activation(YM[:, h, :], PS[0][:, :], ACT.Copy).then_inc(la_out, 1)

        def mla_dve(dve, own, L):
            for h in range(MH):
                for t in range(NT):
                    n, i = (t + 1) * P, 4 * h + t
                    dve.wait_ge(la_s, L * 16 + (i + 1))
                    own(dve.tensor_reduce(NMX[:, i:i + 1], PS[t][:, 0:n], AX_X, ALU.max))
                    dve.tensor_scalar(NMX[:, i:i + 1], NMX[:, i:i + 1], -MLA_SCALE, None, ALU.mult).then_inc(la_max, 1)
                for t in range(NT):
                    n, i = (t + 1) * P, 4 * h + t
                    dve.wait_ge(la_e, L * 16 + (i + 1))
                    own(dve.reciprocal(PSUM_[:, i:i + 1], PSUM_[:, i:i + 1]))
                    p = PX[:, t % 2, 0:n]
                    dve.tensor_scalar(p, p, PSUM_[:, i:i + 1], None, ALU.mult).then_inc(la_p, 1)

        def up_pe(pe, L):
            pe.wait_ge(hn_ready, L * 16 + 5 * KC)
            for b in range(FT // 2):
                n = LB + 25 + b
                arrived(pe, n, (L, L_BLOCKS))
                for m in range(2):
                    for x in range(2):
                        group(pe, LG + GL["up"] + 4 * b + 2 * m + x, (L, L_GROUPS), channel_products(slot(n), 2 * x + m, HN))

        def up_act(act, L):
            def silu(p):
                act.wait_ge(ff_conv, L * 44 + (2 * p + 1))
                fa = FA[:, 2 * (p % 2), :]
                act.activation(fa, fa, ACT.Silu, bias=conv_bias(p)).then_inc(ff_silu, 1)
            act.activation(FP[:, :, 0:2], EPSC[:, 3:4].unsqueeze(2).to_broadcast([P, 4, 2]), ACT.Copy).then_inc(ff_pad, 1)
            for p in range(FT):
                for x in range(2):
                    b = take(act, LG + GL["up"] + 2 * p + x, (L, L_GROUPS))
                    if p >= 2:
                        act.wait_ge(ff_conv, L * 44 + (2 * (p - 2) + x + 1))
                    act.activation(FP[:, 2 * (p % 2) + x, 2:S + 2], b[:, :], ACT.Copy).then_inc(proj_taken, 1)
                if p >= 1:
                    silu(p - 1)
            silu(FT - 1)

        def up_dve(dve, own, L):
            def product(p):
                dve.wait_ge(ff_silu, L * 22 + (p + 1))
                dve.wait_ge(ff_conv, L * 44 + (2 * p + 2))
                i = 2 * (p % 2)
                dve.scalar_tensor_tensor(FF[:, p, :], FA[:, i + 1, :], conv_bias(FT + p), FA[:, i, :], ALU.add, ALU.mult
                                         ).then_inc(ff_ready, 1)
            dve.wait_ge(ff_pad, L + 1)
            for p in range(FT):
                if p >= 2:
                    dve.wait_ge(ff_ready, L * 22 + (p - 1))
                for x in range(2):
                    dve.wait_ge(proj_taken, L * L_GROUPS + (LG + GL["up"] + 2 * p + x + 1))
                    i = 2 * (p % 2) + x
                    acc, src = FA[:, i, :], FP[:, i, :]
                    own(dve.tensor_scalar(acc, src[:, 0:S], conv_col(0, FT * x + p), None, ALU.mult))
                    own(dve.scalar_tensor_tensor(acc, src[:, 1:S + 1], conv_col(1, FT * x + p), acc, ALU.mult, ALU.add))
                    dve.scalar_tensor_tensor(acc, src[:, 2:S + 2], conv_col(2, FT * x + p), acc, ALU.mult, ALU.add).then_inc(ff_conv, 1)
                if p >= 1:
                    product(p - 1)
            product(FT - 1)

        DOWN_K = [(0, 8), (8, 16), (16, FT)]

        def down_pe(pe, L):
            for hf in range(2):
                for kc, (k0, k1) in enumerate(DOWN_K):
                    n = LB + 36 + 3 * hf + kc
                    arrived(pe, n, (L, L_BLOCKS))
                    pe.wait_ge(ff_ready, L * 22 + k1)
                    w = slot(n, kt=k1 - k0)
                    for m in range(4):
                        g = LG + GL["down"] + 4 * hf + m
                        if kc == 0:
                            pe.wait_ge(proj_taken, L * L_GROUPS + (g - 3))
                        for k in range(k0, k1):
                            mm = pe.matmul(PS[g % 4][:, :], w[:, k - k0, m * P:(m + 1) * P], FF[:, k, :],
                                           start=(k == 0), stop=(k == FT - 1))
                        if kc == 2:
                            mm.then_inc(proj_done, 1)
                        elif m == 3:
                            mm.then_inc(down_part, 1)

        OUTB = ar(0, NT, D)

        def output_pe(pe):
            pe.wait_ge(res_added, (1 + 2 * LAYERS) * KC)
            for t in range(NT):
                for hf in range(2):
                    for j in range(4):
                        mm = pe.transpose(PS[(2 * t + hf) % 8][:, j * P:(j + 1) * P],
                                          H[:, 4 * hf + j, t * P:(t + 1) * P], ident)
                    mm.then_inc(out_t, 1)

        def output_act(act):
            for t in range(NT):
                for hf in range(2):
                    act.wait_ge(out_t, 2 * t + hf + 1)
                    act.activation(OUTB[:, t, hf * 512:(hf + 1) * 512], PS[(2 * t + hf) % 8][:, :], ACT.Copy).then_inc(out_ready, 1)

        def block1_parts(n):
            w = a["w_in"][0]
            if n < N_ADA:
                return [(slot(n), rows(a["ada_w"][0], 512 * n, 512))]
            cols = {12: 2080, 13: 2592, 14: 3104, 15: 3616, 16: 0, 17: 512, 18: 1024, 19: 1536,
                    20: 4160, 21: 5184, 23: 4672, 24: 5696}
            if n in cols:
                return [(slot(n), rows(w, cols[n], 512))]
            if n in (22, 25):
                c = 0 if n == 22 else 512
                return [(W[n % RING][:, 2048 * x:2048 * x + 2048].rearrange("p (k n) -> p k n", n=512), rows(a[name][0], c, 512))
                        for x, name in ((0, "w_branch_a"), (1, "w_branch_b"))]
            return [(slot(n), rows(a["w_out"][0], 512 * (n - 26), 512))]

        BLOCK1_END = {12: 7, 13: 11, 14: 15, 15: 19, 16: 23, 17: 27, 18: 31, 19: 35, 20: 49, 21: 50, 22: 51, 23: 65, 24: 66, 25: 67,
                      26: 71, 27: 75}

        def block1_after(n):
            return (ada_acc, n + 1) if n < N_ADA else (proj_done, BLOCK1_END[n] + 1)

        def layer_parts(L, j):
            n = LB + j
            def rows2(name, c0, cols, r0=0, r1=None):
                w = a[name + "_2"]
                v = w[bass.ds(L, 1), r0:r1 if r1 else w.shape[1], c0:c0 + cols]
                return v.rearrange("o (k p) n -> p (o k) n", p=P)
            if j < 12:
                return [(slot(n), rows2("w_ada", 512 * j, 512))]
            if j == 12:
                return [(slot(n, cols=448), rows2("w_in", 0, 448))]
            if j < 16:
                return [(slot(n), rows2("w_in", 448 + 512 * (j - 13), 512))]
            if j == 16:
                r = W[n % RING]
                return [(r[:, 0:1536].rearrange("p (k n) -> p k n", k=2), rows2("w_uq", 0, 768)),
                        (r[:, 1536:2560].rearrange("p (k n) -> p k n", k=1), rows2("w_ukv", 0, 1024))]
            if j < 23:
                hf, b = divmod(j - 17, 3)
                if b < 2:
                    return [(slot(n), rows2("w_in", 1984 + 1024 * b + 512 * hf, 512))]
                return [(W[n % RING][:, 2048 * x:2048 * x + 2048].rearrange("p (k n) -> p k n", n=512), rows2(name, 512 * hf, 512))
                        for x, name in ((0, "w_branch_mla"), (1, "w_branch_sb"))]
            if j < 25:
                return [(slot(n), rows2("w_out", 512 * (j - 23), 512))]
            if j < 36:
                b = j - 25
                return [(slot(n)[:, :, 256 * x:256 * x + 256], rows2("w_up", DFF * x + 256 * b, 256)) for x in range(2)]
            hf, kc = divmod(j - 36, 3)
            k0, k1 = DOWN_K[kc]
            return [(slot(n, kt=k1 - k0), rows2("w_down", 512 * hf, 512, k0 * P, k1 * P))]

        LAYER_END = {12: 3, 13: 7, 14: 11, 15: 15, 16: 31, 17: 45, 18: 46, 19: 47, 20: 61, 21: 62, 22: 63, 23: 67, 24: 71}
        LAYER_END.update({25 + b: 72 + 4 * b + 3 for b in range(11)})
        LAYER_END.update({38: 119, 41: 123})

        def layer_after(L, j):
            if j < RING:
                return proj_done, L * L_GROUPS + LG
            j -= RING
            if j < N_ADA:
                return ada_acc, L * N_ADA + (N_ADA + j + 1)
            if j in LAYER_END:
                return proj_done, L * L_GROUPS + (LG + LAYER_END[j] + 1)
            hf, kc = divmod(j - 36, 3)
            return down_part, L * 4 + (2 * hf + kc + 1)

        @block.sync
        def _(sp):
            sp.dma_start(X[:, :, :], a["x"].rearrange("b (t p) d -> p (b t) d", p=P)).then_inc(x_in, 16)
            for n in range(B1_BLOCKS):
                load(sp, n, None, block1_parts(n), block1_after(n - RING) if n >= RING else None)
            def rows_out(trip, j):
                r0 = (2 * trip + j) * P
                return y_rows[bass.ds(r0, P), :] if not isinstance(trip, int) else y_rows[r0:r0 + P, :]

            sp.wait_ge(table_ready, 1)
            experts = experts_of(sp, 0)
            for j in range(MOE_BLOCKS):
                load(sp, MOE_AT + j, None, expert_parts(experts, j), block1_after(MOE_AT + j - RING))
            with sp.Fori(0, MOE_TRIPS - 1) as i:
                experts = experts_of(sp, i * 2 + 2)
                for j in range(MOE_BLOCKS):
                    used = (moe_up, i * 4 + (2 * j + 2)) if j < 2 else (moe_down, i * 4 + (4 + DOWN_CREDIT))
                    load(sp, MOE_AT + j, None, expert_parts(experts, j), used)
                for j in range(2):
                    sp.wait_ge(moe_yb, i * 4 + (2 * j + 2 + YB_CREDIT))
                    sp.dma_start(rows_out(i, j), YB[:, j, :]).then_inc(y_written[j], 16)
            for j in range(2):
                sp.wait_ge(moe_yb, 2 * (MOE_SLOTS - 2 + j) + 2 + YB_CREDIT)
                sp.dma_start(rows_out(MOE_TRIPS - 1, j), YB[:, j, :]).then_inc(y_written[j], 16)
            sp.wait_ge(moe_up, MOE_SLOTS * 2)
            sp.wait_ge(moe_down, MOE_SLOTS * 2 + DOWN_CREDIT)
            with sp.Fori(0, LAYERS) as L:
                for j in range(L_BLOCKS):
                    load(sp, LB + j, None, layer_parts(L, j), layer_after(L, j))
            sp.wait_ge(out_ready, 2 * NT)
            sp.dma_start(out.rearrange("b (t p) d -> p (b t) d", p=P), OUTB[:, :, :]).then_inc(out_written, 16)
            sp.wait_ge(out_written, 16)

        @block.gpsimd
        def _(pool):
            setup_pool(pool)
            conv_pads(pool)
            pool.memset(BV[:, :, :, HD:HD + 1], 1.0).then_inc(filled, 1)
            gdn_fill_pool(pool)
            gdn_kd_pool(pool)
            rope_tables_pool(pool)
            moe_pool(pool)
            with pool.Fori(0, LAYERS) as L:
                layer_pack_pool(pool, L)

        @block.tensor
        def _(pe):
            setup_pe(pe)
            ada_pe(pe, 0)
            norm_pe(pe, 0)
            pe.wait_ge(hn_ready, KC)
            for t in range(NT):
                group(pe, t, None, token_products(GW, t, HN))
            for n in (12, 13):
                arrived(pe, n, None)
                for m in range(4):
                    group(pe, 4 * (n - 11) + m, None, channel_products(slot(n), m, HN))
            arrived(pe, 14, None)
            for t in range(NT):
                group(pe, 12 + t, None, token_products(slot(14), t, HN))
            ml_gates_pe(pe)
            pe.wait_ge(filled, 9)
            pe.wait_ge(proj_taken, 16)
            ml_pe(pe)
            arrived(pe, 15, None)
            for t in range(NT):
                group(pe, 16 + t, None, token_products(slot(15), t, HN))
            for n in (16, 17, 18):
                arrived(pe, n, None)
                for m in range(4):
                    group(pe, 4 * (n - 11) + m, None, channel_products(slot(n), m, HN))
            pe.wait_ge(ml_h, 1)
            to_channels_pe(pe, HACC, PS[4:8], hb_t)
            l2_pe(pe)
            gdn_gates_pe(pe)
            gdn_pe(pe)
            pe.wait_ge(gd_out, ROUNDS)
            arrived(pe, 19, None)
            for t in range(NT):
                group(pe, 32 + t, None, token_products(slot(19), t, HN))
            pe.wait_ge(gd_o, 1)
            to_channels_pe(pe, O, PS[4:8], oa_t)
            pe.wait_ge(oa_copied, 4)
            merge_pe(pe, 20, 36, None, None, OTV, HBT)
            out_pe(pe, 0, 26, 68, None, None)
            norm_pe(pe, 1)
            router_pe(pe)
            moe_pe(pe)
            norm_pe(pe, 2)
            with pe.Fori(0, LAYERS) as L:
                it, gi = (L, L_BLOCKS), (L, L_GROUPS)
                layer_pack_pe(pe, L)
                ada_pe(pe, L + 1)
                norm_pe(pe, L * 2 + 3)
                attn_proj_pe(pe, L)
                sb_pe(pe, L)
                latent_pe(pe, L)
                heads_proj_pe(pe, L)
                heads_norm_pe(pe, L)
                mla_pe(pe, L)
                pe.wait_ge(la_out, L * 4 + 4)
                merge_pe(pe, LB + 17, LG + GL["merge"], it, gi, YM, YS)
                out_pe(pe, L + 1, LB + 23, LG + GL["out"], it, gi)
                norm_pe(pe, L * 2 + 4)
                up_pe(pe, L)
                down_pe(pe, L)
            output_pe(pe)

        @block.scalar
        def _(act):
            own = Own(act, act_own)
            act.wait_ge(filled, 9)
            setup_act(act)
            act.wait_ge(h_ready, KC)
            norm_act(act, own, 0)
            for t in range(NT):
                act.activation(GT[:, t, :], take(act, t, None)[:, 0:64], ACT.Copy).then_inc(proj_taken, 1)
            conv_act(act, 8, 0, 4, BQK)
            bv_act(act)
            ml_gates_act(act, own)
            ml_act(act)
            for t in range(NT):
                act.activation(BO[:, t, :], take(act, 16 + t, None)[:, :], ACT.Sigmoid).then_inc(proj_taken, 1)
            ml_post_act(act, own)
            conv_act(act, 12, 8, 20, QKV)
            to_channels_act(act, HBT, PS[4:8], hb_t, hb_copied)
            l2_act(act, own)
            tok_act(act)
            gdn_gates_act(act, own)
            gdn_act(act)
            for t in range(NT):
                act.activation(Z[:, t, :], take(act, 32 + t, None)[:, :], ACT.Silu).then_inc(proj_taken, 1)
            gdn_post_act(act, own)
            to_channels_act(act, OTV, PS[4:8], oa_t, oa_copied)
            merge_act(act, 0, 36, None, None)
            residual_act(act, 0, 68, None, 2 * KC)
            act.wait_ge(res_added, KC)
            norm_act(act, own, 1)
            router_act(act, own)
            rope_tables_act(act)
            moe_act_(act)
            act.wait_ge(moe_add, KC)
            norm_act(act, own, 2)
            with act.Fori(0, LAYERS) as L:
                gi = (L, L_GROUPS)
                own.enter(L, ACT_LAYER)
                act.wait_ge(hn_ready, 3 * KC)
                act.wait_ge(res_added, L * 16 + 8)
                layer_pack_act(act, own, L)
                norm_act(act, own, L * 2 + 3)
                attn_proj_act(act, L)
                sb_act(act, own, L)
                latent_act(act, own, L)
                heads_proj_act(act, L)
                heads_norm_act(act, own, L)
                mla_act(act, L)
                merge_act(act, L + 1, LG + GL["merge"], gi, (VEC[:, 0, V2["b_gate"]:V2["b_gate"] + 8],
                                                            VEC[:, 0, V2["b_gate"] + 8:V2["b_gate"] + 16]))
                residual_act(act, L * 2 + 1, LG + GL["out"], gi, 2 * KC)
                act.wait_ge(res_added, L * 16 + 16)
                norm_act(act, own, L * 2 + 4)
                up_act(act, L)
                residual_act(act, L * 2 + 2, LG + GL["down"], gi, 5 * KC)
            own.leave(LAYERS)
            output_act(act)

        @block.vector
        def _(dve):
            own = Own(dve, dve_own)
            ada_dve(dve, own, 0, 0, None, VEC[:, 0, V_ADAB:V_ADAB + NMOD])
            gains_dve(dve, own, 0, VEC[:, 0, V_GMIX:V_GMIX + KC], VEC[:, 0, V_GFFN:V_GFFN + KC])
            norm_dve(dve, own, 0, 0)
            dve.wait_ge(filled, 9)
            conv_dve(dve, own, 8, 0, 4, lambda k, m: VEC[:, 0, V_BCONV + 8 * k + m:V_BCONV + 8 * k + m + 1])
            ml_gates_dve(dve, own)
            ml_dve(dve, own)
            conv_dve(dve, own, 12, 8, 20, lambda k, m: VEC[:, 1, 12 * k + m:12 * k + m + 1])
            l2_dve(dve)
            gdn_gates_dve(dve, own)
            gdn_dve(dve, own)
            merge_dve(dve, own, 0, 36, None)
            residual_dve(dve, 0, 68, None)
            norm_dve(dve, own, 1, 1)
            router_dve(dve, own)
            rope_tables_dve(dve, own)
            moe_dve(dve)
            moe_sum_dve(dve, own)
            final_norm_dve(dve)
            with dve.Fori(0, LAYERS) as L:
                it, gi = (L, L_BLOCKS), (L, L_GROUPS)
                own.enter(L, DVE_LAYER)
                ada_dve(dve, own, L + 1, LB, it, VEC[:, 0, 0:NMOD])
                gains_dve(dve, own, L + 1, VEC[:, 0, V2["g_norm1"]:V2["g_norm1"] + 8], VEC[:, 0, V2["g_norm2"]:V2["g_norm2"] + 8])
                norm_dve(dve, own, L * 2 + 3, 0)
                sb_dve(dve, own, L)
                latent_dve(dve, L)
                heads_norm_dve(dve, own, L)
                mla_dve(dve, own, L)
                merge_dve(dve, own, L + 1, LG + GL["merge"], gi)
                residual_dve(dve, L * 2 + 1, LG + GL["out"], gi)
                norm_dve(dve, own, L * 2 + 4, 1)
                up_dve(dve, own, L)
                residual_dve(dve, L * 2 + 2, LG + GL["down"], gi)
            own.leave(LAYERS)


def kernel(**inputs):
    import numpy as _np
    import concourse.bacc as _bacc
    from concourse import mybir as _mybir
    from concourse.bass_utils import run_bass_kernel_spmd as _run

    nc = _bacc.Bacc("TRN2", target_bir_lowering=False, num_devices=1)
    arrays, args = {}, {}
    for name, value in {**inputs, "masks": masks_array(), "freq": freq_array()}.items():
        v = _np.ascontiguousarray(value)
        arrays[f"in_{name}"] = v
        args[name] = nc.dram_tensor(f"in_{name}", v.shape, _mybir.dt.from_np(v.dtype), kind="ExternalInput").ap()
    hn_rows = nc.dram_tensor("hn_rows", (S, D), F32, kind="Internal").ap()
    idx_rows = nc.dram_tensor("idx_rows", (MOE_SLOTS, P), U32, kind="Internal").ap()
    y_rows = nc.dram_tensor("y_rows", (MOE_SLOTS * P, D), F32, kind="Internal").ap()
    out = nc.dram_tensor("out_0", (1, S, D), F32, kind="ExternalOutput").ap()
    build(nc, args, hn_rows, idx_rows, y_rows, out)
    r = _run(nc, [arrays], core_ids=[0])
    return r.results[0]["out_0"]
```

```python
from contextlib import ExitStack

import concourse.bass as bass
from concourse import mybir

ALU = mybir.AluOpType
ACT = mybir.ActivationFunctionType
F32 = mybir.dt.float32
I32 = mybir.dt.int32
U32 = mybir.dt.uint32
AX_X = mybir.AxisListType.X

P = 128
S = 512
NT = S // P
D = 1024
KC = D // P
EPS = 1e-6
NEG = -1e30
WA = 512
NH = 8
HD = 64
CH = 64
NMOD = 6 * KC
TAPS = 5
NE = 32
DE = 256
NG = 4
RING = 3
SLOT = KC * 512
LAYERS = 2
DFF = 2816
FT = DFF // P
MH = 4
NOPE, ROPE = 128, 64
MLA_SCALE = (NOPE + ROPE) ** -0.5
SB_SCALE = 128 ** -0.5
PI2 = 6.283185307179586

MASKS = ["ident", "ones", "cum0", "cum1", "blk64", "nstr0", "nstr1", "ninc0", "ninc1", "b16n", "off16",
         "ncaus", "nml0", "nml1", "trin", "negones", "sbneg", "sbpast", "rot", "iota"]

N_ADA = NMOD * P // 512
ADA_FIRST = 4 * D // 1024
B1_BLOCKS = ADA_FIRST + 2 + 1 + 1 + 3 + 1 + 6 + 2
MOE_BLOCKS = 3
L_BLOCKS = 4 + 1 + 6 + 2 + 11 + 6
ADA_LATE = N_ADA - ADA_FIRST + LAYERS * N_ADA
MOE_TRIPS = -(-((2 * S + NE * (P - 1)) // P) // 2)
MOE_SLOTS = 2 * MOE_TRIPS
MOE_AT = B1_BLOCKS
L_AT = B1_BLOCKS + MOE_BLOCKS * MOE_TRIPS
B1_GROUPS = 4 + 8 + 4 + 4 + 12 + 4 + 32 + 8 + 4
L_GROUPS = 4 + 4 + 4 + 4 + 8 + 4 + 4 + 32 + 8 + 2 * FT + 8
DVE_LAYER = 196
ACT_LAYER = 28


def masks_array():
    import numpy as np
    p, f = np.arange(P)[:, None], np.arange(P)[None, :]
    same = p // CH == f // CH
    hide = lambda keep: np.where(keep, 0.0, NEG)
    rot = np.zeros((P, P))
    for m in range(ROPE // 2):
        rot[m + ROPE // 2, m] = -1.0
        rot[m, m + ROPE // 2] = 1.0
    same16 = p // 16 == f // 16
    made = {
        "ident": p == f, "ones": np.ones((P, P)), "cum0": same & (p <= f), "cum1": same & (p >= f), "blk64": same,
        "nstr0": hide(same & (p < f)), "nstr1": hide(same & (p > f)), "ninc0": hide(same & (p <= f)),
        "ninc1": hide(same & (p >= f)), "b16n": -1.0 * same16, "off16": ~same16, "ncaus": hide(f <= p),
        "nml0": hide(p <= f), "nml1": hide(p >= f), "trin": -1.0 * (p >= f), "negones": -np.ones((P, P)),
        "sbneg": hide(p < f), "sbpast": p < f, "rot": rot, "iota": f + 0 * p}
    return np.concatenate([np.asarray(made[n], np.float32) for n in MASKS], axis=1)


def freq_array():
    import numpy as np
    half = ROPE // 2
    inv = (1.0 / (10000.0 ** (np.arange(half, dtype=np.float32) * np.float32(2.0 / ROPE)))).astype(np.float32)
    return np.concatenate([inv, inv])[:, None]


class Own:

    def __init__(self, eng, sem):
        self.eng, self.sem, self.n, self.reg, self.per = eng, sem, 0, None, 0

    def __call__(self, ins):
        self.n += 1
        ins.then_inc(self.sem, 1)
        self.eng.wait_ge(self.sem, self.n if self.reg is None else self.reg * self.per + self.n)

    def enter(self, reg, per):
        self.reg, self.per, self.start = reg, per, self.n

    def leave(self, trips):
        used = self.n - self.start
        assert used == self.per, (self.sem, used, self.per)
        self.n, self.reg = self.start + trips * self.per, None


def build(nc, a, hn_rows, idx_rows, y_rows, out):
    with ExitStack() as ctx:
        def sb(name, shape, dt=F32):
            return ctx.enter_context(nc.sbuf_tensor(name, shape, dt))

        def sem(name):
            return ctx.enter_context(nc.semaphore(name))

        H = sb("H", [P, KC, S])
        HN = sb("HN", [P, KC, S])
        W = [sb(f"W{r}", [P, SLOT]) for r in range(RING)]
        MK = sb("MK", [P, len(MASKS), P])
        mask = {n: MK[:, i, :] for i, n in enumerate(MASKS)}
        ident, ones = mask["ident"], mask["ones"]
        PACK = sb("PACK", [P, 3, P])
        VEC = sb("VEC", [P, 3, P])
        MOD = sb("MOD", [P, NMOD])
        GAIN = sb("GAIN", [P, 2, KC])
        CACT = sb("CACT", [P, 2, KC])
        MODL = sb("MODL", [P, LAYERS, NMOD])
        EPSC = sb("EPSC", [P, 4])
        GW = sb("GW", [P, KC, 64])
        RW = sb("RW", [P, KC, NG + NE])
        BC = sb("BC", [P, 32 + HD + WA])
        IFB = sb("IFB", [NH, 4])
        SQ = sb("SQ", [P, 2, S])
        RSTD = sb("RSTD", [P, S])
        TMP = sb("TMP", [P, 2, S])
        HBT = sb("HBT", [P, NT, S])
        COS, SIN = HBT[0:ROPE, 0, :], HBT[0:ROPE, 1, :]
        ROW = HBT[0:1, 2, :]
        CPAD = sb("CPAD", [P, 2 * (S + 4)])
        GT = sb("GT", [P, NT, 64])
        SM = sb("SM", [P, 208])
        FREQ = sb("FREQ", [ROPE, 1])
        ARENA_N = 21504
        AR = sb("AR", [P, ARENA_N])
        PS = [ctx.enter_context(nc.psum_tensor(f"PS{i}", [P, 512], F32)) for i in range(8)]

        def ar(off, *shape):
            n = 1
            for s in shape:
                n *= s
            assert off + n <= ARENA_N, (off, shape)
            v = AR[:, off:off + n]
            if len(shape) == 2:
                v = v.rearrange("p (a b) -> p a b", b=shape[1])
            elif len(shape) == 3:
                v = v.rearrange("p (a b c) -> p a b c", b=shape[1], c=shape[2])
            elif len(shape) == 4:
                v = v.rearrange("p (a b c d) -> p a b c d", b=shape[1], c=shape[2], d=shape[3])
            return v

        V_GMIX, V_GFFN, V_GFIN, V_ADAB, V_C, V_BCONV = 0, 8, 16, 24, 72, 80

        w_loaded = [sem(f"w_loaded{r}") for r in range(RING)]
        consts_in, masks_in, pack_in, x_in = sem("consts_in"), sem("masks_in"), sem("pack_in"), sem("x_in")
        pack_zero, pack1_in, freq_in = sem("pack_zero"), sem("pack1_in"), sem("freq_in")
        cols_done, cols_ready = sem("cols_done"), sem("cols_ready")
        filled = sem("filled")
        xt_done, h_ready = sem("xt_done"), sem("h_ready")
        cact_ready = sem("cact_ready")
        ada_acc, ada_sum, mod_ready, vec_ready = sem("ada_acc"), sem("ada_sum"), sem("mod_ready"), sem("vec_ready")
        ada_in = [sem(f"ada_in{j}") for j in range(2)]
        sq_ready, ss_done, rstd_ready, hn_ready = sem("sq_ready"), sem("ss_done"), sem("rstd_ready"), sem("hn_ready")
        proj_done, proj_taken = sem("proj_done"), sem("proj_taken")
        merged, res_added = sem("merged"), sem("res_added")
        dve_own, act_own = sem("dve_own"), sem("act_own")
        conv_done, conv_out = sem("conv_done"), sem("conv_out")
        down_part, sb_abs = sem("down_part"), sem("sb_abs")
        ff_conv, ff_pad, ff_ready, ff_silu = sem("ff_conv"), sem("ff_pad"), sem("ff_ready"), sem("ff_silu")
        gd_intra, gd_kv, gd_o, gd_out, gd_read = sem("gd_intra"), sem("gd_kv"), sem("gd_o"), sem("gd_out"), sem("gd_read")
        gd_query, gd_added = sem("gd_query"), sem("gd_added")
        gd_rstd, gd_state, gd_var, gd_vnew, gd_zero = sem("gd_rstd"), sem("gd_state"), sem("gd_var"), sem("gd_vnew"), sem("gd_zero")
        gg_abs, gg_cum, gg_exp, gg_ln, gg_ready = sem("gg_abs"), sem("gg_cum"), sem("gg_exp"), sem("gg_ln"), sem("gg_ready")
        gg_sum = sem("gg_sum")
        hb_copied, hb_t = sem("hb_copied"), sem("hb_t")
        hd_done, hd_n, hd_r, hd_rot, hd_sq = sem("hd_done"), sem("hd_n"), sem("hd_r"), sem("hd_rot"), sem("hd_sq")
        hd_ss = sem("hd_ss")
        kd_ready = sem("kd_ready")
        l2_done, l2_r, l2_sq, l2_ss = sem("l2_done"), sem("l2_r"), sem("l2_sq"), sem("l2_ss")
        la_e, la_max, la_out, la_p, la_pt = sem("la_e"), sem("la_max"), sem("la_out"), sem("la_p"), sem("la_pt")
        la_s, la_t, la_y = sem("la_s"), sem("la_t"), sem("la_y")
        lat_n, lat_r, lat_sq, lat_ss = sem("lat_n"), sem("lat_r"), sem("lat_sq"), sem("lat_ss")
        ml_abs, ml_bc, ml_cols, ml_evac, ml_exp = sem("ml_abs"), sem("ml_bc"), sem("ml_cols"), sem("ml_evac"), sem("ml_exp")
        ml_exps, ml_gate_t, ml_h, ml_masked, ml_out = sem("ml_exps"), sem("ml_gate_t"), sem("ml_h"), sem("ml_masked"), sem("ml_out")
        ml_prod, ml_rstd, ml_scan, ml_st, ml_var = sem("ml_prod"), sem("ml_rstd"), sem("ml_scan"), sem("ml_st"), sem("ml_var")
        moe_act, moe_add, moe_down = sem("moe_act"), sem("moe_add"), sem("moe_down")
        moe_up = sem("moe_up")
        oa_copied, oa_t = sem("oa_copied"), sem("oa_t")
        out_ready, out_t, out_written = sem("out_ready"), sem("out_t"), sem("out_written")
        pos_in = sem("pos_in")
        rope_arg, rope_ready = sem("rope_arg"), sem("rope_ready")
        route_arg, route_exp = sem("route_arg"), sem("route_exp")
        row_in = sem("row_in")
        sb_a, sb_ln, sb_out, sb_r, sb_sp = sem("sb_a"), sem("sb_ln"), sem("sb_out"), sem("sb_r"), sem("sb_sp")
        sb_y, sb_z = sem("sb_y"), sem("sb_z")
        tok_copied, tok_done = sem("tok_copied"), sem("tok_done")
        unit_act_done, unit_dve_done, unit_pe_done = (
            [sem(f"unit_{n}_done{p}") for p in range(2)] for n in ("act", "dve", "pe"))
        wt_done, wt_ready = sem("wt_done"), sem("wt_ready")
        hnt_done, hnt_copied, picked, ranked, blk_ready = (
            sem("hnt_done"), sem("hnt_copied"), sem("picked"), sem("ranked"), sem("blk_ready"))
        sel_ready, table_ready, hn_out, gather_go = sem("sel_ready"), sem("table_ready"), sem("hn_out"), sem("gather_go")
        moe_xt, moe_xc, moe_sg, moe_yb, moe_sum, moe_back = (
            sem("moe_xt"), sem("moe_xc"), sem("moe_sg"), sem("moe_yb"), sem("moe_sum"), sem("moe_back"))
        idx_loaded, gathered, y_written = ([sem(f"{n}{j}") for j in range(2)] for n in ("idx_loaded", "gathered", "y_written"))
        y_gathered = [sem(f"y_gathered{t}") for t in range(NT)]
        block = ctx.enter_context(nc.Block())

        def load(sp, n, it, parts, after):
            if after is not None:
                sp.wait_ge(*after)
            for dst, src in parts:
                sp.dma_start(dst, src).then_inc(w_loaded[n % RING], 32 // len(parts))

        def arrived(eng, n, it):
            v = n // RING * 32 + 32
            eng.wait_ge(w_loaded[n % RING], v if it is None else it[0] * (it[1] // RING * 32) + v)

        B1 = ADA_FIRST - 12

        def slot(n, kt=KC, cols=512):
            return W[n % RING][:, 0:kt * cols].rearrange("p (k n) -> p k n", n=cols)

        def rows(w, c0, cols):
            return w[:, c0:c0 + cols].rearrange("(k p) n -> p k n", p=P)

        X = ar(0, NT, D)
        PACK1 = [("norm_mix_g", 0, V_GMIX, 8), ("norm_ffn_g", 0, V_GFFN, 8), ("final_norm_g", 0, V_GFIN, 8),
                 ("ada_b", 0, V_ADAB, 48), ("c", 0, V_C, 8), ("mlstm_conv_w", 0, V_BCONV, 40), ("gdn_conv_w", 1, 0, 60),
                 ("b_ada_2", 2, 0, LAYERS * NMOD), ("c_2", 2, LAYERS * NMOD, KC)]

        def setup_loads_act(act):
            act.dma_start(MK[:, :, :].rearrange("p m f -> p (m f)"), a["masks"]).then_inc(masks_in, 16)
            act.wait_ge(pack_zero, 1)
            for name, pk, r0, nr in PACK1:
                v = a[name]
                flat = {1: "(r c) -> r c", 2: "o (r c) -> (o r) c", 3: "o t (r c) -> (o t r) c"}[len(v.shape)]
                act.dma_start(PACK[r0:r0 + nr, pk, :], v.rearrange(flat, c=P)).then_inc(pack1_in, 16)

        def setup_pool(pool):
            pool.memset(PACK[:, :, :], 0.0).then_inc(pack_zero, 1)
            for c, v in enumerate((EPS, 1.0, -2.0794415416798357, 0.0)):
                pool.memset(EPSC[:, c:c + 1], v).then_inc(filled, 1)
            conv_pads(pool)
            pool.memset(BV[:, :, :, HD:HD + 1], 1.0).then_inc(filled, 1)
            pool.dma_start(FREQ[:, :], a["freq"]).then_inc(freq_in, 16)
            pool.dma_start(GW[:, :, 0:32], rows(a["w_in"][0], 2048, 32)).then_inc(consts_in, 16)
            pool.dma_start(GW[:, :, 32:64], rows(a["w_in"][0], 4128, 32)).then_inc(consts_in, 16)
            pool.dma_start(RW[:, :, 0:NG], rows(a["router_group"][0], 0, NG)).then_inc(consts_in, 16)
            pool.dma_start(RW[:, :, NG:NG + NE], rows(a["router_expert"][0], 0, NE)).then_inc(consts_in, 16)
            for c0, name, w in ((0, "gdn_a_log", 16), (16, "gdn_dt_bias", 16)):
                pool.dma_start(BC[:, c0:c0 + w], a[name].rearrange("o d h -> o (d h)").to_broadcast([P, w])
                               ).then_inc(consts_in, 16)
            for c0, name, w in ((32, "gdn_norm_g", HD), (32 + HD, "mlstm_norm_g", WA)):
                pool.dma_start(BC[:, c0:c0 + w], a[name].to_broadcast([P, w])).then_inc(consts_in, 16)
            for c0, name in ((0, "mlstm_i_bias"), (2, "mlstm_f_bias")):
                pool.dma_start(IFB[:, c0:c0 + 2], a[name].rearrange("o d h -> h (o d)"),
                               allow_slow_non_contiguous=True).then_inc(consts_in, 16)

        N_CONST, N_PACK1 = 10 * 16, 16 * len(PACK1)

        def setup_pe(pe):
            pe.wait_ge(masks_in, 16)
            pe.wait_ge(pack1_in, N_PACK1)
            for k in range(3):
                pe.transpose(PS[k][:, 0:P], PACK[:, k, :], ident).then_inc(cols_done, 1)
            pe.wait_ge(x_in, 16)
            for c in range(KC):
                if c >= 5:
                    pe.wait_ge(cols_ready, c - 4)
                for t in range(NT):
                    mm = pe.transpose(PS[(c + 3) % 8][:, t * P:(t + 1) * P], X[:, t, c * P:(c + 1) * P], ident)
                mm.then_inc(xt_done, 1)

        def setup_act(act):
            for k in range(3):
                act.wait_ge(cols_done, k + 1)
                act.activation(VEC[:, k, :], PS[k][:, 0:P], ACT.Copy).then_inc(cols_ready, 1)
            act.wait_ge(cols_ready, 3)
            act.activation(CACT[:, 0, :], VEC[:, 0, V_C:V_C + KC], ACT.Silu).then_inc(cact_ready, 1)
            act.activation(CACT[:, 1, :], VEC[:, 2, LAYERS * NMOD:LAYERS * NMOD + KC], ACT.Silu).then_inc(cact_ready, 1)
            for c in range(KC):
                act.wait_ge(xt_done, c + 1)
                act.activation(H[:, c, :], PS[(c + 3) % 8][:, :], ACT.Copy).then_inc(h_ready, 1)

        AB = ar(12288, 2, SLOT)
        ADA_EXTRA = ar(20480, 2, S)

        def ada_sums(b):
            return (TMP if b < ADA_FIRST else SQ)[:, b % 2, :] if b % 4 < 2 else ADA_EXTRA[:, b % 2, :]

        def ada_block_dve(dve, own, b, w, c):
            if b >= 4:
                dve.wait_ge(ada_sum, b - 3)
            acc = ada_sums(b)
            own(dve.tensor_scalar(acc, w[:, 0, :], c[:, 0:1], None, ALU.mult))
            for k in range(1, KC):
                ins = dve.scalar_tensor_tensor(acc, w[:, k, :], c[:, k:k + 1], acc, ALU.mult, ALU.add)
                own(ins) if k < KC - 1 else ins.then_inc(ada_acc, 1)

        def ada_block_pe(pe, b):
            pe.wait_ge(ada_acc, b + 1)
            bank, c0 = (5, 4 * b) if b < N_ADA else (7, 4 * (b - N_ADA))
            for j in range(4):
                mm = pe.matmul(PS[bank][:, c0 + j:c0 + j + 1], ada_sums(b)[:, j * P:(j + 1) * P], ones[:, 0:1], start=True, stop=True)
            mm.then_inc(ada_sum, 1)

        def ada_first_dve(dve, own):
            dve.wait_ge(cact_ready, 1)
            for b in range(ADA_FIRST):
                arrived(dve, b, None)
                ada_block_dve(dve, own, b, slot(b), CACT[:, 0, :])
            dve.wait_ge(ada_sum, ADA_FIRST)
            n = 4 * ADA_FIRST
            own(dve.tensor_tensor(MOD[:, 0:n], PS[5][:, 0:n], VEC[:, 0, V_ADAB:V_ADAB + n], ALU.add))

        def gain_dve(dve, own, j, g):
            c0 = (3 * j + 1) * KC
            own(dve.scalar_tensor_tensor(GAIN[:, j, :], MOD[:, c0:c0 + KC], 1.0, g, ALU.add, ALU.mult))

        def ada_late_pool(pool):
            pool.wait_ge(gd_out, NT)
            for i in range(ADA_LATE):
                b = ADA_FIRST + i
                if i >= 2:
                    pool.wait_ge(ada_acc, b - 1)
                layer, j = divmod(b - N_ADA, N_ADA)
                src = rows(a["ada_w"][0], 512 * b, 512) if b < N_ADA else rows(a["w_ada_2"][layer], 512 * j, 512)
                pool.dma_start(AB[:, i % 2, :].rearrange("p (k n) -> p k n", n=512), src).then_inc(ada_in[i % 2], 16)

        def late_blocks(c, out):
            return [24 + c] if out else [3 * c, 3 * c + 1, 3 * c + 2]

        def ada_late_dve(dve, own, c, out):
            for i in late_blocks(c, out):
                b = ADA_FIRST + i
                dve.wait_ge(cact_ready, 2)
                dve.wait_ge(ada_in[i % 2], 16 * (i // 2 + 1))
                ada_block_dve(dve, own, b, AB[:, i % 2, :].rearrange("p (k n) -> p k n", n=512), CACT[:, int(b >= N_ADA), :])
            n = 4 * ADA_FIRST
            if not out and c == 4:
                dve.wait_ge(ada_sum, N_ADA)
                own(dve.tensor_tensor(MOD[:, n:NMOD], PS[5][:, n:NMOD], VEC[:, 0, V_ADAB + n:V_ADAB + NMOD], ALU.add))
                gain_dve(dve, own, 1, VEC[:, 0, V_GFFN:V_GFFN + KC])
                dve.sem_inc(mod_ready, 1)
            if out and c == KC - 1:
                dve.wait_ge(ada_sum, ADA_FIRST + ADA_LATE)
                own(dve.tensor_tensor(MODL[:, :, :].rearrange("p l m -> p (l m)"), PS[7][:, 0:LAYERS * NMOD],
                                      VEC[:, 2, 0:LAYERS * NMOD], ALU.add))

        def ada_late_pe(pe, c, out):
            for i in late_blocks(c, out):
                ada_block_pe(pe, ADA_FIRST + i)

        def square_act(act, k, c):
            if c >= 2:
                act.wait_ge(ss_done, k * KC + c - 1)
            act.activation(SQ[:, c % 2, :], H[:, c, :], ACT.Square).then_inc(sq_ready, 1)

        def rstd_act(act, own, k):
            act.wait_ge(ss_done, k * KC + KC)
            own(act.activation(RSTD[:, :], PS[6][:, :], ACT.Ln, scale=1.0 / D, bias=EPSC[:, 0:1]))
            act.activation(RSTD[:, :], RSTD[:, :], ACT.Exp, scale=-0.5).then_inc(rstd_ready, 1)

        def norm_act(act, own, k):
            for c in range(KC):
                square_act(act, k, c)
            rstd_act(act, own, k)

        def square_pe(pe, k, c):
            pe.wait_ge(sq_ready, k * KC + c + 1)
            pe.matmul(PS[6][:, :], ones, SQ[:, c % 2, :], start=(c == 0), stop=(c == KC - 1)).then_inc(ss_done, 1)

        def norm_pe(pe, k):
            for c in range(KC):
                square_pe(pe, k, c)

        def norm_dve(dve, own, k, j):
            dve.wait_ge(rstd_ready, k + 1)
            for c in range(KC):
                own(dve.scalar_tensor_tensor(TMP[:, c % 2, :], H[:, c, :], GAIN[:, j, c:c + 1], RSTD[:, :],
                                             ALU.mult, ALU.mult))
                sh = 3 * j * KC + c
                dve.tensor_scalar(HN[:, c, :], TMP[:, c % 2, :], MOD[:, sh:sh + 1], None, ALU.add).then_inc(hn_ready, 1)

        def group(pe, g, it, products, tiles_ready=None):
            v = g if it is None else it[0] * it[1] + g
            if it is not None or g >= 4:
                pe.wait_ge(proj_taken, v - 3)
            for i, (l, r) in enumerate(products):
                if tiles_ready:
                    pe.wait_ge(tiles_ready[0], tiles_ready[1] + (i + 1))
                m, n = l.shape[-1], 1
                for s in r.shape[1:]:
                    n *= s
                o = PS[g % 4][0:m, 0:n]
                if len(r.shape) == 3:
                    o = o.rearrange("p (a b) -> p a b", b=r.shape[2])
                mm = pe.matmul(o, l, r, start=(i == 0), stop=(i == len(products) - 1))
            mm.then_inc(proj_done, 1)
            return mm

        def take(act, g, it):
            act.wait_ge(proj_done, (g if it is None else it[0] * it[1] + g) + 1)
            return PS[g % 4]

        def channel_products(w, m, rhs, kt=KC, width=P):
            return [(w[:, k, m * P:m * P + width], rhs[:, k, :]) for k in range(kt)]

        def token_products(w, t, lhs, kt=KC):
            return [(lhs[:, k, t * P:(t + 1) * P], w[:, k, :]) for k in range(kt)]

        MG = ar(0, 2, 4, S)
        YT = ar(4096, KC, S)

        def merge_pe(pe, n0, g0, it, gi, left, right, beside=None):
            for hf in range(2):
                n = n0 + 3 * hf
                for b in range(3):
                    arrived(pe, n + b, it)
                wa = W[(n + 2) % RING][:, 0:2048].rearrange("p (k n) -> p k n", n=512)
                wb = W[(n + 2) % RING][:, 2048:4096].rearrange("p (k n) -> p k n", n=512)
                for m in range(4):
                    g = g0 + 16 * hf + 4 * m
                    group(pe, g, gi, channel_products(slot(n), m, HN))
                    group(pe, g + 1, gi, channel_products(slot(n + 1), m, HN))
                    group(pe, g + 2, gi, channel_products(wa, m, left, 4))
                    group(pe, g + 3, gi, channel_products(wb, m, right, 4))
                    if beside:
                        beside(pe, 4 * hf + m, False)

        def merge_act(act, q, g0, it, bias):
            for c in range(KC):
                if c >= 2:
                    act.wait_ge(merged, q * KC + c - 1)
                for j in range(4):
                    b = take(act, g0 + 4 * c + j, it)
                    if j < 2:
                        kw = {} if bias is None else {"bias": bias[j][:, c:c + 1]}
                        act.activation(MG[:, c % 2, j, :], b[:, :], ACT.Sigmoid, **kw).then_inc(proj_taken, 1)
                    else:
                        act.activation(MG[:, c % 2, j, :], b[:, :], ACT.Copy).then_inc(proj_taken, 1)

        def merge_dve(dve, own, q, g0, it, beside=None):
            for c in range(KC):
                if beside:
                    beside(dve, own, c, False)
                v = g0 + 4 * c + 4
                dve.wait_ge(proj_taken, v if it is None else it[0] * it[1] + v)
                m = MG[:, c % 2, :, :]
                own(dve.tensor_tensor(m[:, 0:2, :], m[:, 0:2, :], m[:, 2:4, :], ALU.mult))
                dve.tensor_tensor(YT[:, c, :], m[:, 0, :], m[:, 1, :], ALU.add).then_inc(merged, 1)

        def residual_act(act, q, g0, it, gate, norm=None):
            for c in range(KC):
                if c >= 2:
                    act.wait_ge(res_added, q * KC + c - 1)
                b = take(act, g0 + c, it)
                act.activation(TMP[:, c % 2, :], b[:, :], ACT.Copy, scale=MOD[:, gate + c:gate + c + 1]
                               ).then_inc(proj_taken, 1)
                if norm is not None and c >= 2:
                    square_act(act, norm, c - 2)
            if norm is not None:
                for c in (KC - 2, KC - 1):
                    act.wait_ge(res_added, q * KC + c + 1)
                    square_act(act, norm, c)

        def residual_dve(dve, own, q, g0, it, beside=None):
            for c in range(KC):
                if beside:
                    beside(dve, own, c, True)
                v = g0 + c + 1
                dve.wait_ge(proj_taken, v if it is None else it[0] * it[1] + v)
                dve.tensor_tensor(H[:, c, :], H[:, c, :], TMP[:, c % 2, :], ALU.add).then_inc(res_added, 1)

        def out_pe(pe, q, n0, g0, it, gi, beside=None, norm=None):
            pe.wait_ge(merged, q * KC + KC)
            for hf in range(2):
                arrived(pe, n0 + hf, it)
                for m in range(4):
                    group(pe, g0 + 4 * hf + m, gi, channel_products(slot(n0 + hf), m, YT))
                    if beside:
                        beside(pe, 4 * hf + m, True)
                    if norm is not None and 4 * hf + m >= 3:
                        square_pe(pe, norm, 4 * hf + m - 3)
            if norm is not None:
                for c in range(KC - 3, KC):
                    square_pe(pe, norm, c)

        def pad(i, width):
            return CPAD[:, (i % 2) * (S + 4):(i % 2) * (S + 4) + width]

        def conv_pads(pool):
            for i in range(2):
                pool.memset(pad(i, 2), 0.0).then_inc(filled, 1)
                pool.memset(pad(i, S + 4)[:, S + 2:S + 4], 0.0).then_inc(filled, 1)

        def conv_act(act, tiles, idx0, g0, dst):
            def silu(m):
                act.wait_ge(conv_done, idx0 + m + 1)
                act.activation(dst[:, m, :], TMP[:, (idx0 + m) % 2, :], ACT.Silu).then_inc(conv_out, 1)
            for m in range(tiles):
                i = idx0 + m
                b = take(act, g0 + m, None)
                if i >= 2:
                    act.wait_ge(conv_done, i - 1)
                act.activation(pad(i, S + 2)[:, 2:S + 2], b[:, :], ACT.Copy).then_inc(proj_taken, 1)
                if m >= 1:
                    silu(m - 1)
            silu(tiles - 1)

        def conv_dve(dve, own, tiles, idx0, g0, wcol):
            for m in range(tiles):
                i = idx0 + m
                dve.wait_ge(proj_taken, g0 + m + 1)
                if i >= 2:
                    dve.wait_ge(conv_out, i - 1)
                acc, x = TMP[:, i % 2, :], pad(i, S + 4)
                own(dve.tensor_scalar(acc, x[:, 0:S], wcol(0, m), None, ALU.mult))
                for k in range(1, TAPS):
                    ins = dve.scalar_tensor_tensor(acc, x[:, k:k + S], wcol(k, m), acc, ALU.mult, ALU.add)
                    own(ins) if k < TAPS - 1 else ins.then_inc(conv_done, 1)
                dve.wait_ge(conv_done, i + 1)

        BQK = ar(0, KC, S)
        BV = ar(4096, NT, NH, HD + 1)
        EW = ar(6176, 2, 2, NT, S)
        HACC = ar(14368, NT, WA)
        ML = ar(16416, 2, 4, S)
        MD = SQ
        MLC = SM[:, 0:128].rearrange("p (d w t h) -> p d w t h", d=2, w=2, t=NT)
        DEN = SM[:, 128:136]
        LNS = SM[:, 136:136 + 64]
        BO = ar(6176, NT, WA)
        HSQ = ar(8224, NT, WA)

        def span(d, s):
            return slice(s * P, S) if d == 0 else slice(0, (s + 1) * P)

        def ml_gates_pe(pe):
            pe.wait_ge(proj_taken, 4)
            for kind in range(2):
                for d in range(2):
                    for t in range(NT):
                        c = 32 + 16 * d + 8 * kind
                        mm = pe.transpose(PS[4 + 2 * kind + d][0:NH, t * P:(t + 1) * P], GT[:, t, c:c + NH], ident)
            mm.then_inc(ml_gate_t, 1)
            pe.wait_ge(ml_scan, 1)
            pe.wait_ge(ml_exp, 2)
            for d in range(2):
                for w in range(2):
                    for t in range(NT):
                        c = ((d * 2 + w) * NT + t) * NH
                        mm = pe.transpose(PS[7][:, c:c + NH], ML[0:NH, d, w, t * P:(t + 1) * P], ident[0:NH, 0:NH])
            mm.then_inc(ml_gate_t, 1)

        def ml_gates_dve(dve, own):
            dve.wait_ge(ml_gate_t, 1)
            dve.wait_ge(consts_in, N_CONST)
            one = EPSC[0:NH, 1:2].to_broadcast([NH, S])
            for d in range(2):
                a_, b_, m_, t_ = (ML[0:NH, d, j, :] for j in range(4))
                own(dve.tensor_scalar(b_, PS[6 + d][0:NH, :], IFB[:, 2 + d:3 + d], None, ALU.add))
                dve.scalar_tensor_tensor(t_, b_, -1.0, b_, ALU.mult, ALU.max).then_inc(ml_abs, 1)
            for d in range(2):
                a_, b_, m_, t_ = (ML[0:NH, d, j, :] for j in range(4))
                rev = (lambda v: v) if d == 0 else (lambda v: v[:, ::-1])
                dve.wait_ge(ml_exp, d + 1)
                own(dve.scalar_tensor_tensor(b_, b_, 0.0, t_, ALU.min, ALU.subtract))
                own(dve.tensor_tensor_scan(rev(t_), one, rev(b_), 0.0, ALU.mult, ALU.add))
                own(dve.scalar_tensor_tensor(a_, PS[4 + d][0:NH, :], IFB[:, d:d + 1], t_, ALU.add, ALU.subtract))
                own(dve.tensor_tensor_scan(rev(m_), rev(a_), rev(a_), 0.0, ALU.max, ALU.max))
                own(dve.scalar_tensor_tensor(b_, t_, -1.0, m_, ALU.mult, ALU.subtract))
                ins = dve.tensor_scalar(m_, m_, -1.0, None, ALU.mult)
                own(ins) if d == 0 else ins.then_inc(ml_scan, 1)

        def ml_gates_act(act, own):
            for d in range(2):
                t_ = ML[0:NH, d, 3, :]
                act.wait_ge(ml_abs, d + 1)
                own(act.activation(t_, t_, ACT.Exp, scale=-1.0))
                act.activation(t_, t_, ACT.Ln, bias=EPSC[0:NH, 1:2]).then_inc(ml_exp, 1)
            act.wait_ge(ml_gate_t, 2)
            own(act.activation(SM[:, 0:128], PS[7][:, 0:128], ACT.Copy))
            for d in range(2):
                own(act.activation(MLC[:, d, 1, :, :], MLC[:, d, 1, :, :], ACT.Exp))
            act.sem_inc(ml_cols, 1)

        def ml_pe(pe):
            def weigh(h):
                pe.wait_ge(ml_prod, 4 * h + 4)
                if h >= 2:
                    pe.wait_ge(ml_evac, 2 * (h - 2) + 2)
                for d in range(2):
                    o = PS[4 + 2 * (h % 2) + d]
                    for t in range(NT):
                        keys = range(t + 1) if d == 0 else range(t, NT)
                        for s in keys:
                            mm = pe.matmul(o[:, t * (HD + 1):(t + 1) * (HD + 1)], EW[:, h % 2, d, s, t * P:(t + 1) * P],
                                           BV[:, s, h, :], start=(s == keys[0]), stop=(s == keys[-1]))
                    mm.then_inc(ml_out, 1)
            pe.wait_ge(conv_out, 8)
            pe.wait_ge(ml_cols, 1)
            def spread(h):
                if h >= 1:
                    pe.wait_ge(ml_exps, 2 * h)
                for d in range(2):
                    pe.matmul(PS[2 + d][:, :], ident[0:NH, h:h + 1].to_broadcast([NH, P]), ML[0:NH, d, 2, :],
                              start=True, stop=True).then_inc(ml_bc, 1)

            spread(0)
            for h in range(NH):
                r = slice(HD * (h % 2), HD * (h % 2) + HD)
                for s in range(NT):
                    if 4 * h + s >= 2:
                        pe.wait_ge(ml_prod, 4 * h + s - 1)
                    pe.matmul(PS[s % 2][:, :], BQK[r, 4 + h // 2, s * P:(s + 1) * P], BQK[r, h // 2, :],
                              start=True, stop=True).then_inc(ml_st, 1)
                    if s == 1 and h >= 1:
                        weigh(h - 1)
                    if s == 1 and h + 1 < NH:
                        spread(h + 1)
            weigh(NH - 1)

        def ml_act(act):
            for h in range(NH):
                if h >= 2:
                    act.wait_ge(ml_out, 2 * (h - 2) + 2)
                for d in range(2):
                    act.wait_ge(ml_masked, 2 * h + d + 1)
                    for s in range(NT):
                        o = slice((s + 1) * P, S) if d == 0 else slice(0, s * P)
                        if o.stop > o.start:
                            act.activation(EW[:, h % 2, d, s, o], PS[2 + d][:, o], ACT.Exp, bias=MLC[:, d, 0, s, h:h + 1])
                    for s in range(NT):
                        o = slice(s * P, (s + 1) * P)
                        ins = act.activation(EW[:, h % 2, d, s, o], MD[:, d, o], ACT.Exp, bias=MLC[:, d, 0, s, h:h + 1])
                    ins.then_inc(ml_exps, 1)

        def ml_dve(dve, own):
            hv = HACC.rearrange("p t (h c) -> p t h c", c=HD)

            def evac(h):
                for d in range(2):
                    dve.wait_ge(ml_out, 2 * h + d + 1)
                    o = PS[4 + 2 * (h % 2) + d][:, 0:NT * (HD + 1)].rearrange("p (t c) -> p t c", c=HD + 1)
                    den = DEN[:, 4 * d:4 * d + 4]
                    own(dve.scalar_tensor_tensor(den, o[:, :, HD], -1.0, MLC[:, d, 1, :, h], ALU.mult, ALU.max))
                    own(dve.tensor_tensor(den, o[:, :, HD], den, ALU.max))
                    own(dve.reciprocal(den, den))
                    dst = hv[:, :, h, :] if d == 0 else TMP[:, 0, 0:NT * HD].rearrange("p (t c) -> p t c", c=HD)
                    dve.tensor_tensor(dst, o[:, :, 0:HD], den.unsqueeze(2).to_broadcast([P, NT, HD]), ALU.mult
                                      ).then_inc(ml_evac, 1)
                    dve.wait_ge(ml_evac, 2 * h + d + 1)
                own(dve.tensor_tensor(hv[:, :, h, :], hv[:, :, h, :], dst, ALU.add))

            dve.wait_ge(ml_cols, 1)
            def masked(h):
                for d in range(2):
                    dve.wait_ge(ml_bc, 2 * h + d + 1)
                    if h >= 1:
                        dve.wait_ge(ml_exps, 2 * (h - 1) + d + 1)
                    dve.tensor_tensor(MD[:, d, :].rearrange("p (t c) -> p t c", c=P),
                                      PS[2 + d][:, :].rearrange("p (t c) -> p t c", c=P),
                                      mask[f"nml{d}"].unsqueeze(1).to_broadcast([P, NT, P]), ALU.add).then_inc(ml_masked, 1)

            masked(0)
            for h in range(NH):
                dve.wait_ge(ml_exps, 2 * h + 2)
                for s in range(NT):
                    dve.wait_ge(ml_st, 4 * h + s + 1)
                    for d in range(2):
                        o = span(d, s)
                        e = EW[:, h % 2, d, s, o]
                        ins = dve.scalar_tensor_tensor(e, PS[s % 2][:, o], HD ** -0.5, e, ALU.mult, ALU.mult)
                    ins.then_inc(ml_prod, 1)
                    if s == 1 and h + 1 < NH:
                        masked(h + 1)
                if h >= 1:
                    evac(h - 1)
            evac(NH - 1)
            h32 = HACC.rearrange("p t (h c) -> p (t h) c", c=HD)
            q32 = HSQ.rearrange("p t (h c) -> p (t h) c", c=HD)
            mu, var = LNS[:, 0:32], LNS[:, 32:64]
            wide = lambda v: v.unsqueeze(2).to_broadcast([P, 32, HD])
            own(dve.tensor_reduce(mu, h32, AX_X, ALU.add))
            own(dve.tensor_scalar(mu, mu, -1.0 / HD, None, ALU.mult))
            own(dve.tensor_tensor(h32, h32, wide(mu), ALU.add))
            own(dve.tensor_tensor(HSQ[:, :, :], HACC[:, :, :], HACC[:, :, :], ALU.mult))
            dve.tensor_reduce(var, q32, AX_X, ALU.add).then_inc(ml_var, 1)
            dve.wait_ge(ml_rstd, 1)
            own(dve.tensor_tensor(h32, h32, wide(var), ALU.mult))
            own(dve.tensor_tensor(HACC[:, :, :], HACC[:, :, :],
                                  BC[:, 32 + HD:32 + HD + WA].unsqueeze(1).to_broadcast([P, NT, WA]), ALU.mult))
            dve.wait_ge(proj_taken, 20)
            dve.tensor_tensor(HACC[:, :, :], HACC[:, :, :], BO[:, :, :], ALU.mult).then_inc(ml_h, 1)

        def ml_post_act(act, own):
            act.wait_ge(ml_var, 1)
            var = LNS[:, 32:64]
            own(act.activation(var, var, ACT.Ln, scale=1.0 / HD, bias=EPSC[:, 0:1]))
            act.activation(var, var, ACT.Exp, scale=-0.5).then_inc(ml_rstd, 1)

        def to_channels_pe(pe, src, banks, done):
            for c in range(4):
                for t in range(NT):
                    mm = pe.transpose(banks[c][:, t * P:(t + 1) * P], src[:, t, c * P:(c + 1) * P], ident)
                mm.then_inc(done, 1)

        def to_channels_act(act, dst, banks, done, copied):
            for c in range(4):
                act.wait_ge(done, c + 1)
                act.activation(dst[:, c, :], banks[c][:, :], ACT.Copy).then_inc(copied, 1)

        def bv_act(act):
            for t in range(NT):
                act.activation(BV[:, t, :, 0:HD], take(act, 12 + t, None)[:, :].rearrange("p (h c) -> p h c", c=HD),
                               ACT.Copy).then_inc(proj_taken, 1)

        QKV = ar(0, 12, S)
        KD = ar(4096, 2, WA)
        U = ar(5120, 2, WA)
        KTOK = ar(6144, NT, WA)
        VTOK = ar(8192, NT, WA)
        O = ar(10240, NT, WA)
        WT = ar(12288, 2, 4, P)
        AT = ar(13312, 2, NH, P)
        ST = ar(15360, 2, 4, P)
        WTOK = ar(16384, WA)
        own4 = lambda off: [x.rearrange("p (a b) -> p a b", b=P) for x in (AR[:, 16896 + off:17408 + off], W[(B1 + 18) % RING][:, off:off + 512])]
        LT, PA, PAT, PB, PBT = (own4(512 * j) for j in range(5))
        INV = [x.rearrange("p (a b) -> p a b", b=P) for x in (AR[:, 20480:20992], W[(B1 + 18) % RING][:, 3584:4096])]
        XR = [x.rearrange("p (a b) -> p a b", b=2 * P) for x in (AR[:, 19456:20480], W[(B1 + 18) % RING][:, 2560:3584])]
        Z = ar(6144, NT, WA)
        OSQ = ar(0, NT, WA)
        SPG = SQ[:, 0, 0:128]
        ABG = SQ[:, 0, 128:256]
        NEA = SQ[:, 0, 256:272]
        SUMS = [CPAD[:, 64 * j:64 * j + 64].rearrange("p (t d h) -> p t d h", t=NT, d=2) for j in range(8)]
        GG, LNB, GC, GCB, NGC, EGC, BEG, BETA = SUMS
        KE = CPAD[:, 512:576].rearrange("p (t d h) -> p t d h", t=NT, d=2)
        CD = CPAD[:, 576:640].rearrange("p (c d h) -> p c d h", c=8, d=2)
        ROUNDS = NT
        OTV = ar(8192, NT, S)

        def l2_act(act, own):
            for pair in range(0, 8, 2):
                for m in (pair, pair + 1):
                    act.wait_ge(l2_ss, m + 1)
                    if m >= 2:
                        act.wait_ge(l2_done, m - 1)
                    own(act.activation(TMP[:, m % 2, :], PS[4 + m % 2][:, :], ACT.Ln, bias=EPSC[:, 0:1]))
                for m in (pair, pair + 1):
                    bias = EPSC[:, 2:3] if m < 4 else EPSC[:, 3:4]
                    act.activation(TMP[:, m % 2, :], TMP[:, m % 2, :], ACT.Exp, scale=-0.5, bias=bias).then_inc(l2_r, 1)

        def l2_pe(pe):
            pe.wait_ge(hb_copied, 4)
            for m in range(8):
                pe.wait_ge(l2_sq, m + 1)
                if m >= 2:
                    pe.wait_ge(l2_r, m - 1)
                pe.matmul(PS[4 + m % 2][:, :], mask["blk64"], SQ[:, m % 2, :], start=True, stop=True).then_inc(l2_ss, 1)
            for j, m in enumerate((8, 9, 10, 11, 4, 5, 6, 7)):
                if m < 8:
                    pe.wait_ge(l2_done, m + 1)
                if j >= 4:
                    pe.wait_ge(tok_copied, j - 3)
                for t in range(NT):
                    mm = pe.transpose(PS[j % 4][:, t * P:(t + 1) * P], QKV[:, m, t * P:(t + 1) * P], ident)
                mm.then_inc(tok_done, 1)

        def l2_dve(dve):
            def squares(m):
                if m >= 2:
                    dve.wait_ge(l2_ss, m - 1)
                dve.tensor_tensor(SQ[:, m % 2, :], QKV[:, m, :], QKV[:, m, :], ALU.mult).then_inc(l2_sq, 1)

            dve.wait_ge(conv_out, 20)
            squares(0)
            for m in range(8):
                if m < 7:
                    squares(m + 1)
                dve.wait_ge(l2_r, m + 1)
                dve.tensor_tensor(QKV[:, m, :], QKV[:, m, :], TMP[:, m % 2, :], ALU.mult).then_inc(l2_done, 1)

        def tok_act(act):
            for j, m in enumerate((8, 9, 10, 11, 4, 5, 6, 7)):
                act.wait_ge(tok_done, j + 1)
                dst = VTOK if m >= 8 else KTOK
                act.activation(dst[:, :, (m % 4) * P:(m % 4 + 1) * P], PS[j % 4][:, :].rearrange("p (t c) -> p t c", c=P),
                               ACT.Copy).then_inc(tok_copied, 1)

        def gdn_gates_dve(dve, own):
            v5 = lambda x: x.rearrange("p (t d k h) -> p t d k h", t=NT, d=2, k=2)
            gt = GT[:, :, 0:32].rearrange("p t (d k h) -> p t d k h", d=2, k=2)
            sp, ab = v5(SPG), v5(ABG)
            dt_bias = BC[:, 16:32].rearrange("p (d h) -> p d h", d=2).unsqueeze(1).to_broadcast([P, NT, 2, NH])
            dve.wait_ge(l2_ss, 8)
            own(dve.tensor_tensor(sp[:, :, :, 0, :], gt[:, :, :, 0, :], dt_bias, ALU.add))
            own(dve.tensor_scalar(sp[:, :, :, 1, :], gt[:, :, :, 1, :], -1.0, None, ALU.mult))
            dve.scalar_tensor_tensor(ABG, SPG, -1.0, SPG, ALU.mult, ALU.max).then_inc(gg_abs, 1)
            dve.wait_ge(gg_ln, 1)
            own(dve.scalar_tensor_tensor(SPG, SPG, 0.0, ABG, ALU.max, ALU.add))
            own(dve.tensor_scalar(NEA, NEA, -1.0, None, ALU.mult))
            own(dve.tensor_scalar(LNB, sp[:, :, :, 1, :], -1.0, None, ALU.mult))
            nea = NEA.rearrange("p (d h) -> p d h", d=2).unsqueeze(1).to_broadcast([P, NT, 2, NH])
            dve.tensor_tensor(GG, sp[:, :, :, 0, :], nea, ALU.mult).then_inc(gg_ready, 1)
            dve.wait_ge(gg_sum, 1)
            ps = lambda k: PS[4 + k][:, 0:64].rearrange("p (t d h) -> p t d h", t=NT, d=2)
            own(dve.tensor_copy(GC, ps(0)))
            own(dve.tensor_tensor(GCB, GC, LNB, ALU.add))
            own(dve.tensor_scalar(NGC, GC, -1.0, None, ALU.mult))
            dve.tensor_tensor(KE, ps(1), NGC, ALU.add).then_inc(gg_cum, 1)
            dve.wait_ge(gg_exp, 1)

        def gdn_gates_act(act, own):
            act.wait_ge(gg_abs, 1)
            own(act.activation(ABG, ABG, ACT.Exp, scale=-1.0))
            own(act.activation(NEA, BC[:, 0:16], ACT.Exp))
            act.activation(ABG, ABG, ACT.Ln, bias=EPSC[:, 1:2]).then_inc(gg_ln, 1)
            act.wait_ge(gg_cum, 1)
            act.activation(EGC, GC, ACT.Exp)
            act.activation(BEG, GCB, ACT.Exp)
            act.activation(BETA, LNB, ACT.Exp)
            act.activation(KE, KE, ACT.Exp)
            for par in range(2):
                r = slice(64 * par, 64 * par + 64)
                ends = PS[6][r, 0:P].rearrange("p (c d j q) -> p c d j q", c=8, d=2, q=2)
                ins = act.activation(CD[r, :, :, 0:4], ends[:, :, :, :, par], ACT.Exp)
            ins.then_inc(gg_exp, 1)

        def gdn_gates_pe(pe):
            pe.wait_ge(gg_ready, 1)
            for t in range(NT):
                for d in range(2):
                    c = (t * 2 + d) * NH
                    pe.matmul(PS[4][:, c:c + NH], mask[f"cum{d}"], GG[:, t, d, :], start=True, stop=True)
                g2 = GG[:, t, :, :].rearrange("p d h -> p (d h)")
                pe.matmul(PS[5][:, 16 * t:16 * t + 16], mask["blk64"], g2, start=True, stop=True)
                for hf in range(2):
                    c = 16 * (2 * t + hf)
                    mm = pe.matmul(PS[6][:, c:c + 16], mask["blk64"][:, 64 * hf:64 * hf + 1].to_broadcast([P, P]), g2,
                                   start=True, stop=True)
            mm.then_inc(gg_sum, 1)

        PE_STEPS = ["spread", "raw", "lower", "fold0", "fold1", "fold2", "fold3", "solve", "zt", "zy", "zzy", "zy1"]
        ACT_STEPS = ["decay_l", "decay_a", "square0", "square1", "square2", "zt", "zy"]
        DVE_STEPS = ["mask_l", "mask_a", "lower", "scores", "split", "inv0", "inv1", "inv2", "inv3", "solved", "y1", "y2"]

        def directions():
            for r in range(ROUNDS):
                for d in range(2):
                    yield 2 * r + d, r, d, (r if d == 0 else NT - 1 - r)

        def after(steps, name, u):
            return u * len(steps) + steps.index(name) + 1

        def by_parity(x, par):
            return x.rearrange("p (j q) c -> p j q c", q=2)[:, :, par, :]

        HJ = [slice(j * P, (j + 1) * P) for j in range(4)]

        def pair_pe(pe, u, r, d, t):
            cols = slice(t * P, (t + 1) * P)

            def step(mm, par):
                mm.then_inc(unit_pe_done[par], 1)

            def dve_at(name, par):
                pe.wait_ge(unit_dve_done[par], after(DVE_STEPS, name, u))

            def act_at(name, par):
                pe.wait_ge(unit_act_done[par], after(ACT_STEPS, name, u))

            def apply(par, left):
                for j in range(4):
                    mm = pe.matmul(PS[4 * par + j // 2][:, (j % 2) * 256:(j % 2) * 256 + 256], left[par][:, j, :], XR[par][:, j, :],
                                   start=True, stop=True)
                return mm

            def square(par, bank, left, right):
                for j in range(4):
                    mm = pe.matmul(PS[4 * par + bank][:, HJ[j]], left[par][:, j, :], right[par][:, j, 0:P], start=True, stop=True)
                return mm

            for par in range(2):
                if u > 0:
                    pe.wait_ge(unit_dve_done[par], after(DVE_STEPS, "y2", u - 1))
                for b, src in ((0, GCB), (1, GC)):
                    for j in range(4):
                        h = 2 * j + par
                        mm = pe.matmul(PS[4 * par + b][:, HJ[j]], src[:, t, d, h:h + 1].to_broadcast([P, P]), ident,
                                       start=True, stop=True)
                step(mm, par)
            if d == 1:
                pe.wait_ge(wt_ready, 2 * r + 1)
            for par in range(2):
                rows_ = slice(64 * par, 64 * par + 64)
                for b, m0 in ((2, 4), (3, 0)):
                    for j in range(4):
                        mm = pe.matmul(PS[4 * par + b][:, HJ[j]], QKV[rows_, 4 + j, cols], QKV[rows_, m0 + j, cols],
                                       start=True, stop=True)
                step(mm, par)
            for par in range(2):
                dve_at("lower", par)
                for j in range(4):
                    mm = pe.transpose(PS[4 * par][:, HJ[j]], LT[par][:, j, :], ident)
                step(mm, par)
            def fold(par, bank, power):
                for j in range(4):
                    mm = pe.matmul(PS[4 * par + bank][:, HJ[j]], power[par][:, j, :], INV[par][:, j, :], start=True, stop=True)
                return mm

            for par in range(2):
                dve_at("split", par)
                square(par, 2, PAT, PA)
                step(square(par, 3, PA, PAT), par)
            for par in range(2):
                act_at("square0", par)
                dve_at("inv0", par)
                fold(par, 0, PB)
                square(par, 2, PBT, PB)
                step(square(par, 3, PB, PBT), par)
            for par in range(2):
                act_at("square1", par)
                dve_at("inv1", par)
                fold(par, 1, PA)
                step(square(par, 2, PAT, PA), par)
            for par in range(2):
                act_at("square2", par)
                dve_at("inv2", par)
                step(fold(par, 0, PBT), par)
            for par in range(2):
                dve_at("inv3", par)
                step(apply(par, INV), par)
            for par in range(2):
                dve_at("solved", par)
                for j in range(4):
                    mm = pe.transpose(PS[4 * par + 2][:, HJ[j]], XR[par][:, j, 0:P], ident)
                step(mm, par)
            for par in range(2):
                act_at("zt", par)
                for j in range(4):
                    mm = pe.matmul(PS[4 * par + 3][:, HJ[j]], LT[par][:, j, :], XR[par][:, j, P:2 * P], start=True, stop=True)
                step(mm, par)
            for par in range(2):
                act_at("zy", par)
                step(square(par, 0, LT, PA), par)
            for par in range(2):
                dve_at("y1", par)
                step(square(par, 1, LT, PAT), par)

        def pair_act(act, u, r, d, t):
            def step(ins, par):
                ins.then_inc(unit_act_done[par], 1)

            def dve_at(name, par):
                act.wait_ge(unit_dve_done[par], after(DVE_STEPS, name, u))

            def pe_at(name, par):
                act.wait_ge(unit_pe_done[par], after(PE_STEPS, name, u))

            flat = lambda x: x.rearrange("p a b -> p (a b)")
            for par in range(2):
                dve_at("mask_l", par)
                step(act.activation(flat(LT[par]), flat(LT[par]), ACT.Exp), par)
                dve_at("mask_a", par)
                at = by_parity(AT[:, d, :, :], par)
                step(act.activation(at, at, ACT.Exp), par)
            for k, (l, lt) in enumerate(((PB, PBT), (PA, PAT))):
                for par in range(2):
                    pe_at(f"fold{k}", par)
                    act.activation(flat(l[par]), PS[4 * par + 2][:, :], ACT.Copy)
                    step(act.activation(flat(lt[par]), PS[4 * par + 3][:, :], ACT.Copy), par)
            for name, dst, b in (("fold2", PBT, 2), ("zt", LT, 2), ("zy", PA, 3)):
                for par in range(2):
                    pe_at(name, par)
                    step(act.activation(flat(dst[par]), PS[4 * par + b][:, :], ACT.Copy), par)

        def pair_dve(dve, u, r, d, t):
            def step(ins, par):
                ins.then_inc(unit_dve_done[par], 1)

            def done(name, par):
                dve.wait_ge(unit_dve_done[par], after(DVE_STEPS, name, u))

            def pe_at(name, par):
                dve.wait_ge(unit_pe_done[par], after(PE_STEPS, name, u))

            def act_at(name, par):
                dve.wait_ge(unit_act_done[par], after(ACT_STEPS, name, u))

            v4 = lambda par, b: PS[4 * par + b][:, :].rearrange("p (j c) -> p j c", c=P)
            over = lambda m: m.unsqueeze(1).to_broadcast([P, 4, P])
            by_head = lambda x, par: by_parity(x.rearrange("p (h c) -> p h c", c=HD), par)
            for par in range(2):
                heads = lambda x, w: x[:, t, d, par::2].unsqueeze(2).to_broadcast([P, 4, w])
                pe_at("spread", par)
                for b, dst, m in ((0, LT[par], f"nstr{d}"), (1, by_parity(AT[:, d, :, :], par), f"ninc{d}")):
                    for j in range(4):
                        h = 2 * j + par
                        ins = dve.scalar_tensor_tensor(dst[:, j, :], v4(par, b)[:, j, :], NGC[:, t, d, h:h + 1], mask[m],
                                                       ALU.add, ALU.add)
                    step(ins, par)
                dve.tensor_tensor(XR[par][:, :, P:P + HD], by_head(VTOK[:, t, :], par), heads(BETA, HD), ALU.mult)
                dve.tensor_tensor(XR[par][:, :, P + HD:2 * P], by_head(KTOK[:, t, :], par), heads(BEG, HD), ALU.mult)
            for par in range(2):
                pe_at("raw", par)
                act_at("decay_l", par)
                step(dve.tensor_tensor(LT[par], LT[par], v4(par, 2), ALU.mult), par)
                act_at("decay_a", par)
                at = by_parity(AT[:, d, :, :], par)
                step(dve.tensor_tensor(at, at, v4(par, 3), ALU.mult), par)
            for par in range(2):
                done("lower", par)
                dve.tensor_tensor(PAT[par], LT[par], over(mask["b16n"]), ALU.mult)
                pe_at("lower", par)
                dve.tensor_tensor(PA[par], v4(par, 0), over(mask["b16n"]), ALU.mult)
                step(dve.tensor_tensor(XR[par][:, :, 0:P], v4(par, 0), over(mask["off16"]), ALU.mult), par)
            for par in range(2):
                done("split", par)
                step(dve.tensor_tensor(INV[par], PAT[par], over(ident), ALU.add), par)
            for k, bank in ((1, 0), (2, 1), (3, 0)):
                for par in range(2):
                    done(f"inv{k - 1}", par)
                    pe_at(f"fold{k}", par)
                    step(dve.tensor_tensor(INV[par], INV[par], v4(par, bank), ALU.add), par)
            for par in range(2):
                pe_at("solve", par)
                for i in range(2):
                    ins = dve.tensor_copy(XR[par][:, 2 * i:2 * i + 2, :], PS[4 * par + i][:, :].rearrange("p (j c) -> p j c", c=2 * P))
                step(ins, par)
            for par in range(2):
                done("solved", par)
                pe_at("zzy", par)
                step(dve.tensor_tensor(PAT[par], XR[par][:, :, P:2 * P], v4(par, 0), ALU.add), par)
            for par in range(2):
                done("y1", par)
                pe_at("zy1", par)
                dve.tensor_tensor(by_head(U[:, d, :], par), PAT[par][:, :, 0:HD], v4(par, 1)[:, :, 0:HD], ALU.subtract)
                step(dve.tensor_tensor(by_head(WTOK, par), PAT[par][:, :, HD:P], v4(par, 1)[:, :, HD:P], ALU.subtract), par)

        def turn_w_pe(pe, r, d):
            for par in range(2):
                pe.wait_ge(unit_dve_done[par], after(DVE_STEPS, "y2", 2 * r + d))
            for j in range(4):
                mm = pe.transpose(PS[2][:, j * P:(j + 1) * P], WTOK[:, j * P:(j + 1) * P], ident)
            mm.then_inc(wt_done, 1)

        def turn_w_act(act, r, d):
            act.wait_ge(wt_done, 2 * r + d + 1)
            act.activation(WT[:, d, :, :].rearrange("p a b -> p (a b)"), PS[2][:, :], ACT.Copy).then_inc(wt_ready, 1)

        def steps_of(r):
            for s in range(2):
                for d in range(2):
                    yield 4 * r + 2 * s + d, s, d, (r if d == 0 else NT - 1 - r), (s if d == 0 else 1 - s)

        def recur_pe(pe, r):
            pe.wait_ge(wt_ready, 2 * r + 2)
            pe.wait_ge(kd_ready, 2 * r + 2)
            for pair in range(2):
                two = list(steps_of(r))[2 * pair:2 * pair + 2]
                for n, s, d, t, hf in two:
                    if n >= 2:
                        pe.wait_ge(gd_state, n - 1)
                    rw = slice(64 * hf, 64 * hf + 64)
                    for j in range(4):
                        mm = pe.matmul(PS[d][rw, j * P:(j + 1) * P], WT[:, d, j, rw], ST[:, d, j, :], start=True, stop=True)
                    mm.then_inc(gd_read, 1)
                for n, s, d, t, hf in two:
                    if n >= 2:
                        pe.wait_ge(gd_added, n - 1)
                    rw = slice(64 * hf, 64 * hf + 64)
                    for j in range(4):
                        c0 = t * P + 64 * hf
                        mm = pe.matmul(PS[2 + d][rw, j * P:(j + 1) * P], QKV[:, j, c0:c0 + 64], ST[:, d, j, :],
                                       start=True, stop=True)
                    mm.then_inc(gd_query, 1)
                for n, s, d, t, hf in two:
                    pe.wait_ge(gd_vnew, n + 1)
                    rw = slice(64 * hf, 64 * hf + 64)
                    for j in range(4):
                        js = slice(j * P, (j + 1) * P)
                        mm = pe.matmul(PS[4 + d][:, js], KD[rw, d, js], U[rw, d, js], start=True, stop=True)
                    mm.then_inc(gd_kv, 1)
            for d in range(2):
                for h in range(NH):
                    hs = slice(h * HD, (h + 1) * HD)
                    mm = pe.matmul(PS[6 + d][:, hs], AT[:, d, h, :], U[:, d, hs], start=True, stop=True)
                mm.then_inc(gd_intra, 1)

        def recur_dve(dve, own, r):
            v8 = lambda x: x.rearrange("p (h c) -> p h c", c=HD)
            for pair in range(2):
                two = list(steps_of(r))[2 * pair:2 * pair + 2]
                for n, s, d, t, hf in two:
                    rw = slice(64 * hf, 64 * hf + 64)
                    dve.wait_ge(gd_read, n + 1)
                    dve.tensor_tensor(U[rw, d, :], U[rw, d, :], PS[d][rw, :], ALU.subtract).then_inc(gd_vnew, 1)
                for n, s, d, t, hf in two:
                    dve.wait_ge(gd_query, n + 1)
                    own(dve.tensor_tensor(ST[:, d, :, :], ST[:, d, :, :],
                                          CD[:, 2 * t + hf, d, 0:4].unsqueeze(2).to_broadcast([P, 4, P]), ALU.mult))
                for n, s, d, t, hf in two:
                    dve.wait_ge(gd_kv, n + 1)
                    for par in range(2):
                        q = slice(64 * par, 64 * par + 64)
                        kv = PS[4 + d][q, :].rearrange("p (j c) -> p j c", c=P)
                        ins = dve.tensor_tensor(ST[q, d, :, q], ST[q, d, :, q], kv[:, :, q], ALU.add)
                        own(ins) if par == 0 else ins.then_inc(gd_state, 1)
                for n, s, d, t, hf in two:
                    rw = slice(64 * hf, 64 * hf + 64)
                    own(dve.tensor_tensor(v8(TMP[rw, d, :]), v8(PS[2 + d][rw, :]),
                                          EGC[rw, t, d, :].unsqueeze(2).to_broadcast([64, NH, HD]), ALU.mult))
                    dve.tensor_tensor(O[rw, t, :], O[rw, t, :], TMP[rw, d, :], ALU.add).then_inc(gd_added, 1)
                    dve.wait_ge(gd_added, n + 1)
                    dve.wait_ge(gd_state, n + 1)
            for d in range(2):
                t = r if d == 0 else NT - 1 - r
                dve.wait_ge(gd_intra, 2 * r + d + 1)
                own(dve.tensor_tensor(O[:, t, :], O[:, t, :], PS[6 + d][:, :], ALU.add))

        def gdn_fill_pool(pool):
            pool.wait_ge(ml_h, 1)
            pool.wait_ge(hb_copied, 4)
            pool.memset(O[:, :, :], 0.0).then_inc(gd_zero, 1)
            pool.memset(ST[:, :, :, :], 0.0).then_inc(gd_zero, 1)

        def gdn_kd_pool(pool):
            pool.wait_ge(gg_exp, 1)
            pool.wait_ge(tok_copied, 8)
            for r in range(ROUNDS):
                for d in range(2):
                    t = r if d == 0 else NT - 1 - r
                    if r >= 1:
                        pool.wait_ge(gd_kv, 4 * (r - 1) + 2 + d + 1)
                    v8 = lambda x: x.rearrange("p (h c) -> p h c", c=HD)
                    pool.tensor_tensor(v8(KD[:, d, :]), v8(KTOK[:, t, :]),
                                       KE[:, t, d, :].unsqueeze(2).to_broadcast([P, NH, HD]), ALU.mult).then_inc(kd_ready, 1)

        def gdn_pe(pe):
            pe.wait_ge(gg_exp, 1)
            pe.wait_ge(tok_copied, 8)
            pe.wait_ge(gd_zero, 2)
            for u, r, d, t in directions():
                if d == 0 and r >= 1:
                    pe.wait_ge(gd_out, r)
                pair_pe(pe, u, r, d, t)
                turn_w_pe(pe, r, d)
                if d == 1:
                    recur_pe(pe, r)

        def gdn_act(act):
            for u, r, d, t in directions():
                pair_act(act, u, r, d, t)
                turn_w_act(act, r, d)

        def gdn_dve(dve, own):
            dve.wait_ge(gd_zero, 2)
            dve.wait_ge(tok_copied, 8)
            for u, r, d, t in directions():
                if u >= 1:
                    dve.wait_ge(wt_done, u)
                pair_dve(dve, u, r, d, t)
                if d == 1:
                    recur_dve(dve, own, r)
                    dve.sem_inc(gd_out, 1)
            o32 = O.rearrange("p t (h c) -> p (t h) c", c=HD)
            q32 = OSQ.rearrange("p t (h c) -> p (t h) c", c=HD)
            var = LNS[:, 0:32]
            own(dve.tensor_tensor(OSQ[:, :, :], O[:, :, :], O[:, :, :], ALU.mult))
            dve.tensor_reduce(var, q32, AX_X, ALU.add).then_inc(gd_var, 1)
            dve.wait_ge(gd_rstd, 1)
            own(dve.tensor_tensor(o32, o32, var.unsqueeze(2).to_broadcast([P, 32, HD]), ALU.mult))
            own(dve.tensor_tensor(o32, o32, BC[:, 32:32 + HD].unsqueeze(1).to_broadcast([P, 32, HD]), ALU.mult))
            dve.wait_ge(proj_taken, 36)
            dve.tensor_tensor(O[:, :, :], O[:, :, :], Z[:, :, :], ALU.mult).then_inc(gd_o, 1)

        def gdn_post_act(act, own):
            act.wait_ge(gd_var, 1)
            var = LNS[:, 0:32]
            own(act.activation(var, var, ACT.Ln, scale=1.0 / HD, bias=EPSC[:, 0:1]))
            act.activation(var, var, ACT.Exp, scale=-0.5).then_inc(gd_rstd, 1)

        def at_route(off, *shape):
            return ar(ROUTE + off, *shape)

        ROUTE = 16384
        RL = at_route(0, NT, NG + NE)
        EL, OH1, OH2, HOT, PICK, POS, BK = (at_route(144 + NT * NE * j, NT, NE) for j in range(7))
        GEX, HIDE, GPICK = (at_route(1040 + NT * NG * j, NT, NG) for j in range(3))
        GMAX, GPROB, GIDX, V1, V2_, IDX1, DENR, WT1, WT2, BK1, BK2, POS1, POS2, TOKID = (
            at_route(1088 + NT * j, NT) for j in range(14))
        BLK = at_route(1152, P)[0:NE, :]
        LE = at_route(1280, MOE_SLOTS)[0:NE, :]
        SEL = at_route(1344, 2 * NT, P)
        BSEL = at_route(2368, 2 * NT, MOE_SLOTS)
        IDXR = at_route(2688, P)[0:MOE_SLOTS, :].bitcast(U32)
        EXPT = at_route(2816, MOE_SLOTS)[0:1, :].bitcast(I32)
        SLU = at_route(2880, 2 * NT).bitcast(U32)
        IDXB = at_route(2896, 2).bitcast(U32)
        IOTA_TMP = at_route(2944, P)
        HNT = ar(12288, NT, D)
        ROUTE_G = 76
        ROUND = 12582912.0

        def router_pe(pe):
            for t in range(NT):
                group(pe, ROUTE_G + t, None, token_products(RW, t, HN), (hn_ready, KC))
            for t in range(NT):
                for hf in range(2):
                    if t == 2 and hf == 0:
                        pe.wait_ge(proj_taken, ROUTE_G + NT)
                    for j in range(4):
                        mm = pe.transpose(PS[(2 * t + hf + 4) % 8][:, j * P:(j + 1) * P], HN[:, 4 * hf + j, t * P:(t + 1) * P],
                                          ident)
                    mm.then_inc(hnt_done, 1)
            pe.wait_ge(hnt_copied, 2 * NT)
            pe.wait_ge(picked, 1)
            for t in range(NT):
                for s in range(t + 1):
                    mm = pe.matmul(PS[4][:, t * NE:(t + 1) * NE], mask["sbpast"] if s == t else ones, HOT[:, s, :],
                                   start=(s == 0), stop=(s == t))
            for t in range(NT):
                mm = pe.matmul(PS[5][0:NE, 0:P], HOT[:, t, :], ones, start=(t == 0), stop=(t == NT - 1))
            mm.then_inc(ranked, 1)
            pe.wait_ge(blk_ready, 1)
            pe.matmul(PS[6][:, 0:NE], BLK, mask["sbpast"][0:NE, 0:NE], start=True, stop=True)
            pe.matmul(PS[7][0:NE, 0:P], mask["cum0"][0:NE, 0:NE], BLK, start=True, stop=True).then_inc(ranked, 1)
            pe.wait_ge(sel_ready, 1)
            for j in range(2 * NT):
                mm = pe.matmul(PS[5][0:MOE_SLOTS, 0:P], BSEL[:, j, :], SEL[:, j, :], start=(j == 0), stop=(j == 2 * NT - 1))
            mm = pe.matmul(PS[3][0:1, 0:MOE_SLOTS], ones[0:NE, 0:1], LE, start=True, stop=True)
            mm.then_inc(ranked, 1)

        def router_act(act, own):
            for t in range(NT):
                b = take(act, ROUTE_G + t, None)
                act.activation(RL[:, t, :], b[:, 0:NG + NE], ACT.Copy).then_inc(proj_taken, 1)
            act.wait_ge(route_arg, 1)
            act.activation(GEX, GEX, ACT.Exp).then_inc(route_exp, 1)
            for t in range(NT):
                for hf in range(2):
                    act.wait_ge(hnt_done, 2 * t + hf + 1)
                    act.activation(HNT[:, t, hf * 512:(hf + 1) * 512], PS[(2 * t + hf + 4) % 8][:, :], ACT.Copy).then_inc(hnt_copied, 1)
            act.wait_ge(route_arg, 2)
            act.activation(DENR, DENR, ACT.Exp).then_inc(route_exp, 1)

        def router_dve(dve, own):
            iota = mask["iota"]
            bc = lambda v, n: v.unsqueeze(2).to_broadcast([P, NT, n])
            counts = lambda n: iota[:, 0:n].unsqueeze(1).to_broadcast([P, NT, n])

            def first(hot, pick, low, n):
                own(dve.scalar_tensor_tensor(pick, hot, -100.0, counts(n), ALU.mult, ALU.add))
                own(dve.tensor_reduce(low, pick, AX_X, ALU.min))
                own(dve.tensor_tensor(hot, pick, bc(low, n), ALU.is_equal))

            own(dve.tensor_tensor(IOTA_TMP, ident, iota, ALU.mult))
            own(dve.tensor_reduce(TOKID[:, 0:1], IOTA_TMP, AX_X, ALU.add))
            for t in range(1, NT):
                dve.tensor_scalar(TOKID[:, t:t + 1], TOKID[:, 0:1], float(t * P), None, ALU.add)
            dve.wait_ge(proj_taken, ROUTE_G + NT)
            gl, el = RL[:, :, 0:NG], RL[:, :, NG:NG + NE]
            own(dve.tensor_reduce(GMAX, gl, AX_X, ALU.max))
            dve.tensor_tensor(GEX, gl, bc(GMAX, NG), ALU.subtract).then_inc(route_arg, 1)
            own(dve.tensor_tensor(HIDE, gl, bc(GMAX, NG), ALU.is_equal))
            first(HIDE, GPICK, GIDX, NG)
            own(dve.tensor_scalar(HIDE, HIDE, -NEG, NEG, ALU.mult, ALU.add))
            e4 = lambda v: v.rearrange("p t (g e) -> p t g e", g=NG)
            own(dve.tensor_tensor(e4(EL), e4(el), HIDE.unsqueeze(3).to_broadcast([P, NT, NG, NE // NG]), ALU.add))
            for v, hot in ((V1, OH1), (V2_, OH2)):
                own(dve.tensor_reduce(v, EL, AX_X, ALU.max))
                own(dve.tensor_tensor(hot, EL, bc(v, NE), ALU.is_equal))
                first(hot, PICK, IDX1, NE)
                if hot is OH1:
                    own(dve.scalar_tensor_tensor(EL, OH1, 3.0 * NEG, EL, ALU.mult, ALU.add))
            dve.tensor_tensor(HOT, OH1, OH2, ALU.add).then_inc(picked, 1)
            dve.tensor_tensor(DENR, V2_, V1, ALU.subtract).then_inc(route_arg, 1)
            dve.wait_ge(ranked, 1)
            own(dve.tensor_scalar(BLK, PS[5][0:NE, 0:P], 1.0 / P, 127.0 / 256.0, ALU.mult, ALU.add))
            own(dve.tensor_scalar(BLK, BLK, ROUND, None, ALU.add))
            dve.tensor_scalar(BLK, BLK, -ROUND, None, ALU.add).then_inc(blk_ready, 1)
            rank = PS[4][:, 0:NT * NE].rearrange("p (t e) -> p t e", t=NT)
            own(dve.tensor_scalar(BK, rank, 1.0 / P, -127.0 / 256.0, ALU.mult, ALU.add))
            own(dve.tensor_scalar(BK, BK, ROUND, None, ALU.add))
            own(dve.tensor_scalar(BK, BK, -ROUND, None, ALU.add))
            own(dve.scalar_tensor_tensor(POS, BK, -float(P), rank, ALU.mult, ALU.add))
            dve.wait_ge(ranked, 2)
            own(dve.tensor_tensor(BK, BK, PS[6][:, 0:NE].unsqueeze(1).to_broadcast([P, NT, NE]), ALU.add))
            dve.tensor_tensor(LE, PS[7][0:NE, 0:MOE_SLOTS], iota[0:NE, 0:MOE_SLOTS], ALU.is_le)
            for hot, bk, pos in ((OH1, BK1, POS1), (OH2, BK2, POS2)):
                own(dve.tensor_tensor(PICK, hot, BK, ALU.mult))
                own(dve.tensor_reduce(bk, PICK, AX_X, ALU.add))
                own(dve.tensor_tensor(PICK, hot, POS, ALU.mult))
                own(dve.tensor_reduce(pos, PICK, AX_X, ALU.add))
            for k, (bk, pos) in enumerate(((BK1, POS1), (BK2, POS2))):
                for t in range(NT):
                    dve.tensor_scalar(SEL[:, NT * k + t, :], iota, pos[:, t:t + 1], None, ALU.is_equal)
                    ins = dve.tensor_scalar(BSEL[:, NT * k + t, :], iota[:, 0:MOE_SLOTS], bk[:, t:t + 1], TOKID[:, t:t + 1],
                                            ALU.is_equal, ALU.mult)
                own(dve.scalar_tensor_tensor(SLU[:, NT * k:NT * k + NT], bk, float(P), pos, ALU.mult, ALU.add))
            dve.sem_inc(sel_ready, 1)
            dve.wait_ge(route_exp, 2)
            own(dve.tensor_reduce(GPROB, GEX, AX_X, ALU.add))
            own(dve.tensor_scalar(WT1, DENR, 1.0, None, ALU.add))
            own(dve.tensor_tensor(WT1, WT1, GPROB, ALU.mult))
            own(dve.reciprocal(WT1, WT1))
            own(dve.tensor_tensor(WT2, WT1, DENR, ALU.mult))
            dve.wait_ge(ranked, 3)
            own(dve.tensor_copy(IDXR, PS[5][0:MOE_SLOTS, 0:P]))
            dve.tensor_scalar(EXPT, PS[3][0:1, 0:MOE_SLOTS], float(NE - 1), None, ALU.min).then_inc(table_ready, 1)

        XG = ar(0, 2, D)
        XT = ar(2048, 2, KC, P)
        SG = ar(4096, 2, 2 * P)
        ACTT = ar(4608, 2, 2, P)
        YB = ar(5120, 2, D)
        YG = ar(8192, NT, 2, D)
        XT_CREDIT, ACT_CREDIT, DOWN_CREDIT, YB_CREDIT, Y_CREDIT = 2, 2, 4, 4, 16

        def expert_slots(j):
            up = W[(MOE_AT + j) % RING]
            down = W[(MOE_AT + 2) % RING][:, 2048 * j:2048 * j + 2048].rearrange("p (k n) -> p k n", k=2)
            return [up[:, 2048 * x:2048 * x + 2048].rearrange("p (k n) -> p k n", k=KC) for x in range(2)], down

        def expert_parts(experts, j):
            rows_of = lambda name, e: a[name][0, bass.ds(e, 1)].rearrange("o (k p) n -> p (o k) n", p=P)
            if j < 2:
                dst, _ = expert_slots(j)
                return [(dst[x], rows_of(name, experts[j])) for x, name in ((0, "w_gate"), (1, "w_up"))]
            return [(expert_slots(x)[1], rows_of("w_down", experts[x])) for x in range(2)]

        def experts_of(sp, first_block):
            return [sp.value_load(EXPT[0:1, bass.ds(first_block + x, 1)], min_val=0, max_val=NE - 1) for x in range(2)]

        def moe_pool(pool):
            pool.wait_ge(hnt_copied, 2 * NT)
            pool.dma_start(hn_rows.rearrange("(t p) d -> p t d", p=P), HNT[:, :, :]).then_inc(hn_out, 16)
            pool.wait_ge(table_ready, 1)
            pool.dma_start(idx_rows, IDXR).then_inc(hn_out, 16)
            pool.wait_ge(hn_out, 32)
            with pool.Fori(0, MOE_TRIPS) as i:
                for j in range(2):
                    pool.wait_ge(moe_xt, i * 2 + (j - 1 + XT_CREDIT))
                    pool.dma_start(IDXB[:, j:j + 1], idx_rows[bass.ds(i * 2 + j, 1), :].rearrange("o p -> p o")
                                   ).then_inc(idx_loaded[j], 16)
                    pool.wait_ge(idx_loaded[j], i * 16 + 16)
                    pool.sem_inc(gather_go, 1)
                    pool.indirect_dma_start(XG[:, j, :], None, hn_rows, bass.IndirectOffsetOnAxis(IDXB[:, j:j + 1], 0)
                                            ).then_inc(gathered[j], 16)
            for j in range(2):
                pool.wait_ge(y_written[j], MOE_TRIPS * 16 + Y_CREDIT)
            for t in range(NT):
                for k in range(2):
                    c = NT * k + t
                    pool.indirect_dma_start(YG[:, t, k, :], None, y_rows, bass.IndirectOffsetOnAxis(SLU[:, c:c + 1], 0)
                                            ).then_inc(y_gathered[t], 16)

        def moe_pe(pe):
            pe.sem_inc(moe_xt, XT_CREDIT)
            pe.sem_inc(moe_down, DOWN_CREDIT)
            pe.wait_ge(table_ready, 1)
            with pe.Fori(0, MOE_TRIPS) as i:
                for j in range(2):
                    pe.wait_ge(gathered[j], i * 16 + 16)
                    for c in range(KC):
                        mm = pe.transpose(PS[2 * j + c // 4][:, (c % 4) * P:(c % 4 + 1) * P], XG[:, j, c * P:(c + 1) * P], ident)
                    mm.then_inc(moe_xt, 1)
                for j in range(2):
                    arrived(pe, MOE_AT + j, (i, MOE_BLOCKS))
                    pe.wait_ge(moe_xc, i * 4 + (2 * j + 2))
                    pe.wait_ge(moe_yb, i * 4 + YB_CREDIT)
                    ups, _ = expert_slots(j)
                    for x, bank in ((0, 4 + j), (1, 2 * j)):
                        for f in range(2):
                            fs = slice(f * P, (f + 1) * P)
                            for k in range(KC):
                                mm = pe.matmul(PS[bank][:, fs], ups[x][:, k, fs], XT[:, j, k, :], start=(k == 0), stop=(k == KC - 1))
                        mm.then_inc(moe_up, 1)
                arrived(pe, MOE_AT + 2, (i, MOE_BLOCKS))
                for j in range(2):
                    _, down = expert_slots(j)
                    pe.wait_ge(moe_act, i * 2 + (j + 1 + ACT_CREDIT))
                    for hf in range(2):
                        for f in range(2):
                            mm = pe.matmul(PS[6 - 2 * j + hf][:, :], ACTT[:, j, f, :], down[:, f, hf * 512:(hf + 1) * 512],
                                           start=(f == 0), stop=(f == 1))
                        mm.then_inc(moe_down, 1)
            pe.wait_ge(moe_yb, MOE_SLOTS * 2 + YB_CREDIT)
            for t in range(NT):
                pe.wait_ge(moe_sum, t + 1)
                for c in range(KC):
                    mm = pe.transpose(PS[c][:, t * P:(t + 1) * P], YG[:, t, 0, c * P:(c + 1) * P], ident)
                    if t == NT - 1:
                        mm.then_inc(moe_back, 1)

        def moe_act_(act):
            act.sem_inc(moe_yb, YB_CREDIT)
            for j in range(2):
                act.sem_inc(y_written[j], Y_CREDIT)
            with act.Fori(0, MOE_TRIPS) as i:
                for j in range(2):
                    act.wait_ge(moe_up, i * 4 + (2 * j + 1))
                    act.wait_ge(moe_act, i * 2 + (j - 1 + ACT_CREDIT))
                    act.activation(SG[:, j, :], PS[4 + j][:, 0:2 * P], ACT.Silu).then_inc(moe_sg, 1)
                for j in range(2):
                    act.wait_ge(y_written[j], i * 16 + 16)
                    for hf in range(2):
                        act.wait_ge(moe_down, i * 4 + (2 * j + hf + 1 + DOWN_CREDIT))
                        act.activation(YB[:, j, hf * 512:(hf + 1) * 512], PS[6 - 2 * j + hf][:, :], ACT.Copy).then_inc(moe_yb, 1)

        def moe_dve(dve):
            dve.sem_inc(moe_act, ACT_CREDIT)
            with dve.Fori(0, MOE_TRIPS) as i:
                for j in range(2):
                    dve.wait_ge(moe_xt, i * 2 + (j + 1 + XT_CREDIT))
                    for hf in range(2):
                        dve.tensor_copy(XT[:, j, 4 * hf:4 * hf + 4, :], PS[2 * j + hf][:, :].rearrange("p (k n) -> p k n", n=P)
                                        ).then_inc(moe_xc, 1)
                for j in range(2):
                    dve.wait_ge(moe_up, i * 4 + (2 * j + 2))
                    dve.wait_ge(moe_sg, i * 2 + (j + 1))
                    dve.wait_ge(moe_down, i * 4 + (2 * j - 2 + DOWN_CREDIT))
                    dve.tensor_tensor(ACTT[:, j, :, :].rearrange("p f n -> p (f n)"), PS[2 * j][:, 0:2 * P], SG[:, j, :],
                                      ALU.mult).then_inc(moe_act, 1)

        def moe_sum_dve(dve, own):
            for t in range(NT):
                dve.wait_ge(y_gathered[t], 32)
                own(dve.tensor_scalar(YG[:, t, 0, :], YG[:, t, 0, :], WT1[:, t:t + 1], None, ALU.mult))
                dve.scalar_tensor_tensor(YG[:, t, 0, :], YG[:, t, 1, :], WT2[:, t:t + 1], YG[:, t, 0, :], ALU.mult, ALU.add
                                         ).then_inc(moe_sum, 1)
            for c in range(KC):
                dve.wait_ge(moe_back, c + 1)
                dve.scalar_tensor_tensor(H[:, c, :], PS[c][:, :], MOD[:, 5 * KC + c:5 * KC + c + 1], H[:, c, :],
                                         ALU.mult, ALU.add).then_inc(moe_add, 1)

        def final_norm_dve(dve):
            dve.wait_ge(rstd_ready, 3)
            for c in range(KC):
                dve.scalar_tensor_tensor(H[:, c, :], H[:, c, :], VEC[:, 0, V_GFIN + c:V_GFIN + c + 1], RSTD[:, :],
                                         ALU.mult, ALU.mult).then_inc(hn_ready, 1)

        def rope_tables_pool(pool):
            pool.wait_ge(merged, KC)
            pool.wait_ge(proj_done, 68)
            pool.dma_start(COS.bitcast(I32), a["positions_2"].to_broadcast([ROPE, S])).then_inc(pos_in, 16)

        def rope_tables_dve(dve, own):
            dve.wait_ge(pos_in, 16)
            dve.wait_ge(freq_in, 16)
            ang, k = TMP[0:ROPE, 0, :], TMP[0:ROPE, 1, :]
            dve.wait_ge(res_added, KC)
            own(dve.tensor_copy(ang, COS.bitcast(I32)))
            own(dve.tensor_scalar(ang, ang, FREQ[:, 0:1], None, ALU.mult))
            for j, (dst, quarter) in enumerate(((SIN, 0.0), (COS, 0.25))):
                own(dve.tensor_scalar(k, ang, 1.0 / PI2, quarter, ALU.mult, ALU.add))
                own(dve.tensor_scalar(k, k, 12582912.0, None, ALU.add))
                own(dve.tensor_scalar(k, k, -12582912.0, None, ALU.add))
                own(dve.scalar_tensor_tensor(dst, k, -6.28125, ang, ALU.mult, ALU.add))
                own(dve.scalar_tensor_tensor(dst, k, -0.0019350051879882812, dst, ALU.mult, ALU.add))
                own(dve.scalar_tensor_tensor(dst, k, -3.019916050561733e-07, dst, ALU.mult, ALU.add))
                own(dve.tensor_scalar(dst, dst, quarter * PI2, None, ALU.add))
                own(dve.tensor_scalar(dst, dst, 3.1415925, -3.1415925, ALU.min, ALU.max))
            dve.sem_inc(rope_arg, 1)

        def rope_tables_act(act):
            act.wait_ge(rope_arg, 1)
            act.activation(SIN, SIN, ACT.Sin)
            act.activation(COS, COS, ACT.Sin).then_inc(rope_ready, 1)

        QLAT, KVLAT, KROPE = ar(18432, 2, S), ar(19456, S), ar(19968, S)[0:ROPE, :]
        SMB = SM[:, 200:204]
        QSB, KSB, VSB = ar(12288, MH, S), ar(14336, MH, S), ar(16384, NT, WA)
        SPB, ATT = [ar(0, NT, S), ar(6144, NT, S)], [ar(2048, NT, S), ar(8192, NT, S)]
        YM, YS = ar(8192, MH, S), ar(10240, MH, S)
        QN, QR, KN, KR = ar(0, MH, S), ar(2048, MH, S)[0:ROPE], ar(4096, MH, S), ar(6144, MH, S)[0:ROPE]
        VM, PT, PX = ar(12288, NT, WA), ar(14336, NT, S), ar(16384, 2, S)
        RTM = ar(17408, S)[0:ROPE, :]
        HEADSQ = ar(14336, 2, 2, S)
        NMX, PSUM_ = SM[:, 0:16], SM[:, 16:32]
        FF, FP, FA = ar(0, FT, S), ar(11264, 4, S + 2), ar(13320, 4, S)
        V2 = {"g_norm1": 48, "g_norm2": 56, "g_q_lat": 64, "g_kv_lat": 66, "b_lat": 75, "b_rope": 78,
              "b_qsb": 79, "b_ksb": 83, "b_gate": 87, "gq": 103, "gq_rope": 104, "gk": 105, "gk_rope": 106}
        LB = L_AT - 12
        LG = B1_GROUPS
        GL = {"lat": 0, "qsb": 4, "ksb": 8, "vsb": 12, "qn": 16, "qr": 20, "kn": 24, "vm": 28, "merge": 32, "out": 64,
              "up": 72, "down": 116}
        vec = lambda name, i=0: VEC[:, 0, V2[name] + i:V2[name] + i + 1]
        conv_col = lambda k, m: VEC[:, 1 + k // 2, 44 * (k % 2) + m:44 * (k % 2) + m + 1]
        conv_bias = lambda m: VEC[:, 2, 44 + m:44 + m + 1]
        lay = lambda L, w: w[bass.ds(L, 1)]

        def layer_pack_pool(pool, L):
            pool.wait_ge(cols_done, L * 3 + 3)
            def vrows(name, r0, c0, n):
                src = lay(L, a[name + "_2"])[:, c0:c0 + n * P].rearrange("o (r c) -> (o r) c", c=P)
                pool.dma_start(PACK[r0:r0 + n, 0, :], src).then_inc(pack_in, 16)
            def half(name, r0, c0):
                pool.dma_start(PACK[r0:r0 + 1, 0, 0:ROPE], lay(L, a[name + "_2"])[:, c0:c0 + ROPE]).then_inc(pack_in, 16)
            vrows("g_norm1", V2["g_norm1"], 0, 8)
            vrows("g_norm2", V2["g_norm2"], 0, 8)
            vrows("g_q_lat", V2["g_q_lat"], 0, 2)
            vrows("g_kv_lat", V2["g_kv_lat"], 0, 1)
            vrows("b_in", V2["b_lat"], 0, 3)
            half("b_in", V2["b_rope"], 384)
            vrows("b_in", V2["b_qsb"], 448, 8)
            vrows("b_in", V2["b_gate"], 1984, 16)
            for name, r0 in (("g_q_head", V2["gq"]), ("g_k_head", V2["gk"])):
                vrows(name, r0, 0, 1)
                half(name, r0 + 1, NOPE)
            for k in range(3):
                src = lay(L, a["w_conv_2"])[:, k, :].rearrange("o (r c) -> (o r) c", c=P)
                pool.dma_start(PACK[44 * (k % 2):44 * (k % 2) + 44, 1 + k // 2, :], src).then_inc(pack_in, 16)
            pool.dma_start(PACK[44:88, 2, :], lay(L, a["b_conv_2"]).rearrange("o (r c) -> (o r) c", c=P)).then_inc(pack_in, 16)
            pool.wait_ge(res_added, L * 16 + 8)
            pool.dma_start(ROW, lay(L, a["b_in_2"])[:, 1472:1984]).then_inc(row_in, 16)

        N_PACK2 = 16 * 16
        PACK_BANKS = [4, 5, 7]

        def layer_pack_pe(pe, L):
            pe.wait_ge(pack_in, L * N_PACK2 + N_PACK2)
            for k in range(3):
                pe.transpose(PS[PACK_BANKS[k]][:, 0:P], PACK[:, k, :], ident).then_inc(cols_done, 1)

        def layer_pack_act(act, own, L):
            for k in range(3):
                act.wait_ge(cols_done, L * 3 + (3 + k + 1))
                act.activation(VEC[:, k, :], PS[PACK_BANKS[k]][:, 0:P], ACT.Copy).then_inc(cols_ready, 1)
            act.wait_ge(cols_ready, L * 3 + 6)
            act.activation(SMB, VEC[:, 0, V2["b_qsb"]:V2["b_qsb"] + 4], ACT.Copy, scale=SB_SCALE).then_inc(vec_ready, 1)

        def attn_proj_pe(pe, L):
            it, gi = (L, L_BLOCKS), (L, L_GROUPS)
            n = LB + 12
            arrived(pe, n, it)
            w = slot(n, cols=448)
            for m in range(4):
                group(pe, LG + GL["lat"] + m, gi, channel_products(w, m, HN, width=P if m < 3 else ROPE),
                      (hn_ready, L * 16 + 3 * KC) if m == 0 else None)
            for b, name in ((1, "qsb"), (2, "ksb")):
                arrived(pe, n + b, it)
                for m in range(MH):
                    group(pe, LG + GL[name] + m, gi, channel_products(slot(n + b), m, HN))
            arrived(pe, n + 3, it)
            pe.wait_ge(row_in, L * 16 + 16)
            for t in range(NT):
                group(pe, LG + GL["vsb"] + t, gi, token_products(slot(n + 3), t, HN) + [(ones[0:1, :], ROW)])

        def attn_proj_act(act, L):
            gi = (L, L_GROUPS)
            act.wait_ge(vec_ready, L + 1)
            dst = [QLAT[:, 0, :], QLAT[:, 1, :], KVLAT, KROPE]
            for m in range(4):
                n = P if m < 3 else ROPE
                act.activation(dst[m], take(act, LG + m, gi)[0:n, :], ACT.Identity, bias=vec("b_lat", m)[0:n]).then_inc(proj_taken, 1)
            for m in range(MH):
                act.activation(QSB[:, m, :], take(act, LG + GL["qsb"] + m, gi)[:, :], ACT.Identity, scale=SB_SCALE,
                               bias=SMB[:, m:m + 1]).then_inc(proj_taken, 1)
            for m in range(MH):
                act.activation(KSB[:, m, :], take(act, LG + GL["ksb"] + m, gi)[:, :], ACT.Identity, bias=vec("b_ksb", m)
                               ).then_inc(proj_taken, 1)
            for t in range(NT):
                act.activation(VSB[:, t, :], take(act, LG + GL["vsb"] + t, gi)[:, :], ACT.Copy).then_inc(proj_taken, 1)

        def sb_pe(pe, L):
            def scores(h):
                if h >= 2:
                    pe.wait_ge(sb_out, L * 4 + (h - 1))
                for j in range(NT):
                    pe.matmul(PS[4 * (h % 2) + j][:, j * P:S], KSB[:, h, j * P:(j + 1) * P], QSB[:, h, j * P:S],
                              start=True, stop=True).then_inc(sb_z, 1)

            def sums(h):
                sp = SPB[h % 2]
                for j in reversed(range(NT)):
                    pe.wait_ge(sb_sp, L * 16 + (4 * h + NT - j))
                    add = lambda l, r, o, last: pe.matmul(PS[4 * (h % 2) + j][:, o:o + r.shape[-1]], l, r, start=False, stop=last,
                                                          skip_group_check=True)
                    add(mask["trin"], sp[:, j, j * P:S], j * P, False)
                    for i in range(j + 1, NT):
                        add(mask["negones"], sp[:, i, i * P:S], i * P, False)
                    add(ident, mask["sbneg"], j * P, True).then_inc(sb_r, 1)

            def weigh(h):
                pe.wait_ge(sb_a, L * 16 + (4 * h + 4))
                for j in range(NT):
                    mm = pe.matmul(PS[4 * (h % 2)][:, j * P:S], VSB[:, j, h * P:(h + 1) * P], ATT[h % 2][:, j, j * P:S],
                                   start=(j == 0), stop=(j == NT - 1))
                mm.then_inc(sb_y, 1)

            pe.wait_ge(proj_taken, L * L_GROUPS + (LG + 16))
            scores(0)
            scores(1)
            sums(0)
            sums(1)
            weigh(0)
            scores(2)
            weigh(1)
            scores(3)
            sums(2)
            sums(3)
            weigh(2)
            weigh(3)

        def sb_act(act, own, L):
            def exponentials(h):
                for j in reversed(range(NT)):
                    act.wait_ge(sb_abs, L * 16 + (4 * h + NT - j))
                    z = ATT[h % 2][:, j, j * P:S]
                    own(act.activation(z, z, ACT.Exp, scale=-1.0))

            def logarithms(h):
                for j in reversed(range(NT)):
                    z = ATT[h % 2][:, j, j * P:S]
                    act.activation(z, z, ACT.Ln, bias=EPSC[:, 1:2]).then_inc(sb_ln, 1)

            def weights(h):
                for j in reversed(range(NT)):
                    act.wait_ge(sb_r, L * 16 + (4 * h + NT - j))
                    act.activation(ATT[h % 2][:, j, j * P:S], PS[4 * (h % 2) + j][:, j * P:S], ACT.Exp).then_inc(sb_a, 1)

            def result(h):
                act.wait_ge(sb_y, L * 4 + (h + 1))
                act.activation(YS[:, h, :], PS[4 * (h % 2)][:, :], ACT.Copy).then_inc(sb_out, 1)

            for pair in (0, 2):
                for stage in (exponentials, logarithms):
                    stage(pair)
                    stage(pair + 1)
                for h in (pair, pair + 1):
                    weights(h)
                    result(h)

        def sb_dve(dve, own, L):
            def absolute(h):
                for j in reversed(range(NT)):
                    dve.wait_ge(sb_z, L * 16 + (4 * h + j + 1))
                    z, positive = PS[4 * (h % 2) + j][:, j * P:S], SPB[h % 2][:, j, j * P:S]
                    own(dve.tensor_scalar(positive, z, 0.0, None, ALU.max))
                    dve.scalar_tensor_tensor(ATT[h % 2][:, j, j * P:S], positive, 2.0, z, ALU.mult, ALU.subtract
                                             ).then_inc(sb_abs, 1)

            def softplus(h):
                for j in reversed(range(NT)):
                    dve.wait_ge(sb_ln, L * 16 + (4 * h + NT - j))
                    sp = SPB[h % 2][:, j, j * P:S]
                    own(dve.tensor_tensor(sp, sp, ATT[h % 2][:, j, j * P:S], ALU.add))
                    sd = SPB[h % 2][:, j, j * P:(j + 1) * P]
                    dve.tensor_tensor(sd, sd, mask["sbpast"], ALU.mult).then_inc(sb_sp, 1)

            for pair in (0, 2):
                for h in (pair, pair + 1):
                    absolute(h)
                for h in (pair, pair + 1):
                    softplus(h)

        def latent_act(act, own, L):
            act.wait_ge(ss_done, L * 16 + 4 * KC)
            for x, src in enumerate((QLAT[:, 0, :], QLAT[:, 1, :], KVLAT)):
                if x == 2:
                    act.wait_ge(lat_ss, L * 2 + 1)
                act.activation(SQ[:, x % 2, :], src, ACT.Square).then_inc(lat_sq, 1)
            for x, n in ((0, 256), (1, 128)):
                act.wait_ge(lat_ss, L * 2 + (x + 1))
                own(act.activation(TMP[:, x, :], PS[4 + x][:, :], ACT.Ln, scale=1.0 / n, bias=EPSC[:, 0:1]))
            for x in range(2):
                act.activation(TMP[:, x, :], TMP[:, x, :], ACT.Exp, scale=-0.5).then_inc(lat_r, 1)

        def latent_pe(pe, L):
            pe.wait_ge(sb_out, L * 4 + 4)
            for x in range(3):
                pe.wait_ge(lat_sq, L * 3 + (x + 1))
                mm = pe.matmul(PS[4 + x // 2][:, :], ones, SQ[:, x % 2, :], start=(x != 1), stop=(x != 0))
                if x >= 1:
                    mm.then_inc(lat_ss, 1)

        def latent_dve(dve, L):
            for x, (dst, g) in enumerate(((QLAT[:, 0, :], vec("g_q_lat")), (QLAT[:, 1, :], vec("g_q_lat", 1)),
                                          (KVLAT, vec("g_kv_lat")))):
                dve.wait_ge(lat_r, L * 2 + (x // 2 + 1))
                dve.scalar_tensor_tensor(dst, dst, g, TMP[:, x // 2, :], ALU.mult, ALU.mult).then_inc(lat_n, 1)

        def heads_proj_pe(pe, L):
            it, gi = (L, L_BLOCKS), (L, L_GROUPS)
            n = LB + 16
            arrived(pe, n, it)
            wq = W[n % RING][:, 0:1536].rearrange("p (k n) -> p k n", k=2)
            wkv = W[n % RING][:, 1536:2560]
            pe.wait_ge(lat_n, L * 3 + 3)
            for name, c0, width in (("qn", 0, NOPE), ("qr", NOPE, ROPE)):
                for h in range(MH):
                    c = h * (NOPE + ROPE) + c0
                    group(pe, LG + GL[name] + h, gi, [(wq[:, k, c:c + width], QLAT[:, k, :]) for k in range(2)])
            for h in range(MH):
                group(pe, LG + GL["kn"] + h, gi, [(wkv[:, 256 * h:256 * h + NOPE], KVLAT)])
            wv = wkv.rearrange("p (h c) -> p h c", c=256)[:, :, NOPE:256]
            for t in range(NT):
                group(pe, LG + GL["vm"] + t, gi, [(KVLAT[:, t * P:(t + 1) * P], wv)])

        def heads_proj_act(act, L):
            gi = (L, L_GROUPS)
            for name, dst, n in (("qn", QN, NOPE), ("qr", QR, ROPE), ("kn", KN, NOPE), ("vm", VM, P)):
                for h in range(4):
                    act.activation(dst[:, h, :], take(act, LG + GL[name] + h, gi)[0:n, :], ACT.Copy).then_inc(proj_taken, 1)

        def head_of(i):
            return (QN[:, i, :], QR[:, i, :], QR[:, i, :], "gq") if i < MH else (KN[:, i - MH, :], KROPE, KR[:, i - MH, :], "gk")

        def heads_norm_act(act, own, L):
            for pair in range(0, 2 * MH, 2):
                for i in (pair, pair + 1):
                    act.wait_ge(hd_ss, L * 8 + (i + 1))
                    if i >= 2:
                        act.wait_ge(hd_n, L * 8 + (i - 1))
                    own(act.activation(TMP[:, i % 2, :], PS[4 + i % 2][:, :], ACT.Ln, scale=1.0 / (NOPE + ROPE), bias=EPSC[:, 0:1]))
                for i in (pair, pair + 1):
                    act.activation(TMP[:, i % 2, :], TMP[:, i % 2, :], ACT.Exp, scale=-0.5).then_inc(hd_r, 1)

        def heads_norm_pe(pe, L):
            def rotate(i):
                pe.wait_ge(hd_n, L * 8 + (i + 1))
                if i >= 2:
                    pe.wait_ge(hd_done, L * 8 + (i - 1))
                pe.matmul(PS[6 + i % 2][:, :], mask["rot"][0:ROPE, :], head_of(i)[2], start=True, stop=True
                          ).then_inc(hd_rot, 1)
            for i in range(2 * MH):
                pe.wait_ge(hd_sq, L * 8 + (i + 1))
                if i >= 2:
                    pe.wait_ge(hd_r, L * 8 + (i - 1))
                pe.matmul(PS[4 + i % 2][:, :], ones, HEADSQ[:, i % 2, 0, :], start=True, stop=False)
                pe.matmul(PS[4 + i % 2][:, :], ones[0:ROPE, :], HEADSQ[0:ROPE, i % 2, 1, :], start=False, stop=True).then_inc(hd_ss, 1)
                if i >= 1:
                    rotate(i - 1)
            rotate(2 * MH - 1)

        def heads_norm_dve(dve, own, L):
            dve.wait_ge(rope_ready, 1)

            def squares(i):
                nope, raw, _, _ = head_of(i)
                if i >= 2:
                    dve.wait_ge(hd_ss, L * 8 + (i - 1))
                dve.tensor_tensor(HEADSQ[:, i % 2, 0, :], nope, nope, ALU.mult)
                dve.tensor_tensor(HEADSQ[0:ROPE, i % 2, 1, :], raw, raw, ALU.mult).then_inc(hd_sq, 1)

            def rotate(i):
                dve.wait_ge(hd_rot, L * 8 + (i + 1))
                rope = head_of(i)[2]
                if i >= 1:
                    dve.wait_ge(hd_done, L * 8 + i)
                own(dve.tensor_tensor(RTM, PS[6 + i % 2][0:ROPE, :], SIN, ALU.mult))
                own(dve.tensor_tensor(rope, rope, COS, ALU.mult))
                dve.tensor_tensor(rope, rope, RTM, ALU.add).then_inc(hd_done, 1)
            dve.wait_ge(proj_taken, L * L_GROUPS + (LG + GL["merge"]))
            squares(0)
            for i in range(2 * MH):
                nope, raw, rope, g = head_of(i)
                if i + 1 < 2 * MH:
                    squares(i + 1)
                dve.wait_ge(hd_r, L * 8 + (i + 1))
                r = TMP[:, i % 2, :]
                dve.scalar_tensor_tensor(nope, nope, vec(g), r, ALU.mult, ALU.mult)
                dve.scalar_tensor_tensor(rope, raw, vec(g + "_rope")[0:ROPE], r[0:ROPE, :], ALU.mult, ALU.mult).then_inc(hd_n, 1)
                if i >= 1:
                    rotate(i - 1)
            rotate(2 * MH - 1)

        def mla_pe(pe, L):
            def scores(h):
                for t in range(NT):
                    ts_, n = slice(t * P, (t + 1) * P), (t + 1) * P
                    if h >= 1:
                        pe.wait_ge(la_e, L * 16 + (4 * (h - 1) + t + 1))
                    pe.matmul(PS[t][:, 0:n], QN[:, h, ts_], KN[:, h, 0:n], start=True, stop=False)
                    pe.matmul(PS[t][:, 0:n], QR[:, h, ts_], KR[:, h, 0:n], start=False, stop=True)
                    pe.matmul(PS[t][:, t * P:n], ident, mask["ncaus"], start=False, stop=True, skip_group_check=True
                              ).then_inc(la_s, 1)

            pe.wait_ge(hd_done, L * 8 + 8)
            scores(0)
            for h in range(MH):
                if h >= 1:
                    pe.wait_ge(la_out, L * 4 + h)
                for t in range(NT):
                    pe.wait_ge(la_p, L * 16 + (4 * h + t + 1))
                    for s in range(t + 1):
                        mm = pe.transpose(PS[4 + s][:, t * P:(t + 1) * P], PX[:, t % 2, s * P:(s + 1) * P], ident)
                    mm.then_inc(la_t, 1)
                if h + 1 < MH:
                    scores(h + 1)
                for s in range(NT):
                    pe.wait_ge(la_pt, L * 16 + (4 * h + s + 1))
                    mm = pe.matmul(PS[4][:, s * P:S], VM[:, s, h * P:(h + 1) * P], PT[:, s, s * P:S], start=(s == 0), stop=(s == NT - 1))
                mm.then_inc(la_y, 1)

        def mla_act(act, L):
            for h in range(MH):
                for t in range(NT):
                    n, i = (t + 1) * P, 4 * h + t
                    act.wait_ge(la_max, L * 16 + (i + 1))
                    if i >= 2:
                        act.wait_ge(la_t, L * 16 + (i - 1))
                    act.activation(PX[:, t % 2, 0:n], PS[t][:, 0:n], ACT.Exp, scale=MLA_SCALE, bias=NMX[:, i:i + 1],
                                   accum_out=PSUM_[:, i:i + 1]).then_inc(la_e, 1)
                act.wait_ge(la_t, L * 16 + (4 * h + 4))
                for s in range(NT):
                    act.activation(PT[:, s, s * P:S], PS[4 + s][:, s * P:S], ACT.Copy).then_inc(la_pt, 1)
                act.wait_ge(la_y, L * 4 + (h + 1))
                act.activation(YM[:, h, :], PS[4][:, :], ACT.Copy).then_inc(la_out, 1)

        def mla_dve(dve, own, L):
            for h in range(MH):
                for t in range(NT):
                    n, i = (t + 1) * P, 4 * h + t
                    dve.wait_ge(la_s, L * 16 + (i + 1))
                    own(dve.tensor_reduce(NMX[:, i:i + 1], PS[t][:, 0:n], AX_X, ALU.max))
                    dve.tensor_scalar(NMX[:, i:i + 1], NMX[:, i:i + 1], -MLA_SCALE, None, ALU.mult).then_inc(la_max, 1)
                for t in range(NT):
                    n, i = (t + 1) * P, 4 * h + t
                    dve.wait_ge(la_e, L * 16 + (i + 1))
                    own(dve.reciprocal(PSUM_[:, i:i + 1], PSUM_[:, i:i + 1]))
                    p = PX[:, t % 2, 0:n]
                    dve.tensor_scalar(p, p, PSUM_[:, i:i + 1], None, ALU.mult).then_inc(la_p, 1)

        def up_pe(pe, L):
            for b in range(FT // 2):
                n = LB + 25 + b
                arrived(pe, n, (L, L_BLOCKS))
                for m in range(2):
                    for x in range(2):
                        group(pe, LG + GL["up"] + 4 * b + 2 * m + x, (L, L_GROUPS), channel_products(slot(n), 2 * x + m, HN),
                              (hn_ready, L * 16 + 4 * KC) if b + m + x == 0 else None)

        def up_act(act, L):
            def silu(p):
                act.wait_ge(ff_conv, L * 44 + (2 * p + 1))
                fa = FA[:, 2 * (p % 2), :]
                act.activation(fa, fa, ACT.Silu, bias=conv_bias(p)).then_inc(ff_silu, 1)
            act.activation(FP[:, :, 0:2], EPSC[:, 3:4].unsqueeze(2).to_broadcast([P, 4, 2]), ACT.Copy).then_inc(ff_pad, 1)
            for p in range(FT):
                for x in range(2):
                    b = take(act, LG + GL["up"] + 2 * p + x, (L, L_GROUPS))
                    if p >= 2:
                        act.wait_ge(ff_conv, L * 44 + (2 * (p - 2) + x + 1))
                    act.activation(FP[:, 2 * (p % 2) + x, 2:S + 2], b[:, :], ACT.Copy).then_inc(proj_taken, 1)
                if p >= 1:
                    silu(p - 1)
            silu(FT - 1)

        def up_dve(dve, own, L):
            def product(p):
                dve.wait_ge(ff_silu, L * 22 + (p + 1))
                dve.wait_ge(ff_conv, L * 44 + (2 * p + 2))
                i = 2 * (p % 2)
                dve.scalar_tensor_tensor(FF[:, p, :], FA[:, i + 1, :], conv_bias(FT + p), FA[:, i, :], ALU.add, ALU.mult
                                         ).then_inc(ff_ready, 1)
            dve.wait_ge(ff_pad, L + 1)
            for p in range(FT):
                if p >= 2:
                    dve.wait_ge(ff_ready, L * 22 + (p - 1))
                for x in range(2):
                    dve.wait_ge(proj_taken, L * L_GROUPS + (LG + GL["up"] + 2 * p + x + 1))
                    i = 2 * (p % 2) + x
                    acc, src = FA[:, i, :], FP[:, i, :]
                    own(dve.tensor_scalar(acc, src[:, 0:S], conv_col(0, FT * x + p), None, ALU.mult))
                    own(dve.scalar_tensor_tensor(acc, src[:, 1:S + 1], conv_col(1, FT * x + p), acc, ALU.mult, ALU.add))
                    dve.scalar_tensor_tensor(acc, src[:, 2:S + 2], conv_col(2, FT * x + p), acc, ALU.mult, ALU.add).then_inc(ff_conv, 1)
                if p >= 1:
                    product(p - 1)
            product(FT - 1)

        DOWN_K = [(0, 8), (8, 16), (16, FT)]
        PART_CREDIT = 4

        def down_pe(pe, L):
            for hf in range(2):
                for kc, (k0, k1) in enumerate(DOWN_K):
                    n = LB + 36 + 3 * hf + kc
                    arrived(pe, n, (L, L_BLOCKS))
                    pe.wait_ge(ff_ready, L * 22 + k1)
                    w = slot(n, kt=k1 - k0)
                    for m in range(4):
                        g = LG + GL["down"] + 4 * hf + m
                        if kc == 0:
                            pe.wait_ge(proj_taken, L * L_GROUPS + (g - 3))
                        for k in range(k0, k1):
                            mm = pe.matmul(PS[g % 4][:, :], w[:, k - k0, m * P:(m + 1) * P], FF[:, k, :],
                                           start=(k == 0), stop=(k == FT - 1))
                        if kc == 2:
                            mm.then_inc(proj_done, 1)
                        elif m == 3:
                            mm.then_inc(down_part, 1)

        OUTB = ar(0, NT, D)

        def output_pe(pe):
            pe.wait_ge(res_added, (1 + 2 * LAYERS) * KC)
            for t in range(NT):
                for hf in range(2):
                    for j in range(4):
                        mm = pe.transpose(PS[(2 * t + hf) % 8][:, j * P:(j + 1) * P],
                                          H[:, 4 * hf + j, t * P:(t + 1) * P], ident)
                    mm.then_inc(out_t, 1)

        def output_act(act):
            for t in range(NT):
                for hf in range(2):
                    act.wait_ge(out_t, 2 * t + hf + 1)
                    act.activation(OUTB[:, t, hf * 512:(hf + 1) * 512], PS[(2 * t + hf) % 8][:, :], ACT.Copy).then_inc(out_ready, 1)

        def block1_parts(n):
            w = a["w_in"][0]
            if n < ADA_FIRST:
                return [(slot(n), rows(a["ada_w"][0], 512 * n, 512))]
            cols = {12: 2080, 13: 2592, 14: 3104, 15: 3616, 16: 0, 17: 512, 18: 1024, 19: 1536,
                    20: 4160, 21: 5184, 23: 4672, 24: 5696}
            j = n - B1
            if j in cols:
                return [(slot(n), rows(w, cols[j], 512))]
            if j in (22, 25):
                c = 0 if j == 22 else 512
                return [(W[n % RING][:, 2048 * x:2048 * x + 2048].rearrange("p (k n) -> p k n", n=512), rows(a[name][0], c, 512))
                        for x, name in ((0, "w_branch_a"), (1, "w_branch_b"))]
            return [(slot(n), rows(a["w_out"][0], 512 * (j - 26), 512))]

        BLOCK1_END = {12: 7, 13: 11, 14: 15, 15: 19, 16: 23, 17: 27, 18: 31, 19: 35, 20: 49, 21: 50, 22: 51, 23: 65, 24: 66, 25: 67,
                      26: 71, 27: 75}

        def block1_after(n):
            if n == B1 + 18:
                return gd_out, ROUNDS
            return (ada_acc, n + 1) if n < ADA_FIRST else (proj_done, BLOCK1_END[n - B1] + 1)

        def layer_parts(L, j):
            n = LB + j
            def rows2(name, c0, cols, r0=0, r1=None):
                w = a[name + "_2"]
                v = w[bass.ds(L, 1), r0:r1 if r1 else w.shape[1], c0:c0 + cols]
                return v.rearrange("o (k p) n -> p (o k) n", p=P)
            if j == 12:
                return [(slot(n, cols=448), rows2("w_in", 0, 448))]
            if j < 16:
                return [(slot(n), rows2("w_in", 448 + 512 * (j - 13), 512))]
            if j == 16:
                r = W[n % RING]
                return [(r[:, 0:1536].rearrange("p (k n) -> p k n", k=2), rows2("w_uq", 0, 768)),
                        (r[:, 1536:2560].rearrange("p (k n) -> p k n", k=1), rows2("w_ukv", 0, 1024))]
            if j < 23:
                hf, b = divmod(j - 17, 3)
                if b < 2:
                    return [(slot(n), rows2("w_in", 1984 + 1024 * b + 512 * hf, 512))]
                return [(W[n % RING][:, 2048 * x:2048 * x + 2048].rearrange("p (k n) -> p k n", n=512), rows2(name, 512 * hf, 512))
                        for x, name in ((0, "w_branch_mla"), (1, "w_branch_sb"))]
            if j < 25:
                return [(slot(n), rows2("w_out", 512 * (j - 23), 512))]
            if j < 36:
                b = j - 25
                return [(slot(n)[:, :, 256 * x:256 * x + 256], rows2("w_up", DFF * x + 256 * b, 256)) for x in range(2)]
            hf, kc = divmod(j - 36, 3)
            k0, k1 = DOWN_K[kc]
            return [(slot(n, kt=k1 - k0), rows2("w_down", 512 * hf, 512, k0 * P, k1 * P))]

        LAYER_END = {12: 3, 13: 7, 14: 11, 15: 15, 16: 31, 17: 45, 18: 46, 19: 47, 20: 61, 21: 62, 22: 63, 23: 67, 24: 71}
        LAYER_END.update({25 + b: 72 + 4 * b + 3 for b in range(11)})
        LAYER_END.update({38: 119, 41: 123})

        def layer_after(L, j):
            j -= RING
            if j < 12:
                return (proj_done, L * L_GROUPS + LG) if j == 11 else (down_part, L * 4 + (j - 6))
            if j in LAYER_END:
                return proj_done, L * L_GROUPS + (LG + LAYER_END[j] + 1)
            hf, kc = divmod(j - 36, 3)
            return down_part, L * 4 + (2 * hf + kc + 1 + PART_CREDIT)

        @block.sync
        def _(sp):
            for n in range(B1_BLOCKS):
                if n == 1:
                    sp.wait_ge(pack1_in, N_PACK1)
                    sp.dma_start(X[:, :, :], a["x"].rearrange("b (t p) d -> p (b t) d", p=P)).then_inc(x_in, 16)
                load(sp, n, None, block1_parts(n), block1_after(n - RING) if n >= RING else None)
            def rows_out(trip, j):
                r0 = (2 * trip + j) * P
                return y_rows[bass.ds(r0, P), :] if not isinstance(trip, int) else y_rows[r0:r0 + P, :]

            sp.wait_ge(table_ready, 1)
            experts = experts_of(sp, 0)
            for j in range(MOE_BLOCKS):
                load(sp, MOE_AT + j, None, expert_parts(experts, j), block1_after(MOE_AT + j - RING))
            with sp.Fori(0, MOE_TRIPS - 1) as i:
                experts = experts_of(sp, i * 2 + 2)
                for j in range(MOE_BLOCKS):
                    used = (moe_up, i * 4 + (2 * j + 2)) if j < 2 else (moe_down, i * 4 + (4 + DOWN_CREDIT))
                    load(sp, MOE_AT + j, None, expert_parts(experts, j), used)
                for j in range(2):
                    sp.wait_ge(moe_yb, i * 4 + (2 * j + 2 + YB_CREDIT))
                    sp.dma_start(rows_out(i, j), YB[:, j, :]).then_inc(y_written[j], 16)
            for j in range(2):
                sp.wait_ge(moe_yb, 2 * (MOE_SLOTS - 2 + j) + 2 + YB_CREDIT)
                sp.dma_start(rows_out(MOE_TRIPS - 1, j), YB[:, j, :]).then_inc(y_written[j], 16)
            sp.wait_ge(moe_up, MOE_SLOTS * 2)
            sp.wait_ge(moe_down, MOE_SLOTS * 2 + DOWN_CREDIT)
            with sp.Fori(0, LAYERS) as L:
                for j in range(12, 12 + L_BLOCKS):
                    load(sp, LB + j, None, layer_parts(L, j), layer_after(L, j))
            sp.wait_ge(out_ready, 2 * NT)
            sp.dma_start(out.rearrange("b (t p) d -> p (b t) d", p=P), OUTB[:, :, :]).then_inc(out_written, 16)
            sp.wait_ge(out_written, 16)

        @block.gpsimd
        def _(pool):
            setup_pool(pool)
            gdn_fill_pool(pool)
            gdn_kd_pool(pool)
            ada_late_pool(pool)
            rope_tables_pool(pool)
            moe_pool(pool)
            with pool.Fori(0, LAYERS) as L:
                layer_pack_pool(pool, L)

        @block.tensor
        def _(pe):
            setup_pe(pe)
            pe.wait_ge(h_ready, KC)
            for b in range(ADA_FIRST):
                ada_block_pe(pe, b)
            norm_pe(pe, 0)
            pe.wait_ge(consts_in, N_CONST)
            for t in range(NT):
                group(pe, t, None, token_products(GW, t, HN), (hn_ready, 0))
            for n in (12, 13):
                arrived(pe, B1 + n, None)
                for m in range(4):
                    group(pe, 4 * (n - 11) + m, None, channel_products(slot(B1 + n), m, HN))
            arrived(pe, B1 + 14, None)
            for t in range(NT):
                group(pe, 12 + t, None, token_products(slot(B1 + 14), t, HN))
            ml_gates_pe(pe)
            pe.wait_ge(filled, 9)
            pe.wait_ge(proj_taken, 16)
            ml_pe(pe)
            arrived(pe, B1 + 15, None)
            for t in range(NT):
                group(pe, 16 + t, None, token_products(slot(B1 + 15), t, HN))
            for n in (16, 17, 18):
                arrived(pe, B1 + n, None)
                for m in range(4):
                    group(pe, 4 * (n - 11) + m, None, channel_products(slot(B1 + n), m, HN))
            pe.wait_ge(ml_h, 1)
            to_channels_pe(pe, HACC, PS[4:8], hb_t)
            l2_pe(pe)
            gdn_gates_pe(pe)
            gdn_pe(pe)
            pe.wait_ge(gd_out, ROUNDS)
            arrived(pe, B1 + 19, None)
            for t in range(NT):
                group(pe, 32 + t, None, token_products(slot(B1 + 19), t, HN))
            pe.wait_ge(gd_o, 1)
            to_channels_pe(pe, O, PS[4:8], oa_t)
            pe.wait_ge(oa_copied, 4)
            merge_pe(pe, B1 + 20, 36, None, None, OTV, HBT, ada_late_pe)
            out_pe(pe, 0, B1 + 26, 68, None, None, ada_late_pe)
            norm_pe(pe, 1)
            router_pe(pe)
            moe_pe(pe)
            norm_pe(pe, 2)
            pe.sem_inc(down_part, PART_CREDIT)
            with pe.Fori(0, LAYERS) as L:
                it, gi = (L, L_BLOCKS), (L, L_GROUPS)
                layer_pack_pe(pe, L)
                norm_pe(pe, L * 2 + 3)
                attn_proj_pe(pe, L)
                sb_pe(pe, L)
                latent_pe(pe, L)
                heads_proj_pe(pe, L)
                heads_norm_pe(pe, L)
                mla_pe(pe, L)
                pe.wait_ge(la_out, L * 4 + 4)
                merge_pe(pe, LB + 17, LG + GL["merge"], it, gi, YM, YS)
                out_pe(pe, L + 1, LB + 23, LG + GL["out"], it, gi, norm=L * 2 + 4)
                up_pe(pe, L)
                down_pe(pe, L)
            output_pe(pe)

        @block.scalar
        def _(act):
            own = Own(act, act_own)
            setup_loads_act(act)
            act.wait_ge(filled, 9)
            setup_act(act)
            act.wait_ge(h_ready, KC)
            norm_act(act, own, 0)
            for t in range(NT):
                act.activation(GT[:, t, :], take(act, t, None)[:, 0:64], ACT.Copy).then_inc(proj_taken, 1)
            conv_act(act, 8, 0, 4, BQK)
            bv_act(act)
            ml_gates_act(act, own)
            ml_act(act)
            for t in range(NT):
                act.activation(BO[:, t, :], take(act, 16 + t, None)[:, :], ACT.Sigmoid).then_inc(proj_taken, 1)
            ml_post_act(act, own)
            conv_act(act, 12, 8, 20, QKV)
            to_channels_act(act, HBT, PS[4:8], hb_t, hb_copied)
            l2_act(act, own)
            tok_act(act)
            gdn_gates_act(act, own)
            gdn_act(act)
            for t in range(NT):
                act.activation(Z[:, t, :], take(act, 32 + t, None)[:, :], ACT.Silu).then_inc(proj_taken, 1)
            gdn_post_act(act, own)
            to_channels_act(act, OTV, PS[4:8], oa_t, oa_copied)
            merge_act(act, 0, 36, None, None)
            act.wait_ge(mod_ready, 1)
            residual_act(act, 0, 68, None, 2 * KC)
            act.wait_ge(res_added, KC)
            norm_act(act, own, 1)
            router_act(act, own)
            rope_tables_act(act)
            moe_act_(act)
            act.wait_ge(moe_add, KC)
            norm_act(act, own, 2)
            with act.Fori(0, LAYERS) as L:
                gi = (L, L_GROUPS)
                own.enter(L, ACT_LAYER)
                act.wait_ge(hn_ready, 3 * KC)
                act.wait_ge(res_added, L * 16 + 8)
                layer_pack_act(act, own, L)
                norm_act(act, own, L * 2 + 3)
                attn_proj_act(act, L)
                sb_act(act, own, L)
                latent_act(act, own, L)
                heads_proj_act(act, L)
                heads_norm_act(act, own, L)
                mla_act(act, L)
                merge_act(act, L + 1, LG + GL["merge"], gi, (VEC[:, 0, V2["b_gate"]:V2["b_gate"] + 8],
                                                            VEC[:, 0, V2["b_gate"] + 8:V2["b_gate"] + 16]))
                residual_act(act, L * 2 + 1, LG + GL["out"], gi, 2 * KC, norm=L * 2 + 4)
                rstd_act(act, own, L * 2 + 4)
                up_act(act, L)
                residual_act(act, L * 2 + 2, LG + GL["down"], gi, 5 * KC)
            own.leave(LAYERS)
            output_act(act)

        @block.vector
        def _(dve):
            own = Own(dve, dve_own)
            ada_first_dve(dve, own)
            gain_dve(dve, own, 0, VEC[:, 0, V_GMIX:V_GMIX + KC])
            norm_dve(dve, own, 0, 0)
            dve.wait_ge(filled, 9)
            conv_dve(dve, own, 8, 0, 4, lambda k, m: VEC[:, 0, V_BCONV + 8 * k + m:V_BCONV + 8 * k + m + 1])
            ml_gates_dve(dve, own)
            ml_dve(dve, own)
            conv_dve(dve, own, 12, 8, 20, lambda k, m: VEC[:, 1, 12 * k + m:12 * k + m + 1])
            l2_dve(dve)
            gdn_gates_dve(dve, own)
            gdn_dve(dve, own)
            merge_dve(dve, own, 0, 36, None, ada_late_dve)
            residual_dve(dve, own, 0, 68, None, ada_late_dve)
            rope_tables_dve(dve, own)
            norm_dve(dve, own, 1, 1)
            router_dve(dve, own)
            moe_dve(dve)
            moe_sum_dve(dve, own)
            final_norm_dve(dve)
            with dve.Fori(0, LAYERS) as L:
                it, gi = (L, L_BLOCKS), (L, L_GROUPS)
                own.enter(L, DVE_LAYER)
                own(dve.tensor_copy(MOD[:, :], MODL[:, 0, :]))
                own(dve.tensor_copy(MODL[:, 0, :], MODL[:, 1, :]))
                dve.wait_ge(vec_ready, L + 1)
                for j, g in ((0, "g_norm1"), (1, "g_norm2")):
                    gain_dve(dve, own, j, VEC[:, 0, V2[g]:V2[g] + KC])
                norm_dve(dve, own, L * 2 + 3, 0)
                sb_dve(dve, own, L)
                latent_dve(dve, L)
                heads_norm_dve(dve, own, L)
                mla_dve(dve, own, L)
                merge_dve(dve, own, L + 1, LG + GL["merge"], gi)
                residual_dve(dve, own, L * 2 + 1, LG + GL["out"], gi)
                norm_dve(dve, own, L * 2 + 4, 1)
                up_dve(dve, own, L)
                residual_dve(dve, own, L * 2 + 2, LG + GL["down"], gi)
            own.leave(LAYERS)


def kernel(**inputs):
    import numpy as _np
    import concourse.bacc as _bacc
    from concourse import mybir as _mybir
    from concourse.bass_utils import run_bass_kernel_spmd as _run

    nc = _bacc.Bacc("TRN2", target_bir_lowering=False, num_devices=1)
    arrays, args = {}, {}
    for name, value in {**inputs, "masks": masks_array(), "freq": freq_array()}.items():
        v = _np.ascontiguousarray(value)
        arrays[f"in_{name}"] = v
        args[name] = nc.dram_tensor(f"in_{name}", v.shape, _mybir.dt.from_np(v.dtype), kind="ExternalInput").ap()
    hn_rows = nc.dram_tensor("hn_rows", (S, D), F32, kind="Internal").ap()
    idx_rows = nc.dram_tensor("idx_rows", (MOE_SLOTS, P), U32, kind="Internal").ap()
    y_rows = nc.dram_tensor("y_rows", (MOE_SLOTS * P, D), F32, kind="Internal").ap()
    out = nc.dram_tensor("out_0", (1, S, D), F32, kind="ExternalOutput").ap()
    build(nc, args, hn_rows, idx_rows, y_rows, out)
    r = _run(nc, [arrays], core_ids=[0])
    return r.results[0]["out_0"]
```
